# Optimizing a Trainium2 kernel written in Bass

```python
import jax, jax.numpy as jnp
from jax import lax
import numpy as np

D_MODEL = 1024
BATCH = 1
SEQ = 256
DEPTH = 2

HEAD_DIM = 64
ROT_DIM = HEAD_DIM // 4
ROPE_THETA = 500000.0
BLOCK = 128
EPS = 1e-5
NEG_INF = -1e30

A_Q_HEADS = 16
A_KV_HEADS = 4
A_REP = A_Q_HEADS // A_KV_HEADS
A_WINDOW = 128
A_Q_W = A_Q_HEADS * HEAD_DIM
A_KV_W = A_KV_HEADS * HEAD_DIM

B_GROUPS = 12
B_CH = 64
B_WIDTH = B_GROUPS * B_CH
B_CHUNK = 128

C_PAIRS = ((128, 1), (512, 4), (2048, 16))
C_HEADS_PER_GROUP = 4
C_HEADS = C_HEADS_PER_GROUP * len(C_PAIRS)
C_QKV_W = 3 * C_HEADS * HEAD_DIM
C_OUT_W = C_HEADS_PER_GROUP * HEAD_DIM

N_BRANCH = 3
GATE_W = N_BRANCH * D_MODEL
IN_SPLITS = [A_Q_W, A_Q_W + A_KV_W, A_Q_W + 2 * A_KV_W, A_Q_W + 2 * A_KV_W + 2 * B_WIDTH,
             A_Q_W + 2 * A_KV_W + 2 * B_WIDTH + C_QKV_W]
D_IN = A_Q_W + 2 * A_KV_W + 2 * B_WIDTH + C_QKV_W + GATE_W

N_EXPERT_GROUPS = 4
EXPERTS_PER_GROUP = 8
N_EXPERTS = N_EXPERT_GROUPS * EXPERTS_PER_GROUP
TOP_K = 2
D_EXPERT = 256

kernel_name = "hybrid_gated_swa_sgu_dilated_hmoe"

def rms_norm(x, g):
    xf = x.astype(jnp.float32)
    y = xf * lax.rsqrt(jnp.mean(xf * xf, -1, keepdims=True) + EPS)
    return (y * g.astype(jnp.float32)).astype(x.dtype)

def layer_norm(x, g, bias):
    xf = x.astype(jnp.float32)
    mu = jnp.mean(xf, -1, keepdims=True)
    var = jnp.mean(jnp.square(xf - mu), -1, keepdims=True)
    y = (xf - mu) * lax.rsqrt(var + EPS) * g.astype(jnp.float32) + bias.astype(jnp.float32)
    return y.astype(x.dtype)

def rope_tables(positions):
    inv = ROPE_THETA ** (-jnp.arange(0, ROT_DIM, 2, dtype=jnp.float32) / ROT_DIM)
    ang = positions.astype(jnp.float32)[..., None] * inv
    return jnp.cos(ang)[:, None], jnp.sin(ang)[:, None]

def partial_rope(t, cos, sin):
    half = ROT_DIM // 2
    t1 = t[..., :half].astype(jnp.float32)
    t2 = t[..., half:ROT_DIM].astype(jnp.float32)
    rot = jnp.concatenate([t1 * cos - t2 * sin, t2 * cos + t1 * sin], -1).astype(t.dtype)
    return jnp.concatenate([rot, t[..., ROT_DIM:]], -1)

def split_heads(t, n_heads):
    b, s, _ = t.shape
    return t.reshape(b, s, n_heads, HEAD_DIM).transpose(0, 2, 1, 3)

def banded_attention(q, k, v, max_dist, sink=None):
    b, hk, r, L, hd = q.shape
    nb = L // BLOCK
    qb = q.reshape(b, hk, r, nb, BLOCK, hd)

    def band(t):
        tb = t.reshape(b, hk, nb, BLOCK, hd)
        prev = jnp.pad(tb[:, :, :-1], ((0, 0), (0, 0), (1, 0), (0, 0), (0, 0)))
        return jnp.concatenate([prev, tb], axis=3)

    kb, vb = band(k), band(v)
    s = jnp.einsum("bhrnqd,bhnkd->bhrnqk", qb, kb).astype(jnp.float32) * (hd ** -0.5)
    qi = jnp.arange(BLOCK)[:, None] + BLOCK
    kj = jnp.arange(2 * BLOCK)[None, :]
    dist = qi - kj
    blk = jnp.arange(nb)[:, None, None]
    valid = (dist >= 0) & (dist <= max_dist) & ((blk > 0) | (kj >= BLOCK))
    s = jnp.where(valid, s, NEG_INF)
    m = jnp.max(s, -1, keepdims=True)
    if sink is not None:
        sk = sink.astype(jnp.float32).reshape(1, hk, r, 1, 1, 1)
        m = jnp.maximum(m, sk)
    p = jnp.exp(s - m)
    denom = jnp.sum(p, -1, keepdims=True)
    if sink is not None:
        denom = denom + jnp.exp(sk - m)
    o = jnp.einsum("bhrnqk,bhnkd->bhrnqd", (p / denom).astype(v.dtype), vb)
    lse = (m + jnp.log(denom))[..., 0]
    return o.reshape(b, hk, r, L, hd), lse.reshape(b, hk, r, L)

def dilated_group(q, k, v, window, dilation):
    b, h, s, hd = q.shape
    n = s // dilation
    lr = -(-n // BLOCK) * BLOCK

    def to_res(t):
        t = t.reshape(b, h, n, dilation, hd).transpose(0, 1, 3, 2, 4).reshape(b, h * dilation, n, hd)
        return jnp.pad(t, ((0, 0), (0, 0), (0, lr - n), (0, 0)))

    o, lse = banded_attention(to_res(q)[:, :, None], to_res(k), to_res(v), window // dilation)
    o = o[:, :, 0, :n].reshape(b, h, dilation, n, hd).transpose(0, 1, 3, 2, 4).reshape(b, h, s, hd)
    lse = lse[:, :, 0, :n].reshape(b, h, dilation, n).transpose(0, 1, 3, 2).reshape(b, h, s)
    return o, lse

def spatial_gating(zb, ln_g, ln_b, w_s, b_s):
    b, s, _ = zb.shape
    uv = jax.nn.gelu(zb)
    u, v = uv[..., :B_WIDTH], uv[..., B_WIDTH:]
    v = layer_norm(v, ln_g, ln_b)
    vc = v.reshape(b, s // B_CHUNK, B_CHUNK, B_GROUPS, B_CH)
    ws = w_s * jnp.tril(jnp.ones((B_CHUNK, B_CHUNK), w_s.dtype))
    sv = jnp.einsum("gts,bnsgc->bntgc", ws, vc) + b_s.T[None, None, :, :, None]
    return u * sv.reshape(b, s, B_WIDTH)

def hier_moe(h, w_rg, w_re, w_gate, w_up, w_down):
    b, s, d = h.shape
    t = h.reshape(b * s, d)
    pg = jax.nn.softmax((t @ w_rg).astype(jnp.float32), -1)
    pg_top, g_idx = lax.top_k(pg, 1)
    le = (t @ w_re).astype(jnp.float32).reshape(-1, N_EXPERT_GROUPS, EXPERTS_PER_GROUP)
    le_sel = jnp.take_along_axis(le, g_idx[:, :, None], axis=1)[:, 0]
    pe_top, e_idx = lax.top_k(jax.nn.softmax(le_sel, -1), TOP_K)
    w = pg_top * pe_top / jnp.sum(pe_top, -1, keepdims=True)
    ids = g_idx * EXPERTS_PER_GROUP + e_idx
    combine = jnp.sum(jax.nn.one_hot(ids, N_EXPERTS, dtype=jnp.float32) * w[..., None], 1)
    hg = jnp.einsum("nd,edf->nef", t, w_gate)
    hu = jnp.einsum("nd,edf->nef", t, w_up)
    a = jax.nn.silu(hg) * hu * combine[..., None].astype(t.dtype)
    return jnp.einsum("nef,efd->nd", a, w_down).reshape(b, s, d)

def setup_inputs(seed: int = 0) -> dict:
    key = jax.random.key(seed)
    ks = jax.random.split(key, 24)
    f32 = jnp.float32

    def nrm(k, shape, scale):
        return jax.random.normal(k, shape, f32) * scale

    L = DEPTH
    positions = (jax.random.randint(ks[1], (BATCH, 1), 0, 4096, dtype=jnp.int32)
                 + jnp.arange(SEQ, dtype=jnp.int32)[None, :])
    return {
        "x": nrm(ks[0], (BATCH, SEQ, D_MODEL), 1.0),
        "positions": positions,
        "norm1_g": 1.0 + nrm(ks[2], (L, D_MODEL), 0.02),
        "w_in": nrm(ks[3], (L, D_MODEL, D_IN), D_MODEL ** -0.5),
        "b_in": nrm(ks[4], (L, D_IN), 0.02),
        "attn_sinks": nrm(ks[5], (L, A_Q_HEADS), 0.5),
        "sgu_ln_g": 1.0 + nrm(ks[6], (L, B_WIDTH), 0.02),
        "sgu_ln_b": nrm(ks[7], (L, B_WIDTH), 0.02),
        "w_spatial": nrm(ks[8], (L, B_GROUPS, B_CHUNK, B_CHUNK), B_CHUNK ** -0.5),
        "b_spatial": 1.0 + nrm(ks[9], (L, B_GROUPS, B_CHUNK), 0.02),
        "w_proj_a": nrm(ks[10], (L, A_Q_W, D_MODEL), A_Q_W ** -0.5),
        "w_proj_b": nrm(ks[11], (L, B_WIDTH, D_MODEL), B_WIDTH ** -0.5),
        "w_proj_c": nrm(ks[12], (L, C_OUT_W, D_MODEL), C_OUT_W ** -0.5),
        "w_out": nrm(ks[13], (L, D_MODEL, D_MODEL), D_MODEL ** -0.5),
        "norm2_g": 1.0 + nrm(ks[14], (L, D_MODEL), 0.02),
        "w_router_group": nrm(ks[15], (L, D_MODEL, N_EXPERT_GROUPS), D_MODEL ** -0.5),
        "w_router_expert": nrm(ks[16], (L, D_MODEL, N_EXPERTS), D_MODEL ** -0.5),
        "w_expert_gate": nrm(ks[17], (L, N_EXPERTS, D_MODEL, D_EXPERT), D_MODEL ** -0.5),
        "w_expert_up": nrm(ks[18], (L, N_EXPERTS, D_MODEL, D_EXPERT), D_MODEL ** -0.5),
        "w_expert_down": nrm(ks[19], (L, N_EXPERTS, D_EXPERT, D_MODEL), D_EXPERT ** -0.5),
        "norm_f_g": 1.0 + nrm(ks[20], (D_MODEL,), 0.02),
    }

def reference(x, positions, norm1_g, w_in, b_in, attn_sinks, sgu_ln_g, sgu_ln_b, w_spatial, b_spatial,
              w_proj_a, w_proj_b, w_proj_c, w_out, norm2_g, w_router_group, w_router_expert,
              w_expert_gate, w_expert_up, w_expert_down, norm_f_g):
    b, s, _ = x.shape
    cos, sin = rope_tables(positions)
    for l in range(DEPTH):
        h = rms_norm(x, norm1_g[l])
        z = jnp.einsum("bsd,de->bse", h, w_in[l]) + b_in[l]
        za_q, za_k, za_v, zb, zc, zg = jnp.split(z, IN_SPLITS, axis=-1)

        qa = partial_rope(split_heads(za_q, A_Q_HEADS), cos, sin).reshape(b, A_KV_HEADS, A_REP, s, HEAD_DIM)
        ka = partial_rope(split_heads(za_k, A_KV_HEADS), cos, sin)
        va = split_heads(za_v, A_KV_HEADS)
        oa, _ = banded_attention(qa, ka, va, A_WINDOW - 1, attn_sinks[l].reshape(A_KV_HEADS, A_REP))
        oa = oa.reshape(b, A_Q_HEADS, s, HEAD_DIM).transpose(0, 2, 1, 3).reshape(b, s, A_Q_W)

        ob = spatial_gating(zb, sgu_ln_g[l], sgu_ln_b[l], w_spatial[l], b_spatial[l])

        zc = zc.reshape(b, s, 3, C_HEADS, HEAD_DIM).transpose(2, 0, 3, 1, 4)
        qc = partial_rope(zc[0], cos, sin)
        kc = partial_rope(zc[1], cos, sin)
        vc = zc[2]
        outs, lses = [], []
        for g, (win, dil) in enumerate(C_PAIRS):
            sl = slice(g * C_HEADS_PER_GROUP, (g + 1) * C_HEADS_PER_GROUP)
            o_g, lse_g = dilated_group(qc[:, sl], kc[:, sl], vc[:, sl], win, dil)
            outs.append(o_g)
            lses.append(lse_g)
        wgt = jax.nn.softmax(jnp.stack(lses, 0), axis=0)
        oc = jnp.sum(wgt[..., None] * jnp.stack(outs, 0).astype(jnp.float32), 0).astype(x.dtype)
        oc = oc.transpose(0, 2, 1, 3).reshape(b, s, C_OUT_W)

        gates = jax.nn.sigmoid(zg).reshape(b, s, N_BRANCH, D_MODEL)
        merged = (gates[:, :, 0] * (oa @ w_proj_a[l])
                  + gates[:, :, 1] * (ob @ w_proj_b[l])
                  + gates[:, :, 2] * (oc @ w_proj_c[l]))
        x = x + merged @ w_out[l]

        x = x + hier_moe(rms_norm(x, norm2_g[l]), w_router_group[l], w_router_expert[l],
                         w_expert_gate[l], w_expert_up[l], w_expert_down[l])
    return rms_norm(x, norm_f_g)


_drawn_inputs = setup_inputs


def setup_inputs(seed=0):
    import zlib

    import numpy as np

    out = dict(_drawn_inputs(seed))
    spreads = {}
    factors = {'attn_sinks': 4.124, 'sgu_ln_g': 2.762, 'sgu_ln_b': 2.68, 'norm_f_g': 2.96}
    for name, (base, spread) in spreads.items():
        noise = np.random.default_rng([zlib.crc32(name.encode()), seed]).standard_normal(out[name].shape)
        drawn = base * np.exp(spread * noise) if base else spread * noise
        out[name] = __import__('jax').numpy.asarray(drawn.astype(out[name].dtype))
    for name, factor in factors.items():
        out[name] = (out[name] * factor).astype(out[name].dtype)
    return out
```

```python
from contextlib import ExitStack

import concourse.bass as bass
import numpy as np
from concourse import mybir

ALU = mybir.AluOpType
ACT = mybir.ActivationFunctionType
AX = mybir.AxisListType.X
F32 = mybir.dt.float32
F32R = mybir.dt.float32r
I32 = mybir.dt.int32
U32 = mybir.dt.uint32
ds = bass.ds

P = 128
HD = 64
ROT, HALF = 16, 8
THETA = 500000.0
EPS = 1e-5
NEG = -1e30
SCALE = HD ** -0.5
BANK = 512
SLOT = 2048

A_HEADS, A_KV, A_WIN = 16, 4, 128
B_GROUPS, B_W = 12, 768
C_PAIRS = ((128, 1), (512, 4), (2048, 16))
C_PER = 4
ZQ, ZK, ZV = 0, 1024, 1280
ZU, ZN = 1536, 2304
CQ, CK, CV = 3072, 3840, 4608
ZG = 5376

GROUPS, PER_GROUP, F = 4, 8, 256
EXPERTS = GROUPS * PER_GROUP
EC = 64
UNIT = PER_GROUP * EC
PAIRS = PER_GROUP // 2


def trunk_program(nc, x, positions, norm1_g, w_in, b_in, attn_sinks, sgu_ln_g, sgu_ln_b, w_spatial,
                  b_spatial, w_proj_a, w_proj_b, w_proj_c, w_out, norm2_g, w_router_group,
                  w_router_expert, w_expert_gate, w_expert_up, w_expert_down, norm_f_g, out):
    S, D = x.shape[1:]
    DEPTH, _, D_IN = w_in.shape
    TB, KB = S // P, D // P
    assert TB == 2 and KB == 8 and D_IN == ZG + 3 * D

    with ExitStack() as whole:
        def sb(name, shape, dt=F32, ctx=whole):
            return ctx.enter_context(nc.sbuf_tensor(name, shape, dt))

        sems = []

        def sem(name):
            s = whole.enter_context(nc.semaphore(name))
            sems.append(s)
            return s

        ps = whole.enter_context(nc.psum_tensor("ps", [P, 8, BANK], F32))

        xs = sb("xs", [P, TB, D])
        work = sb("work", [P, TB, D])
        ident = sb("ident", [P, P])
        ones = sb("ones", [P, P])
        before = sb("before", [P, P])
        mask_a = sb("mask_a", [P, 384])
        mask_c = sb("mask_c", [P, 3, 384])
        slot_iota = sb("slot_iota", [P, EC])
        idx_iota = sb("idx_iota", [P, PER_GROUP])
        cos = sb("cos", [P, TB, HALF])
        sin = sb("sin", [P, TB, HALF])
        ss = sb("ss", [P, TB])
        rstd = sb("rstd", [P, TB])
        gain = sb("gain", [P, KB])
        rk = sb("rk", [P, TB, EXPERTS])
        comb = sb("comb", [P, TB, EXPERTS])
        rounds = sb("rounds", [P, 1], I32)

        ring_in = [sem(f"ring_in{i}") for i in range(12)]
        small_in = sem("small_in")
        bias_in = sem("bias_in")
        wsp_in = sem("wsp_in")
        ln_in = sem("ln_in")
        dve_step = sem("dve_step")
        act_step = sem("act_step")
        pool_step = sem("pool_step")
        squares = sem("squares")
        recips = sem("recips")
        roots = sem("roots")
        normed = sem("normed")
        turned = sem("turned")
        turned_hi = sem("turned_hi")
        turned_lo = sem("turned_lo")
        hi_ready = sem("hi_ready")
        low_split = sem("low_split")
        conv_used = sem("conv_used")
        z_ready = sem("z_ready")
        z_evac = sem("z_evac")
        tril_done = sem("tril_done")
        wst_ready = sem("wst_ready")
        wst_evac = sem("wst_evac")
        gelu_done = sem("gelu_done")
        lnv_ready = sem("lnv_ready")
        ln_root = sem("ln_root")
        vn_ready = sem("vn_ready")
        v_ready = sem("v_ready")
        gates_ready = sem("gates_ready")
        roped = sem("roped")
        t_ready = sem("t_ready")
        t_evac = sem("t_evac")
        s_ready = sem("s_ready")
        s_free = sem("s_free")
        neg_ready = sem("neg_ready")
        exp_ready = sem("exp_ready")
        p_ready = sem("p_ready")
        pv_turned = sem("pv_turned")
        pv_mm = sem("pv_mm")
        o_ready = sem("o_ready")
        o_hi = sem("o_hi")
        o_lo = sem("o_lo")
        sv_ready = sem("sv_ready")
        ob_ready = sem("ob_ready")
        obt_ready = sem("obt_ready")
        obt_hi = sem("obt_hi")
        obt_lo = sem("obt_lo")
        proj_ready = sem("proj_ready")
        gated = sem("gated")
        merged = sem("merged")
        mt_ready = sem("mt_ready")
        mt_hi = sem("mt_hi")
        mt_lo = sem("mt_lo")
        out_ready = sem("out_ready")
        logits_ready = sem("logits_ready")
        h2t_ready = sem("h2t_ready")
        router_exp = sem("router_exp")
        router_in = sem("router_in")
        picked = sem("picked")
        ranks_ready = sem("ranks_ready")
        onehot_ready = sem("onehot_ready")
        onehot_used = sem("onehot_used")
        gath_ready = sem("gath_ready")
        gath_act = sem("gath_act")
        gath_dve = sem("gath_dve")
        st_ready = sem("st_ready")
        st_evac = sem("st_evac")
        gu_ready = sem("gu_ready")
        silu_done = sem("silu_done")
        a_ready = sem("a_ready")
        at_ready = sem("at_ready")
        at_evac = sem("at_evac")
        y_ready = sem("y_ready")
        y_hi = sem("y_hi")
        y_lo = sem("y_lo")
        back_ready = sem("back_ready")
        back_done = sem("back_done")
        out_done = sem("out_done")
        sem_range = range(min(s.num for s in sems), max(s.num for s in sems) + 1)

        def end_of_stage():
            nc.all_engine_barrier(sems_to_clear=sem_range)

        def chain(eng, s):
            count = [0]

            def link(ins):
                count[0] += 1
                ins.then_inc(s, 1)
                eng.wait_ge(s, count[0])
            return link

        def bcast(ap, shape):
            return ap.to_broadcast(shape)

        with ExitStack() as ctx:
            pos_i = sb("pos_i", [P, TB], I32, ctx)
            pos_f = sb("pos_f", [P, TB], F32, ctx)
            inv = sb("inv", [P, HALF], F32, ctx)
            ang = sb("ang", [P, TB, HALF], F32, ctx)
            turns = sb("turns", [P, TB, HALF], F32, ctx)
            folded = sb("folded", [P, TB, HALF], F32, ctx)
            dist_i = sb("dist_i", [P, 384], I32, ctx)
            dist = sb("dist", [P, 384], F32, ctx)
            rem_i = sb("rem_i", [P, 384], I32, ctx)
            rem = sb("rem", [P, 384], F32, ctx)
            causal = sb("causal", [P, 384], F32, ctx)
            within = sb("within", [P, 384], F32, ctx)
            iota_i = sb("iota_i", [P, EC], I32, ctx)
            iota8_i = sb("iota8_i", [P, PER_GROUP], I32, ctx)

            with nc.Block() as block:
                @block.sync
                def _(sp):
                    sp.dma_start(xs[:], x.rearrange("o (t p) d -> p (o t) d", p=P)).then_inc(ring_in[0], 16)
                    with nc.allow_non_contiguous_dma(reason="256 positions"):
                        sp.dma_start(pos_i[:], positions.rearrange("o (t p) -> p (o t)", p=P)).then_inc(small_in, 16)
                    sp.wait_ge(ring_in[0], 16)

                @block.gpsimd
                def _(pool):
                    link = chain(pool, pool_step)
                    link(pool.memset(ident[:], 0.0))
                    link(pool.affine_select(out=ident[:], in_=ident[:], compare_op=ALU.not_equal, fill=1.0,
                                            base=0, pattern=[[-1, P]], channel_multiplier=1))
                    link(pool.memset(ones[:], 1.0))
                    link(pool.affine_select(out=before[:], in_=ones[:], compare_op=ALU.is_gt, fill=0.0,
                                            base=0, pattern=[[1, P]], channel_multiplier=-1))
                    pool.iota(iota_i[:], pattern=[[1, EC]], base=0, channel_multiplier=0)
                    pool.iota(iota8_i[:], pattern=[[1, PER_GROUP]], base=0, channel_multiplier=0)
                    pool.iota(dist_i[:, 0:P], pattern=[[-1, P]], base=0, channel_multiplier=1)
                    pool.iota(dist_i[:, P:3 * P], pattern=[[-1, 2 * P]], base=P,
                              channel_multiplier=1).then_inc(tril_done, 1)

                @block.vector
                def _(dve):
                    link = chain(dve, dve_step)
                    dve.wait_ge(tril_done, 1)
                    dve.tensor_copy(slot_iota[:], iota_i[:])
                    dve.tensor_copy(idx_iota[:], iota8_i[:])
                    link(dve.tensor_copy(dist[:], dist_i[:]))
                    link(dve.tensor_scalar(causal[:], dist[:], 0.0, None, ALU.is_ge))

                    def finish_mask(m):
                        link(dve.tensor_scalar(m, within[:], 1.0, -NEG, ALU.subtract, ALU.mult))

                    link(dve.scalar_tensor_tensor(out=within[:], in0=dist[:], scalar=float(A_WIN - 1),
                                                  in1=causal[:], op0=ALU.is_le, op1=ALU.mult))
                    finish_mask(mask_a[:])
                    for g, (win, dil) in enumerate(C_PAIRS):
                        link(dve.tensor_scalar(rem_i[:], dist_i[:], dil - 1, None, ALU.bitwise_and))
                        link(dve.tensor_copy(rem[:], rem_i[:]))
                        link(dve.scalar_tensor_tensor(out=rem[:], in0=rem[:], scalar=0.0, in1=causal[:],
                                                      op0=ALU.is_equal, op1=ALU.mult))
                        link(dve.scalar_tensor_tensor(out=within[:], in0=dist[:], scalar=float(win),
                                                      in1=rem[:], op0=ALU.is_le, op1=ALU.mult))
                        finish_mask(mask_c[:, g, :])
                    for i in range(HALF):
                        f = float(np.float32(THETA) ** np.float32(-2.0 * i / ROT))
                        dve.memset(inv[:, i:i + 1], f)
                    dve.wait_ge(small_in, 16)
                    link(dve.tensor_copy(pos_f[:], pos_i[:]))
                    link(dve.tensor_tensor(ang[:], bcast(pos_f[:].unsqueeze(2), [P, TB, HALF]),
                                           bcast(inv[:].unsqueeze(1), [P, TB, HALF]), ALU.mult))
                    magic = 1.5 * 2.0 ** 23
                    link(dve.tensor_scalar(turns[:], ang[:], float(1 / (2 * np.pi)), magic, ALU.mult, ALU.add))
                    link(dve.tensor_scalar(turns[:], turns[:], magic, None, ALU.subtract))
                    c1 = 6.28125
                    c2 = float(np.round((2 * np.pi - c1) * 2 ** 20) / 2 ** 20)
                    c3 = float(2 * np.pi - c1 - c2)
                    for c in (c1, c2, c3):
                        link(dve.scalar_tensor_tensor(out=ang[:], in0=turns[:], scalar=-c, in1=ang[:],
                                                      op0=ALU.mult, op1=ALU.add))
                    link(dve.tensor_scalar(ang[:], ang[:], float(np.float32(3.1415925)),
                                           -float(np.float32(3.1415925)), ALU.min, ALU.max))
                    link(dve.tensor_scalar(folded[:], ang[:], -1.0, None, ALU.mult))
                    link(dve.tensor_tensor(folded[:], folded[:], ang[:], ALU.min))
                    link(dve.tensor_scalar(folded[:], folded[:], float(np.pi / 2), None, ALU.add))
                    dve.sem_inc(picked, 1)

                @block.scalar
                def _(act):
                    act.wait_ge(picked, 1)
                    act.activation(sin[:], ang[:], ACT.Sin)
                    act.activation(cos[:], folded[:], ACT.Sin)
            end_of_stage()

        def rms_inverse(act, dve, which, junk):
            if which == "act":
                for tb in range(TB):
                    last = act.activation(junk[:, tb, :], xs[:, tb, :], ACT.Square, accum_out=ss[:, tb:tb + 1])
                last.then_inc(squares, 1)
                act.wait_ge(recips, 1)
                act.activation(rstd[:], ss[:], ACT.Sqrt).then_inc(roots, 1)
            else:
                link = which
                dve.wait_ge(squares, 1)
                link(dve.tensor_scalar(ss[:], ss[:], 1.0 / D, EPS, ALU.mult, ALU.add))
                dve.reciprocal(ss[:], ss[:]).then_inc(recips, 1)
                dve.wait_ge(roots, 1)
                for tb in range(TB):
                    last = dve.tensor_scalar(work[:, tb, :], xs[:, tb, :], rstd[:, tb:tb + 1], None, ALU.mult)
                last.then_inc(normed, 1)

        def layer_of(w, l):
            return w[ds(l, 1)].squeeze(0)

        def trunk_stage(l):
            with ExitStack() as ctx:
                RING = 4
                Z_CONV = 68
                CHUNKS = 16
                TAIL = D_IN - CHUNKS * BANK
                ring = sb("ring_t", [P, RING, SLOT], F32, ctx)
                z = sb("z", [P, TB, D_IN], F32, ctx)
                whi = sb("whi", [P, 2, SLOT // 2], F32R, ctx)
                wlo = sb("wlo", [P, 2, SLOT // 2], F32R, ctx)
                ahi = sb("ahi", [P, 16, S], F32R, ctx)
                alo = sb("alo", [P, 16, S], F32R, ctx)
                wst = sb("wst", [P, B_GROUPS, P], F32, ctx)
                probs = sb("probs", [P, 2, 4, 384], F32, ctx)
                qkt = sb("qkt", [P, 3, BANK], F32, ctx)
                pts = sb("pts", [P, 2, 384], F32, ctx)
                tmp = sb("tmp", [P, 2, BANK], F32, ctx)
                k_twice = sb("k_twice", [P, TB, A_KV, 2 * HD], F32, ctx)
                sinks = sb("sinks", [P, A_HEADS], F32, ctx)
                bsp = sb("bsp", [P, B_GROUPS], F32, ctx)
                mx = sb("mx", [P, 2, TB, 4], F32, ctx)
                neg = sb("neg", [P, 2, TB, 4], F32, ctx)
                ex = sb("ex", [P, 2, TB, 4], F32, ctx)
                den = sb("den", [P, 2, TB, 4], F32, ctx)
                mxg = sb("mxg", [P, 2, TB], F32, ctx)
                stats = sb("stats", [P, TB, 2, 6], F32, ctx)
                mv = sb("mv", [P, TB, 2], F32, ctx)
                wsp = probs[:].rearrange("p a b c -> p (a b c)")[:, 0:B_GROUPS * P].rearrange(
                    "p (g s) -> p g s", g=B_GROUPS)
                ln_gb = work[:].rearrange("p t d -> p (t d)")[:, 0:2 * B_W].rearrange("p (n c) -> p n c", n=2)

                w_in_l = layer_of(w_in, l).rearrange("(p k) n -> p k n", k=KB)
                proj = ([(layer_of(w_proj_a, l), r) for r in range(4)]
                        + [(layer_of(w_proj_b, l), r) for r in range(3)]
                        + [(layer_of(w_proj_c, l), r) for r in range(1)]
                        + [(layer_of(w_out, l), r) for r in range(4)])

                def t_count(b):
                    order, n = [], 0
                    for s in range(9):
                        if s < 8:
                            order.append(("qk", s, {0: 2, 1: 2, 2: 2, 3: 2, 4: 3, 6: 3}.get(s, 0)))
                        if s >= 1:
                            order.append(("pv", s - 1, 4 if s - 1 < 4 else 3))
                    table = {}
                    for kind, s, k in order:
                        table[kind, s] = (n, k)
                        n += k
                    return table[b]

                def heads(b):
                    return 4 if b < 4 else 3

                def pairs_of(b):
                    return (2 * b, 2 * b + 1) if b < 4 else {5: (8,), 7: (9,)}.get(b, ())

                with nc.Block() as block:
                    @block.sync
                    def _(sp):
                        sp.dma_start(wsp, layer_of(w_spatial, l).rearrange("g t s -> t g s")).then_inc(wsp_in, 16)
                        with nc.allow_non_contiguous_dma(reason="small parameters"):
                            sp.dma_start(gain[:], layer_of(norm1_g, l).rearrange("(p k) -> p k", k=KB)).then_inc(small_in, 16)
                            sp.dma_start(bsp[:], layer_of(b_spatial, l).rearrange("g t -> t g")).then_inc(small_in, 16)
                        sp.dma_start(sinks[:], layer_of(attn_sinks, l).partition_broadcast(P)).then_inc(small_in, 16)
                        sp.dma_start(z[:, 0, :], layer_of(b_in, l).partition_broadcast(P)).then_inc(bias_in, 16)

                        def load_z_item(s, it):
                            src = w_in_l[:, 4 * (s % 2):4 * (s % 2) + 4, ds(it * 2 * BANK + (s // 2) * BANK, BANK)]
                            dst = ring[:, s, :].rearrange("p (k n) -> p k n", k=4)
                            sp.dma_start(dst, src).then_inc(ring_in[s], 16)

                        for s in range(4):
                            load_z_item(s, 0)
                        sp.wait_ge(turned, 4)
                        sp.dma_start(ln_gb[:, 0, :], layer_of(sgu_ln_g, l).partition_broadcast(P)).then_inc(ln_in, 16)
                        sp.dma_start(ln_gb[:, 1, :], layer_of(sgu_ln_b, l).partition_broadcast(P)).then_inc(ln_in, 16)
                        with sp.Fori(1, CHUNKS // 2) as it:
                            for s in range(4):
                                sp.wait_ge(low_split, it * 8 + 2 * (s + 1) - 8)
                                load_z_item(s, it)
                        for half in range(2):
                            sp.wait_ge(low_split, 2 * (4 * 7 + half + 1))
                            src = w_in_l[:, 4 * half:4 * half + 4, CHUNKS * BANK:D_IN]
                            dst = ring[:, half, 0:4 * TAIL].rearrange("p (k n) -> p k n", k=4)
                            sp.dma_start(dst, src).then_inc(ring_in[half], 16)
                        for i, (w, r) in enumerate(proj):
                            item = 34 + i
                            sp.wait_ge(low_split, 2 * (item - 4 + 1))
                            src = w[2 * r * P:2 * (r + 1) * P, :].rearrange("(k p) n -> p k n", p=P)
                            dst = ring[:, item % 4, :].rearrange("p (k n) -> p k n", k=2)
                            sp.dma_start(dst, src).then_inc(ring_in[item % 4], 16)

                    @block.gpsimd
                    def _(pool):
                        link = chain(pool, pool_step)
                        pool.wait_ge(wsp_in, 16)
                        pool.affine_select(out=wsp, in_=wsp, compare_op=ALU.is_ge, fill=0.0, base=0,
                                           pattern=[[0, B_GROUPS], [-1, P]], channel_multiplier=1).then_inc(tril_done, 1)

                        def rope(first, n):
                            for tb in range(TB):
                                hd = z[:, tb, first:first + n * HD].rearrange("p (h c) -> p h c", c=HD)
                                t1, t2 = hd[:, :, 0:HALF], hd[:, :, HALF:ROT]
                                c = bcast(cos[:, tb, :].unsqueeze(1), [P, n, HALF])
                                s = bcast(sin[:, tb, :].unsqueeze(1), [P, n, HALF])
                                t1s = tmp[:, 0, 0:n * HALF].rearrange("p (h c) -> p h c", c=HALF)
                                t2s = tmp[:, 1, 0:n * HALF].rearrange("p (h c) -> p h c", c=HALF)
                                pool.tensor_tensor(t1s, t1, s, ALU.mult)
                                link(pool.tensor_tensor(t2s, t2, s, ALU.mult))
                                pool.tensor_tensor(t1, t1, c, ALU.mult)
                                link(pool.tensor_tensor(t2, t2, c, ALU.mult))
                                pool.tensor_tensor(t1, t1, t2s, ALU.subtract)
                                link(pool.tensor_tensor(t2, t2, t1s, ALU.add))

                        pool.wait_ge(z_evac, 2 * 3)
                        rope(ZQ, A_HEADS + A_KV)
                        k_heads = z[:, :, ZK:ZK + A_KV * HD].rearrange("p t (h c) -> p t h c", c=HD)
                        pool.tensor_copy(k_twice[:, :, :, 0:HD], k_heads)
                        pool.tensor_copy(k_twice[:, :, :, HD:2 * HD], k_heads).then_inc(roped, 1)
                        pool.wait_ge(z_evac, 2 * 9)
                        rope(CQ, 2 * 3 * C_PER)
                        pool.sem_inc(roped, 1)
                        v = z[:, :, ZN:ZN + B_W]
                        pool.wait_ge(vn_ready, 1)
                        pool.wait_ge(ln_in, 32)
                        link(pool.tensor_tensor(v, v, bcast(ln_gb[:, 0:1, :], [P, TB, B_W]), ALU.mult))
                        pool.tensor_tensor(v, v, bcast(ln_gb[:, 1:2, :], [P, TB, B_W]), ALU.add).then_inc(v_ready, 1)

                    def half_slot(j, w):
                        n = 2 * w
                        return ring[:, (j // 2) % RING, (j % 2) * n:(j % 2) * n + n]

                    @block.scalar
                    def _(act):
                        rms_inverse(act, None, "act", z[:, 1, 0:2 * D].rearrange("p (t d) -> p t d", t=TB))
                        act.wait_ge(small_in, 48)
                        for i in range(4):
                            act.wait_ge(turned, i + 1)
                            for k in (2 * i, 2 * i + 1):
                                act.activation(ahi[:, k, :], ps[:, i, (k % 2) * S:(k % 2) * S + S], ACT.Copy,
                                               scale=gain[:, k:k + 1]).then_inc(turned_hi, 1)
                        for i in range(3):
                            act.wait_ge(wst_ready, i + 1)
                            act.copy(wst[:, 4 * i:4 * i + 4, :].rearrange("p g t -> p (g t)"),
                                     ps[:, 4 + i, :]).then_inc(wst_evac, 1)

                        def high(jj, w, landed, used):
                            act.wait_ge(ring_in[(jj // 2) % RING], landed)
                            if used is not None:
                                act.wait_ge(conv_used, used)
                            act.copy(whi[:, jj % 2, 0:2 * w], half_slot(jj, w)).then_inc(hi_ready, 1)

                        for j in range(8):
                            high(j, BANK, 16, j - 1 if j >= 2 else None)
                        with act.Fori(1, CHUNKS // 2) as it:
                            for j in range(8):
                                high(j, BANK, it * 16 + 16, it * 8 + (j - 1))
                        for j in range(64, Z_CONV):
                            high(j, TAIL, 16 * (j // 8 + 1), j - 1)

                        act.wait_ge(z_evac, 2 * 6)
                        act.activation(z[:, :, ZN:ZN + B_W], z[:, :, ZN:ZN + B_W], ACT.Gelu_apprx_tanh).then_inc(gelu_done, 1)
                        act.activation(z[:, :, ZU:ZU + B_W], z[:, :, ZU:ZU + B_W], ACT.Gelu_apprx_tanh).then_inc(gelu_done, 1)
                        act.wait_ge(lnv_ready, 1)
                        act.activation(mv[:, :, 1], mv[:, :, 1], ACT.Sqrt).then_inc(ln_root, 1)
                        act.wait_ge(z_evac, 2 * (CHUNKS + 1))
                        act.activation(z[:, :, ZG:], z[:, :, ZG:], ACT.Sigmoid).then_inc(gates_ready, 1)

                        def qk_out(b):
                            first, n = t_count(("qk", b))
                            for i in range(n):
                                act.wait_ge(t_ready, first + i + 1)
                                w = S if (b < 4 and i == 1) else BANK
                                act.copy(qkt[:, i, 0:w], ps[:, 4 + (first + i) % 2, 0:w]).then_inc(t_evac, 1)

                        def exps(b):
                            act.wait_ge(neg_ready, b + 1)
                            i = b % 2
                            for n in range(heads(b)):
                                for tb, lo, hi in ((0, 0, P), (1, P, 3 * P)):
                                    act.activation(probs[:, i, n, lo:hi], probs[:, i, n, lo:hi], ACT.Exp,
                                                   bias=neg[:, i, tb, n:n + 1], accum_out=den[:, i, tb, n:n + 1])
                            act.activation(ex[:, i, :, 0:heads(b)], ex[:, i, :, 0:heads(b)],
                                           ACT.Exp).then_inc(exp_ready, 1)

                        def pv_out(b):
                            first, n = t_count(("pv", b))
                            for i in range(n):
                                act.wait_ge(t_ready, first + i + 1)
                                u = (4 * b if b < 4 else 16 + 3 * (b - 4)) + i
                                if u >= 2:
                                    act.wait_ge(pv_mm, u - 1)
                                act.copy(pts[:, u % 2, :], ps[:, 4 + (first + i) % 2, 0:384]).then_inc(t_evac, 1)

                        def o_high(b):
                            for p in pairs_of(b):
                                act.wait_ge(o_ready, p + 1)
                                kb = p if p < 8 else 14 + p - 8
                                act.copy(ahi[:, kb, :], ps[:, 6 + p % 2, 0:S]).then_inc(o_hi, 1)

                        qk_out(0)
                        act.wait_ge(gates_ready, 1)
                        for b in range(9):
                            if b + 1 < 8:
                                qk_out(b + 1)
                            if b == 0:
                                exps(0)
                            if b + 1 < 8:
                                exps(b + 1)
                            if b < 8:
                                pv_out(b)
                                o_high(b)

                        def high_p(j):
                            high(j, BANK, 16 * (j // 8 + 1), j - 1)
                        for j in range(68, 78):
                            high_p(j)
                        for i in range(3):
                            act.wait_ge(obt_ready, i + 1)
                            act.copy(ahi[:, 8 + 2 * i:10 + 2 * i, :].rearrange("p k t -> p (k t)"),
                                     ps[:, i, :]).then_inc(obt_hi, 1)
                        for j in range(78, 86):
                            high_p(j)
                        for i in range(4):
                            act.wait_ge(mt_ready, i + 1)
                            act.copy(ahi[:, 2 * i:2 * i + 2, :].rearrange("p k t -> p (k t)"),
                                     ps[:, i, :]).then_inc(mt_hi, 1)
                        for j in range(86, 92):
                            high_p(j)

                    @block.vector
                    def _(dve):
                        link = chain(dve, dve_step)
                        rms_inverse(None, dve, link, None)
                        dve.wait_ge(small_in, 48)
                        for k in range(KB):
                            dve.wait_ge(turned_hi, k // 2 * 2 + 2)
                            dve.scalar_tensor_tensor(out=alo[:, k, :], in0=ps[:, k // 2, (k % 2) * S:(k % 2) * S + S],
                                                     scalar=gain[:, k:k + 1], in1=ahi[:, k, :].bitcast(F32),
                                                     op0=ALU.mult, op1=ALU.subtract).then_inc(turned_lo, 1)

                        def low(jj, w, ready):
                            dve.wait_ge(hi_ready, ready)
                            dve.tensor_tensor(wlo[:, jj % 2, 0:2 * w], half_slot(jj, w),
                                              whi[:, jj % 2, 0:2 * w].bitcast(F32), ALU.subtract).then_inc(low_split, 1)

                        def z_out(bank, c, w, done):
                            dve.wait_ge(z_ready, done)
                            cols = ds(c * BANK, w)
                            dve.tensor_tensor(z[:, 1, cols], ps[:, bank + 1, 0:w], z[:, 0, cols], ALU.add).then_inc(z_evac, 1)
                            dve.tensor_tensor(z[:, 0, cols], ps[:, bank, 0:w], z[:, 0, cols], ALU.add).then_inc(z_evac, 1)

                        for j in range(8):
                            low(j, BANK, j + 1)
                            if j == 5:
                                dve.wait_ge(bias_in, 16)
                                z_out(0, 0, BANK, 1)
                        with dve.Fori(1, CHUNKS // 2) as it:
                            for j in range(8):
                                low(j, BANK, it * 8 + (j + 1))
                                if j == 1:
                                    z_out(2, it * 2 - 1, BANK, it * 2)
                                if j == 5:
                                    z_out(0, it * 2, BANK, it * 2 + 1)
                        for j in range(64, Z_CONV):
                            low(j, TAIL, j + 1)
                            if j == 65:
                                z_out(2, CHUNKS - 1, BANK, CHUNKS)
                        z_out(0, CHUNKS, TAIL, CHUNKS + 1)

                        dve.wait_ge(gelu_done, 1)
                        for tb in range(TB):
                            for h in range(2):
                                last = dve.bn_stats(stats[:, tb, h, :], z[:, tb, ZN + 384 * h:ZN + 384 * (h + 1)])
                        link(last)
                        for tb in range(TB):
                            last = dve.bn_aggr(mv[:, tb, :], stats[:, tb, :, :])
                        link(last)
                        link(dve.tensor_scalar(mv[:, :, 1], mv[:, :, 1], EPS, None, ALU.add))
                        dve.reciprocal(mv[:, :, 1], mv[:, :, 1]).then_inc(lnv_ready, 1)
                        dve.wait_ge(ln_root, 1)
                        for tb in range(TB):
                            v = z[:, tb, ZN:ZN + B_W]
                            last = dve.tensor_scalar(v, v, mv[:, tb, 0:1], mv[:, tb, 1:2], ALU.subtract, ALU.mult)
                        last.then_inc(vn_ready, 1)

                        def softmax_in(b):
                            i, n = b % 2, heads(b)
                            dve.wait_ge(s_ready, b + 1)
                            if b >= 2:
                                dve.wait_ge(pv_turned, b - 1)
                            mask = bcast(mask_a[:].unsqueeze(1), [P, 4, 384]) if b < 4 else mask_c[:]
                            ins = dve.scalar_tensor_tensor(out=probs[:, i, 0:n, :], in0=ps[:, 0:n, 0:384],
                                                           scalar=SCALE, in1=mask, op0=ALU.mult, op1=ALU.add)
                            ins.then_inc(s_free, 1)
                            dve.wait_ge(s_free, b + 1)
                            dve.tensor_reduce(mx[:, i, 0, 0:n], probs[:, i, 0:n, 0:P], AX, ALU.max)
                            link(dve.tensor_reduce(mx[:, i, 1, 0:n], probs[:, i, 0:n, P:3 * P], AX, ALU.max))
                            m = mx[:, i, :, 0:n]
                            if b < 4:
                                sk = bcast(sinks[:, 4 * b:4 * b + 4].unsqueeze(1), [P, TB, 4])
                                link(dve.tensor_tensor(m, m, sk, ALU.max))
                                dve.tensor_tensor(ex[:, i, :, :], sk, m, ALU.subtract)
                            else:
                                link(dve.tensor_reduce(mxg[:, i, :], m, AX, ALU.max))
                                dve.tensor_tensor(ex[:, i, :, 0:n], m, bcast(mxg[:, i, :].unsqueeze(2), [P, TB, n]),
                                                  ALU.subtract)
                            dve.tensor_scalar(neg[:, i, :, 0:n], m, -1.0, None, ALU.mult).then_inc(neg_ready, 1)

                        def softmax_out(b):
                            i, n = b % 2, heads(b)
                            dve.wait_ge(exp_ready, b + 1)
                            d, e = den[:, i, :, 0:n], ex[:, i, :, 0:n]
                            if b < 4:
                                link(dve.tensor_tensor(d, d, e, ALU.add))
                                link(dve.reciprocal(d, d))
                            else:
                                link(dve.tensor_tensor(d, d, e, ALU.mult))
                                link(dve.tensor_reduce(mxg[:, i, :], d, AX, ALU.add))
                                link(dve.reciprocal(mxg[:, i, :], mxg[:, i, :]))
                                link(dve.tensor_tensor(d, e, bcast(mxg[:, i, :].unsqueeze(2), [P, TB, n]), ALU.mult))
                            for tb, lo, hi in ((0, 0, P), (1, P, 3 * P)):
                                p = probs[:, i, 0:n, lo:hi]
                                last = dve.tensor_tensor(p, p, bcast(den[:, i, tb, 0:n].unsqueeze(2), [P, n, hi - lo]),
                                                         ALU.mult)
                            last.then_inc(p_ready, 1)

                        def o_low(b):
                            for p in pairs_of(b):
                                dve.wait_ge(o_hi, p + 1)
                                kb = p if p < 8 else 14 + p - 8
                                dve.tensor_tensor(alo[:, kb, :], ps[:, 6 + p % 2, 0:S],
                                                  ahi[:, kb, :].bitcast(F32), ALU.subtract).then_inc(o_lo, 1)

                        softmax_in(0)
                        for b in range(8):
                            if b + 1 < 8:
                                softmax_in(b + 1)
                            softmax_out(b)
                            if b >= 1:
                                o_low(b - 1)
                        o_low(7)

                        low(68, BANK, 69)
                        low(69, BANK, 70)
                        dve.wait_ge(sv_ready, 1)
                        for g in range(B_GROUPS):
                            u = z[:, :, ZU + HD * g:ZU + HD * (g + 1)]
                            sv = ps[:, g // 4, (g % 4) * P:(g % 4 + 1) * P].rearrange("p (t c) -> p t c", t=TB)
                            last = dve.scalar_tensor_tensor(out=u, in0=sv, scalar=bsp[:, g:g + 1], in1=u,
                                                            op0=ALU.add, op1=ALU.mult)
                        last.then_inc(ob_ready, 1)
                        for j in range(70, 78):
                            low(j, BANK, j + 1)
                        for i in range(3):
                            dve.wait_ge(obt_hi, i + 1)
                            dve.tensor_tensor(alo[:, 8 + 2 * i:10 + 2 * i, :].rearrange("p k t -> p (k t)"), ps[:, i, :],
                                              ahi[:, 8 + 2 * i:10 + 2 * i, :].rearrange("p k t -> p (k t)").bitcast(F32),
                                              ALU.subtract).then_inc(obt_lo, 1)

                        dve.wait_ge(gates_ready, 1)

                        def gate(branch):
                            base = (4, 0, 4)[branch]
                            dve.wait_ge(proj_ready, branch + 1)
                            for q in range(4):
                                tb, nh = q // 2, q % 2
                                g = z[:, tb, ZG + branch * D + nh * BANK:ZG + branch * D + (nh + 1) * BANK]
                                to = work[:, tb, nh * BANK:(nh + 1) * BANK]
                                pr = ps[:, base + q, :]
                                if branch == 0:
                                    dve.tensor_tensor(to, pr, g, ALU.mult).then_inc(gated, 1)
                                    continue
                                dve.tensor_tensor(tmp[:, q % 2, :], pr, g, ALU.mult).then_inc(gated, 1)
                                dve.wait_ge(gated, branch * 4 + q + 1)
                                last = dve.tensor_tensor(to, to, tmp[:, q % 2, :], ALU.add)
                            if branch == 2:
                                last.then_inc(merged, 1)

                        gate(0)
                        for j in range(78, 84):
                            low(j, BANK, j + 1)
                        gate(1)
                        low(84, BANK, 85)
                        low(85, BANK, 86)
                        gate(2)
                        for i in range(4):
                            dve.wait_ge(mt_hi, i + 1)
                            dve.tensor_tensor(alo[:, 2 * i:2 * i + 2, :].rearrange("p k t -> p (k t)"), ps[:, i, :],
                                              ahi[:, 2 * i:2 * i + 2, :].rearrange("p k t -> p (k t)").bitcast(F32),
                                              ALU.subtract).then_inc(mt_lo, 1)
                        for j in range(86, 92):
                            low(j, BANK, j + 1)
                        dve.wait_ge(out_ready, 1)
                        for q in range(4):
                            to = xs[:, q // 2, (q % 2) * BANK:(q % 2 + 1) * BANK]
                            dve.tensor_tensor(to, ps[:, 4 + q, :], to, ALU.add)

                    @block.tensor
                    def _(pe):
                        pe.wait_ge(normed, 1)
                        for k in range(KB):
                            for tb in range(TB):
                                mm = pe.transpose(ps[:, k // 2, (k % 2) * S + tb * P:(k % 2) * S + (tb + 1) * P],
                                                  work[:, tb, k:D:KB], ident[:])
                            if k % 2:
                                mm.then_inc(turned, 1)
                        pe.wait_ge(tril_done, 1)
                        for g in range(B_GROUPS):
                            mm = pe.transpose(ps[:, 4 + g // 4, (g % 4) * P:(g % 4 + 1) * P], wsp[:, g, :], ident[:])
                            if g % 4 == 3:
                                mm.then_inc(wst_ready, 1)

                        def three_passes(o, kb, tb, rhs_hi, rhs_lo, first, last):
                            hi = ahi[:, kb, tb * P:(tb + 1) * P]
                            lo = alo[:, kb, tb * P:(tb + 1) * P]
                            pe.matmul(o, hi, rhs_hi, start=first, stop=False)
                            pe.matmul(o, hi, rhs_lo, start=False, stop=False)
                            return pe.matmul(o, lo, rhs_hi, start=False, stop=last)

                        def z_conv(jj, bank, w, ready):
                            pe.wait_ge(low_split, ready)
                            for kk in range(2):
                                kb = 2 * (jj % 4) + kk
                                for tb in range(TB):
                                    mm = three_passes(ps[:, bank + tb, 0:w], kb, tb, whi[:, jj % 2, kk * w:(kk + 1) * w],
                                                      wlo[:, jj % 2, kk * w:(kk + 1) * w], kb == 0, kb == KB - 1)
                            mm.then_inc(conv_used, 1)

                        pe.wait_ge(turned_lo, KB)
                        for j in range(8):
                            z_conv(j, 2 * (j // 4), BANK, j + 1)
                            if j % 4 == 3:
                                pe.wait_ge(conv_used, j + 1)
                                pe.sem_inc(z_ready, 1)
                        with pe.Fori(1, CHUNKS // 2) as it:
                            for j in range(8):
                                if j % 4 == 0:
                                    pe.wait_ge(z_evac, it * 4 + (-2 if j == 0 else 0))
                                z_conv(j, 2 * (j // 4), BANK, it * 8 + (j + 1))
                                if j % 4 == 3:
                                    pe.wait_ge(conv_used, it * 8 + (j + 1))
                                    pe.sem_inc(z_ready, 1)
                        pe.wait_ge(z_evac, 2 * (CHUNKS - 1))
                        for j in range(64, Z_CONV):
                            z_conv(j, 0, TAIL, j + 1)
                        pe.wait_ge(conv_used, Z_CONV)
                        pe.sem_inc(z_ready, 1)

                        pe.wait_ge(wst_evac, 3)
                        pe.wait_ge(z_evac, 2 * (CHUNKS + 1))

                        def bank_for(t):
                            if t >= 2:
                                pe.wait_ge(t_evac, t - 1)
                            return 4 + t % 2

                        def qk(b):
                            first, n = t_count(("qk", b))
                            if n == 0:
                                return
                            pe.wait_ge(roped, 1 if b < 4 else 2)
                            for i in range(n):
                                bank = bank_for(first + i)
                                for tb in range(TB):
                                    if b < 4 and i == 0:
                                        srcs = [z[:, tb, ZQ + (4 * b + 2 * pr) * HD:ZQ + (4 * b + 2 * pr + 2) * HD]
                                                for pr in range(2)]
                                    elif b < 4:
                                        srcs = [k_twice[:, tb, b, :]]
                                    else:
                                        h = C_PER * i + b - 4
                                        srcs = [z[:, tb, at + h * HD:at + (h + 2) * HD] for at in (CQ, CK)]
                                    for n_src, src in enumerate(srcs):
                                        mm = pe.transpose(ps[:, bank, n_src * S + tb * P:n_src * S + (tb + 1) * P],
                                                          src, ident[:])
                                mm.then_inc(t_ready, 1)

                        def scores(b):
                            src = b if b < 4 else 4 + 2 * ((b - 4) // 2)
                            first, n = t_count(("qk", src))
                            pe.wait_ge(t_evac, first + n)
                            if b >= 1:
                                pe.wait_ge(s_free, b)
                            for i in range(heads(b)):
                                r = HD * (i % 2 if b < 4 else b % 2)
                                rows = slice(r, r + HD)
                                q = (qkt[rows, 0, (i // 2) * S:(i // 2 + 1) * S] if b < 4 else qkt[rows, i, 0:S])
                                k = qkt[rows, 1, 0:S] if b < 4 else qkt[rows, i, S:2 * S]
                                pe.matmul(ps[:, i, 0:P], q[:, 0:P], k[:, 0:P], start=True, stop=True)
                                mm = pe.matmul(ps[:, i, P:3 * P], q[:, P:S], k[:, 0:S], start=True, stop=True)
                            mm.then_inc(s_ready, 1)

                        def pv(b):
                            first, n = t_count(("pv", b))
                            u0 = 4 * b if b < 4 else 16 + 3 * (b - 4)
                            pe.wait_ge(p_ready, b + 1)

                            def turn(i):
                                bank = bank_for(first + i)
                                for c in range(3):
                                    mm = pe.transpose(ps[:, bank, c * P:(c + 1) * P],
                                                      probs[:, b % 2, i, c * P:(c + 1) * P], ident[:])
                                mm.then_inc(t_ready, 1)

                            def product(i):
                                pe.wait_ge(t_evac, first + i + 1)
                                if b < 4:
                                    p, r, at, g0, g1 = 2 * b + i // 2, HD * (i % 2), ZV + b * HD, True, True
                                else:
                                    p, r, at = 8 + (b - 4) // 2, HD * (b % 2), CV + (C_PER * i + b - 4) * HD
                                    g0, g1 = i == 0, i == n - 1
                                if p >= 2:
                                    pe.wait_ge(o_lo, p - 1)
                                o = ps[r:r + HD, 6 + p % 2, 0:S]
                                pt = pts[:, (u0 + i) % 2, :]
                                pe.matmul(o, z[:, 0, at:at + HD], pt[:, 0:S], start=g0, stop=False)
                                mm = pe.matmul(o[:, P:S], z[:, 1, at:at + HD], pt[:, S:3 * P], start=False, stop=g1)
                                mm.then_inc(pv_mm, 1)

                            for i in range(n + 1):
                                if i < n:
                                    turn(i)
                                if i >= 1:
                                    product(i - 1)
                            pe.wait_ge(pv_mm, u0 + n)
                            pe.sem_inc(pv_turned, 1)
                            for p in pairs_of(b):
                                pe.sem_inc(o_ready, 1)

                        qk(0)
                        scores(0)
                        for b in range(8):
                            if b + 1 < 8:
                                qk(b + 1)
                                scores(b + 1)
                            pv(b)

                        pe.wait_ge(s_free, 8)
                        pe.wait_ge(v_ready, 1)
                        for g in range(B_GROUPS):
                            mm = pe.matmul(ps[:, g // 4, (g % 4) * P:(g % 4 + 1) * P], wst[:, g, :],
                                           z[:, :, ZN + HD * g:ZN + HD * (g + 1)], start=True, stop=True)
                        mm.then_inc(sv_ready, 1)

                        def project(j0, kb0, n, base):
                            for i in range(n):
                                j = j0 + i
                                pe.wait_ge(low_split, j + 1)
                                for tb in range(TB):
                                    for nh in range(2):
                                        mm = three_passes(ps[:, base + 2 * tb + nh, :], kb0 + i, tb,
                                                          whi[:, j % 2, nh * BANK:(nh + 1) * BANK],
                                                          wlo[:, j % 2, nh * BANK:(nh + 1) * BANK], i == 0, i == n - 1)
                                mm.then_inc(conv_used, 1)
                            pe.wait_ge(conv_used, j + 1)

                        pe.wait_ge(o_lo, 10)
                        project(68, 0, 8, 4)
                        pe.sem_inc(proj_ready, 1)
                        pe.wait_ge(ob_ready, 1)
                        for k in range(6):
                            for tb in range(TB):
                                mm = pe.transpose(ps[:, k // 2, (k % 2) * S + tb * P:(k % 2) * S + (tb + 1) * P],
                                                  z[:, tb, ZU + k * P:ZU + (k + 1) * P], ident[:])
                            if k % 2:
                                mm.then_inc(obt_ready, 1)
                        pe.wait_ge(obt_lo, 3)
                        project(76, 8, 6, 0)
                        pe.sem_inc(proj_ready, 1)
                        pe.wait_ge(gated, 4)
                        project(82, 14, 2, 4)
                        pe.sem_inc(proj_ready, 1)
                        pe.wait_ge(merged, 1)
                        for k in range(KB):
                            for tb in range(TB):
                                mm = pe.transpose(ps[:, k // 2, (k % 2) * S + tb * P:(k % 2) * S + (tb + 1) * P],
                                                  work[:, tb, k * P:(k + 1) * P], ident[:])
                            if k % 2:
                                mm.then_inc(mt_ready, 1)
                        pe.wait_ge(mt_lo, 4)
                        project(84, 0, 8, 4)
                        pe.sem_inc(out_ready, 1)
            end_of_stage()

        def expert_stage(l):
            with ExitStack() as ctx:
                xnh = sb("xnh", [P, TB, D], F32R, ctx)
                xnl = sb("xnl", [P, TB, D], F32R, ctx)
                with ExitStack() as rctx:
                    h2t = sb("h2t", [P, KB, S], F32, rctx)
                    wr = sb("wr", [P, KB, GROUPS + EXPERTS], F32, rctx)
                    lg = sb("lg", [P, TB, 8], F32, rctx)
                    le = sb("le", [P, TB, EXPERTS], F32, rctx)
                    top = sb("top", [P, TB, 8], F32, rctx)
                    top_i = sb("top_i", [P, TB, 8], U32, rctx)
                    gid = sb("gid", [P, TB, 8], F32, rctx)
                    gmask = sb("gmask", [P, TB, GROUPS], F32, rctx)
                    les = sb("les", [P, TB, 8], F32, rctx)
                    etop = sb("etop", [P, TB, 8], F32, rctx)
                    eid = sb("eid", [P, TB, 8], F32, rctx)
                    lse = sb("lse", [P, TB, 8], F32, rctx)
                    pg = sb("pg", [P, TB], F32, rctx)
                    w12 = sb("w12", [P, TB, 2], F32, rctx)
                    pick = sb("pick", [P, 2, TB, 8], F32, rctx)
                    sel = sb("sel", [P, TB, EXPERTS], F32, rctx)
                    wsel = sb("wsel", [P, TB, EXPERTS], F32, rctx)
                    big = sb("big", [P, TB, EXPERTS], F32, rctx)
                    cnt = sb("cnt", [P, 4], F32, rctx)

                    with nc.Block() as block:
                        @block.sync
                        def _(sp):
                            with nc.allow_non_contiguous_dma(reason="small parameters"):
                                sp.dma_start(gain[:], layer_of(norm2_g, l).rearrange("(p k) -> p k", k=KB)).then_inc(small_in, 16)
                                sp.dma_start(wr[:, :, 0:GROUPS], layer_of(w_router_group, l).rearrange(
                                    "(p k) n -> p k n", k=KB)).then_inc(small_in, 16)
                                sp.dma_start(wr[:, :, GROUPS:], layer_of(w_router_expert, l).rearrange(
                                    "(p k) n -> p k n", k=KB)).then_inc(small_in, 16)

                        @block.scalar
                        def _(act):
                            rms_inverse(act, None, "act", h2t[:].rearrange("p k s -> p (k s)").rearrange(
                                "p (t d) -> p t d", t=TB))
                            act.wait_ge(normed, 1)
                            act.copy(xnh[:], work[:]).then_inc(hi_ready, 1)
                            act.wait_ge(small_in, 48)
                            for i in range(4):
                                act.wait_ge(turned, i + 1)
                                for k in (2 * i, 2 * i + 1):
                                    last = act.activation(h2t[:, k, :], ps[:, i, (k % 2) * S:(k % 2) * S + S], ACT.Copy,
                                                          scale=gain[:, k:k + 1])
                            last.then_inc(h2t_ready, 1)
                            act.wait_ge(router_in, 1)
                            act.activation(lse[:], lse[:], ACT.Exp).then_inc(router_exp, 1)

                        @block.tensor
                        def _(pe):
                            pe.wait_ge(normed, 1)
                            for k in range(KB):
                                for tb in range(TB):
                                    mm = pe.transpose(ps[:, k // 2, (k % 2) * S + tb * P:(k % 2) * S + (tb + 1) * P],
                                                      work[:, tb, k:D:KB], ident[:])
                                if k % 2:
                                    mm.then_inc(turned, 1)
                            pe.wait_ge(h2t_ready, 1)
                            n = GROUPS + EXPERTS
                            for tb in range(TB):
                                for k in range(KB):
                                    mm = pe.matmul(ps[:, 4 + tb, 0:n], h2t[:, k, tb * P:(tb + 1) * P], wr[:, k, :],
                                                   start=(k == 0), stop=(k == KB - 1))
                            mm.then_inc(logits_ready, 1)
                            pe.wait_ge(picked, 1)
                            pe.matmul(ps[:, 6, 0:EXPERTS], before[:], sel[:, 0, :], start=True, stop=True)
                            pe.matmul(ps[:, 6, 64:64 + EXPERTS], before[:], sel[:, 1, :], start=True, stop=False)
                            pe.matmul(ps[:, 6, 64:64 + EXPERTS], ones[:], sel[:, 0, :], start=False, stop=True)
                            pe.matmul(ps[:, 6, 128:128 + EXPERTS], ones[:], sel[:, 0, :], start=True, stop=False)
                            pe.matmul(ps[:, 6, 128:128 + EXPERTS], ones[:], sel[:, 1, :], start=False,
                                      stop=True).then_inc(ranks_ready, 1)

                        @block.vector
                        def _(dve):
                            link = chain(dve, dve_step)
                            link(dve.memset(lg[:], -3e38))
                            rms_inverse(None, dve, link, None)
                            dve.wait_ge(hi_ready, 1)
                            dve.tensor_tensor(xnl[:], work[:], xnh[:].bitcast(F32), ALU.subtract)
                            dve.wait_ge(logits_ready, 1)
                            link(dve.tensor_copy(lg[:, :, 0:GROUPS], ps[:, 4:6, 0:GROUPS]))
                            dve.tensor_copy(le[:], ps[:, 4:6, GROUPS:GROUPS + EXPERTS])
                            for tb in range(TB):
                                link(dve.max(top[:, tb, :], lg[:, tb, :]))
                                link(dve.max_index(top_i[:, tb, :], top[:, tb, :], lg[:, tb, :]))
                            link(dve.tensor_copy(gid[:], top_i[:]))
                            link(dve.tensor_tensor(gmask[:], bcast(idx_iota[:, 0:GROUPS].unsqueeze(1), [P, TB, GROUPS]),
                                                   bcast(gid[:, :, 0:1], [P, TB, GROUPS]), ALU.is_equal))
                            for tb in range(TB):
                                link(dve.tensor_tensor(big[:, tb, :].rearrange("p (g e) -> p g e", g=GROUPS),
                                                       le[:, tb, :].rearrange("p (g e) -> p g e", g=GROUPS),
                                                       bcast(gmask[:, tb, :].unsqueeze(2), [P, GROUPS, PER_GROUP]), ALU.mult))
                                link(dve.tensor_reduce(les[:, tb, :], big[:, tb, :].rearrange("p (g e) -> p e g", g=GROUPS),
                                                       AX, ALU.add))
                                link(dve.max(etop[:, tb, :], les[:, tb, :]))
                                link(dve.max_index(top_i[:, tb, :], etop[:, tb, :], les[:, tb, :]))
                            link(dve.tensor_copy(eid[:], top_i[:]))
                            link(dve.tensor_tensor(lse[:, :, 0:GROUPS], lg[:, :, 0:GROUPS],
                                                   bcast(top[:, :, 0:1], [P, TB, GROUPS]), ALU.subtract))
                            dve.tensor_tensor(lse[:, :, GROUPS:], etop[:, :, 0:4], bcast(etop[:, :, 0:1], [P, TB, 4]),
                                              ALU.subtract).then_inc(router_in, 1)
                            dve.wait_ge(router_exp, 1)
                            link(dve.tensor_reduce(pg[:], lse[:, :, 0:GROUPS], AX, ALU.add))
                            link(dve.scalar_tensor_tensor(out=pg[:], in0=lse[:, :, GROUPS + 1], scalar=1.0, in1=pg[:],
                                                          op0=ALU.add, op1=ALU.mult))
                            link(dve.reciprocal(w12[:, :, 0], pg[:]))
                            link(dve.tensor_tensor(w12[:, :, 1], w12[:, :, 0], lse[:, :, GROUPS + 1], ALU.mult))
                            for c in range(2):
                                link(dve.tensor_tensor(pick[:, c, :, :], bcast(idx_iota[:].unsqueeze(1), [P, TB, 8]),
                                                       bcast(eid[:, :, c:c + 1], [P, TB, 8]), ALU.is_equal))
                            for tb in range(TB):
                                def by_group(t):
                                    return t[:, tb, :].rearrange("p (g e) -> p g e", g=GROUPS)
                                gm = bcast(gmask[:, tb, :].unsqueeze(2), [P, GROUPS, PER_GROUP])
                                link(dve.tensor_tensor(big[:, tb, 0:8], pick[:, 0, tb, :], pick[:, 1, tb, :], ALU.add))
                                link(dve.tensor_tensor(by_group(sel), bcast(big[:, tb, 0:8].unsqueeze(1), [P, GROUPS, 8]),
                                                       gm, ALU.mult))
                                link(dve.tensor_scalar(big[:, tb, 8:16], pick[:, 0, tb, :], w12[:, tb, 0:1], None, ALU.mult))
                                link(dve.scalar_tensor_tensor(out=big[:, tb, 16:24], in0=pick[:, 1, tb, :],
                                                              scalar=w12[:, tb, 1:2], in1=big[:, tb, 8:16],
                                                              op0=ALU.mult, op1=ALU.add))
                                link(dve.tensor_tensor(by_group(comb), bcast(big[:, tb, 16:24].unsqueeze(1), [P, GROUPS, 8]),
                                                       gm, ALU.mult))
                            dve.sem_inc(picked, 1)
                            dve.wait_ge(ranks_ready, 1)
                            for tb in range(TB):
                                link(dve.scalar_tensor_tensor(out=rk[:, tb, :], in0=ps[:, 6, 64 * tb:64 * tb + EXPERTS],
                                                              scalar=1.0, in1=sel[:, tb, :], op0=ALU.add, op1=ALU.mult))
                            link(dve.tensor_scalar(rk[:], rk[:], 1.0, None, ALU.subtract))
                            link(dve.tensor_reduce(cnt[:, 0:1], ps[:, 6, 128:128 + EXPERTS], AX, ALU.max))
                            for i in range(1, S // EC):
                                link(dve.tensor_scalar(cnt[:, i:i + 1], cnt[:, 0:1], float(EC * i), None, ALU.is_gt))
                            link(dve.tensor_reduce(cnt[:, 0:1], cnt[:, 1:S // EC], AX, ALU.add))
                            dve.tensor_scalar(rounds[:], cnt[:, 0:1], 1.0, None, ALU.add)
                n_rounds = nc.values_load(rounds[0:1, 0:1], min_val=1, max_val=S // EC)
                end_of_stage()

                RING = 12
                ring = sb("ring_e", [P, RING, SLOT], F32, ctx)
                onehot = sb("onehot", [P, TB, UNIT], F32R, ctx)
                xsel = sb("xsel", [P, KB, UNIT], F32, ctx)
                st = sb("st", [P, PAIRS, S], F32R, ctx)
                wslot = sb("wslot", [P, PAIRS], F32, ctx)
                sg = sb("sg", [P, 2, F], F32, ctx)
                a_sb = sb("a_sb", [P, 2, F], F32, ctx)
                at_sb = sb("at_sb", [P, 2, 2, P], F32, ctx)
                yh = sb("yh", [P, PAIRS, D], F32R, ctx)
                yl = sb("yl", [P, PAIRS, D], F32R, ctx)
                wg_l = layer_of(w_expert_gate, l)
                wu_l = layer_of(w_expert_up, l)
                wd_l = layer_of(w_expert_down, l)

                with nc.Fori(0, n_rounds) as _:
                    def units(eng, body):
                        body(0)
                        with eng.Fori(1, GROUPS) as u:
                            body(u)

                    def after(eng, s, u, per_unit, count):
                        if isinstance(u, int):
                            if per_unit * u + count > 0:
                                eng.wait_ge(s, per_unit * u + count)
                        else:
                            eng.wait_ge(s, u * per_unit + count)

                    with nc.Block() as block:
                        @block.sync
                        def _(sp):
                            def body(u):
                                for q in range(PAIRS):
                                    for i in range(6):
                                        n = 6 * q + i
                                        e = 2 * q + (i // 2 if i < 4 else i - 4)
                                        q_old = q - 2
                                        after(sp, gu_ready if i < 4 else y_ready, u, PAIRS if i < 4 else 2 * PAIRS,
                                              q_old + 1 if i < 4 else 2 * (q_old + 1))
                                        w = (wg_l, wu_l)[i % 2] if i < 4 else wd_l
                                        if isinstance(u, int):
                                            src = w[e + u * PER_GROUP]
                                        else:
                                            src = w[ds(u * PER_GROUP + e, 1)].squeeze(0)
                                        src = src.rearrange("(p k) f -> p (k f)", p=P)
                                        sp.dma_start(ring[:, n % RING, :], src).then_inc(ring_in[n % RING], 16)
                            units(sp, body)

                        @block.tensor
                        def _(pe):
                            def spread(q, u):
                                after(pe, st_evac, u, PAIRS, q)
                                for tb in range(TB):
                                    pe.transpose(ps[:, 6, tb * P:(tb + 1) * P],
                                                 onehot[:, tb, q * P:(q + 1) * P].bitcast(F32), ident[:])
                                for tb in range(TB):
                                    e = 2 * q if isinstance(u, int) else u * PER_GROUP + 2 * q
                                    rhs = comb[:, tb, ds(e, 2)] if not isinstance(e, int) else comb[:, tb, e:e + 2]
                                    mm = pe.matmul(ps[:, 6, S:S + 2], onehot[:, tb, q * P:(q + 1) * P].bitcast(F32),
                                                   rhs, start=(tb == 0), stop=(tb == TB - 1))
                                mm.then_inc(st_ready, 1)

                            def gate_up(q, u):
                                after(pe, a_ready, u, PAIRS, q - 1)
                                for i in range(4):
                                    slot = (6 * q + i) % RING
                                    n = (6 * q + i) // RING
                                    after(pe, ring_in[slot], u, 32, 16 * (n + 1))
                                for k in range(KB):
                                    for e in range(2):
                                        slot = (6 * q + 2 * e) % RING
                                        w = ring[:, slot:slot + 2, k * F:(k + 1) * F]
                                        c = (2 * q + e) * EC
                                        mm = pe.matmul(ps[e * EC:(e + 1) * EC, q % 2, :].rearrange("p (a f) -> p a f", a=2),
                                                       xsel[:, k, c:c + EC], w, start=(k == 0), stop=(k == KB - 1),
                                                       skip_group_check=True)
                                mm.then_inc(gu_ready, 1)

                            def down(q, u):
                                after(pe, a_ready, u, PAIRS, q + 1)
                                after(pe, at_evac, u, PAIRS, q)
                                for kf in range(2):
                                    mm = pe.transpose(ps[:, 7, kf * P:(kf + 1) * P], a_sb[:, q % 2, kf:F:2], ident[:])
                                mm.then_inc(at_ready, 1)
                                after(pe, at_evac, u, PAIRS, q + 1)
                                for i in (4, 5):
                                    slot = (6 * q + i) % RING
                                    after(pe, ring_in[slot], u, 32, 16 * ((6 * q + i) // RING + 1))
                                for nh in range(2):
                                    after(pe, y_lo, u, 2 * PAIRS, 2 * q + nh - 1)
                                    for kf in range(2):
                                        for e in range(2):
                                            slot = (6 * q + 4 + e) % RING
                                            w = ring[:, slot, kf * D + nh * BANK:kf * D + (nh + 1) * BANK]
                                            mm = pe.matmul(ps[e * EC:(e + 1) * EC, 2 + nh, :],
                                                           at_sb[:, q % 2, kf, e * EC:(e + 1) * EC], w, start=(kf == 0),
                                                           stop=(kf == 1), skip_group_check=True)
                                    mm.then_inc(y_ready, 1)

                            def body(u):
                                after(pe, onehot_ready, u, 1, 1)
                                for k in range(KB):
                                    if k >= 2:
                                        after(pe, gath_act if k % 2 == 0 else gath_dve, u, 4, k // 2)
                                    elif k == 0:
                                        after(pe, back_done, u, 4, 0)
                                    for tb in range(TB):
                                        for part, p in enumerate((xnh, xnl)):
                                            mm = pe.matmul(ps[:, 4 + k % 2, :], p[:, tb, k:D:KB], onehot[:, tb, :],
                                                           start=(tb == 0 and part == 0), stop=(tb == 1 and part == 1))
                                    mm.then_inc(gath_ready, 1)
                                spread(0, u)
                                after(pe, gath_act, u, 4, 4)
                                after(pe, gath_dve, u, 4, 4)
                                gate_up(0, u)
                                for q in range(PAIRS):
                                    if q + 1 < PAIRS:
                                        spread(q + 1, u)
                                        gate_up(q + 1, u)
                                    down(q, u)
                                after(pe, y_lo, u, 2 * PAIRS, 2 * PAIRS)
                                for q in range(4):
                                    tb, nh = q // 2, q % 2
                                    if q >= 2:
                                        after(pe, back_done, u, 4, q - 1)
                                    for p in range(PAIRS):
                                        for part, y in enumerate((yh, yl)):
                                            mm = pe.matmul(ps[:, 4 + q % 2, :], st[:, p, tb * P:(tb + 1) * P],
                                                           y[:, p, nh * BANK:(nh + 1) * BANK],
                                                           start=(p == 0 and part == 0), stop=(p == PAIRS - 1 and part == 1))
                                    mm.then_inc(back_ready, 1)
                            units(pe, body)

                        @block.scalar
                        def _(act):
                            def body(u):
                                for k in range(0, KB, 2):
                                    after(act, gath_ready, u, KB, k + 1)
                                    act.activation(xsel[:, k, :], ps[:, 4, :], ACT.Copy, scale=gain[:, k:k + 1]).then_inc(gath_act, 1)
                                for q in range(PAIRS + 1):
                                    if q < PAIRS:
                                        after(act, st_ready, u, PAIRS, q + 1)
                                        act.copy(st[:, q, :], ps[:, 6, 0:S])
                                        for e in range(2):
                                            rows = slice(e * EC, (e + 1) * EC)
                                            last = act.copy(wslot[rows, q:q + 1], ps[rows, 6, S + e:S + e + 1])
                                        last.then_inc(st_evac, 1)
                                        after(act, gu_ready, u, PAIRS, q + 1)
                                        after(act, a_ready, u, PAIRS, q - 1)
                                        act.activation(sg[:, q % 2, :], ps[:, q % 2, 0:F], ACT.Silu).then_inc(silu_done, 1)
                                    if q >= 1:
                                        after(act, at_ready, u, PAIRS, q)
                                        act.copy(at_sb[:, (q - 1) % 2, :, :].rearrange("p k s -> p (k s)"),
                                                 ps[:, 7, 0:2 * P]).then_inc(at_evac, 1)
                                        for nh in range(2):
                                            after(act, y_ready, u, 2 * PAIRS, 2 * (q - 1) + nh + 1)
                                            if q == 1 and nh == 0:
                                                after(act, back_ready, u, 4, 0)
                                            act.copy(yh[:, q - 1, nh * BANK:(nh + 1) * BANK], ps[:, 2 + nh, :]).then_inc(y_hi, 1)
                            units(act, body)

                        @block.vector
                        def _(dve):
                            def build(u):
                                for tb in range(TB):
                                    e = 0 if isinstance(u, int) else u * PER_GROUP
                                    r = rk[:, tb, ds(e, PER_GROUP)] if not isinstance(e, int) else rk[:, tb, 0:PER_GROUP]
                                    last = dve.tensor_tensor(
                                        onehot[:, tb, :].rearrange("p (e c) -> p e c", e=PER_GROUP),
                                        bcast(slot_iota[:].unsqueeze(1), [P, PER_GROUP, EC]),
                                        bcast(r.unsqueeze(2), [P, PER_GROUP, EC]), ALU.is_equal)
                                last.then_inc(onehot_ready, 1)

                            def body(u):
                                after(dve, st_ready, u, PAIRS, 0)
                                build(u)
                                for k in range(1, KB, 2):
                                    after(dve, gath_ready, u, KB, k + 1)
                                    dve.tensor_scalar(xsel[:, k, :], ps[:, 5, :], gain[:, k:k + 1], None,
                                                      ALU.mult).then_inc(gath_dve, 1)
                                for q in range(PAIRS + 1):
                                    if q < PAIRS:
                                        after(dve, silu_done, u, PAIRS, q + 1)
                                        after(dve, at_ready, u, PAIRS, q - 1)
                                        dve.scalar_tensor_tensor(out=a_sb[:, q % 2, :], in0=ps[:, q % 2, F:2 * F],
                                                                 scalar=wslot[:, q:q + 1], in1=sg[:, q % 2, :],
                                                                 op0=ALU.mult, op1=ALU.mult).then_inc(a_ready, 1)
                                    if q >= 1:
                                        for nh in range(2):
                                            after(dve, y_hi, u, 2 * PAIRS, 2 * (q - 1) + nh + 1)
                                            cols = slice(nh * BANK, (nh + 1) * BANK)
                                            dve.tensor_tensor(yl[:, q - 1, cols], ps[:, 2 + nh, :],
                                                              yh[:, q - 1, cols].bitcast(F32), ALU.subtract).then_inc(y_lo, 1)
                                for q in range(4):
                                    after(dve, back_ready, u, 4, q + 1)
                                    to = xs[:, q // 2, (q % 2) * BANK:(q % 2 + 1) * BANK]
                                    dve.tensor_tensor(to, ps[:, 4 + q % 2, :], to, ALU.add).then_inc(back_done, 1)
                            units(dve, body)
                            dve.tensor_scalar(rk[:], rk[:], float(EC), None, ALU.subtract)
                    end_of_stage()

        with nc.Fori(0, DEPTH) as l:
            trunk_stage(l)
            expert_stage(l)

        with ExitStack() as ctx:
            gf = sb("gf", [P, D], F32, ctx)
            junk = sb("junk", [P, TB, D], F32, ctx)
            with nc.Block() as block:
                @block.sync
                def _(sp):
                    sp.dma_start(gf[:], norm_f_g.partition_broadcast(P)).then_inc(small_in, 16)
                    sp.wait_ge(merged, 1)
                    sp.dma_start(out.rearrange("o (t p) d -> p (o t) d", p=P), work[:]).then_inc(out_done, 16)
                    sp.wait_ge(out_done, 16)

                @block.scalar
                def _(act):
                    rms_inverse(act, None, "act", junk[:])

                @block.vector
                def _(dve):
                    link = chain(dve, dve_step)
                    rms_inverse(None, dve, link, None)
                    dve.wait_ge(normed, 1)
                    dve.wait_ge(small_in, 16)
                    dve.tensor_tensor(work[:], work[:], bcast(gf[:].unsqueeze(1), [P, TB, D]), ALU.mult).then_inc(merged, 1)


_INS = ['x', 'positions', 'norm1_g', 'w_in', 'b_in', 'attn_sinks', 'sgu_ln_g', 'sgu_ln_b', 'w_spatial', 'b_spatial',
        'w_proj_a', 'w_proj_b', 'w_proj_c', 'w_out', 'norm2_g', 'w_router_group', 'w_router_expert', 'w_expert_gate',
        'w_expert_up', 'w_expert_down', 'norm_f_g']


def kernel(**inputs):
    import numpy as _np
    import concourse.bacc as _bacc
    from concourse import mybir as _mybir
    from concourse.bass_utils import run_bass_kernel_spmd as _run

    nc = _bacc.Bacc("TRN2", target_bir_lowering=False, num_devices=1)
    arrays, args = {}, []
    for name in _INS:
        a = _np.ascontiguousarray(inputs[name])
        arrays[f"in_{name}_dram"] = a
        args.append(nc.dram_tensor(f"in_{name}_dram", a.shape, _mybir.dt.from_np(a.dtype), kind="ExternalInput").ap())
    args.append(nc.dram_tensor("out_dram", inputs["x"].shape, _mybir.dt.float32, kind="ExternalOutput").ap())
    trunk_program(nc, *args)
    r = _run(nc, [arrays], core_ids=[0])
    return r.results[0]["out_dram"]
```

```python
from contextlib import ExitStack

import concourse.bass as bass
import numpy as np
from concourse import mybir

ALU = mybir.AluOpType
ACT = mybir.ActivationFunctionType
AX = mybir.AxisListType.X
F32 = mybir.dt.float32
F32R = mybir.dt.float32r
I32 = mybir.dt.int32
U32 = mybir.dt.uint32
ds = bass.ds

P = 128
HD = 64
ROT, HALF = 16, 8
THETA = 500000.0
EPS = 1e-5
NEG = -1e30
SCALE = HD ** -0.5
BANK = 512
SLOT = 2048

A_HEADS, A_KV, A_WIN = 16, 4, 128
B_GROUPS, B_W = 12, 768
C_PAIRS = ((128, 1), (512, 4), (2048, 16))
C_PER = 4
ZQ, ZK, ZV = 0, 1024, 1280
ZU, ZN = 1536, 2304
CQ, CK, CV = 3072, 3840, 4608
ZG = 5376

GROUPS, PER_GROUP, F = 4, 8, 256
EXPERTS = GROUPS * PER_GROUP
EC = 64
UNIT = PER_GROUP * EC
PAIRS = PER_GROUP // 2


def trunk_program(nc, x, positions, norm1_g, w_in, b_in, attn_sinks, sgu_ln_g, sgu_ln_b, w_spatial,
                  b_spatial, w_proj_a, w_proj_b, w_proj_c, w_out, norm2_g, w_router_group,
                  w_router_expert, w_expert_gate, w_expert_up, w_expert_down, norm_f_g, out):
    S, D = x.shape[1:]
    DEPTH, _, D_IN = w_in.shape
    TB, KB = S // P, D // P
    assert TB == 2 and KB == 8 and D_IN == ZG + 3 * D

    with ExitStack() as whole:
        def sb(name, shape, dt=F32, ctx=whole):
            return ctx.enter_context(nc.sbuf_tensor(name, shape, dt))

        sems = []

        def sem(name):
            s = whole.enter_context(nc.semaphore(name))
            sems.append(s)
            return s

        ps = whole.enter_context(nc.psum_tensor("ps", [P, 8, BANK], F32))

        xs = sb("xs", [P, TB, D])
        work = sb("work", [P, TB, D])
        ident = sb("ident", [P, P])
        ones = sb("ones", [P, P])
        before = sb("before", [P, P])
        mask_a = sb("mask_a", [P, 384])
        mask_c = sb("mask_c", [P, 3, 384])
        slot_iota = sb("slot_iota", [P, EC])
        idx_iota = sb("idx_iota", [P, PER_GROUP])
        cos = sb("cos", [P, TB, HALF])
        sin = sb("sin", [P, TB, HALF])
        ss = sb("ss", [P, TB])
        rstd = sb("rstd", [P, TB])
        gain = sb("gain", [P, KB])
        rk = sb("rk", [P, TB, EXPERTS])
        comb = sb("comb", [P, TB, EXPERTS])
        extra = sb("extra", [P, 1], I32)

        ring_in = [sem(f"ring_in{i}") for i in range(12)]
        small_in = sem("small_in")
        bias_in = sem("bias_in")
        wsp_in = sem("wsp_in")
        ln_in = sem("ln_in")
        dve_step = sem("dve_step")
        act_step = sem("act_step")
        pool_step = sem("pool_step")
        squares = sem("squares")
        recips = sem("recips")
        roots = sem("roots")
        normed = sem("normed")
        turned = sem("turned")
        turned_hi = sem("turned_hi")
        turned_lo = sem("turned_lo")
        hi_ready = sem("hi_ready")
        low_split = sem("low_split")
        conv_used = sem("conv_used")
        z_ready = sem("z_ready")
        z_evac = sem("z_evac")
        tril_done = sem("tril_done")
        wst_ready = sem("wst_ready")
        wst_evac = sem("wst_evac")
        gelu_done = sem("gelu_done")
        lnv_ready = sem("lnv_ready")
        ln_root = sem("ln_root")
        vn_ready = sem("vn_ready")
        v_ready = sem("v_ready")
        gates_ready = sem("gates_ready")
        roped = sem("roped")
        t_ready = sem("t_ready")
        t_evac = sem("t_evac")
        s_ready = sem("s_ready")
        s_free = sem("s_free")
        neg_ready = sem("neg_ready")
        exp_ready = sem("exp_ready")
        p_ready = sem("p_ready")
        pv_turned = sem("pv_turned")
        pv_mm = sem("pv_mm")
        o_ready = sem("o_ready")
        o_evac = sem("o_evac")
        o_hi = sem("o_hi")
        o_lo = sem("o_lo")
        sv_ready = sem("sv_ready")
        ob_ready = sem("ob_ready")
        obt_ready = sem("obt_ready")
        obt_hi = sem("obt_hi")
        obt_lo = sem("obt_lo")
        proj_ready = sem("proj_ready")
        gated = sem("gated")
        merged = sem("merged")
        mt_ready = sem("mt_ready")
        mt_hi = sem("mt_hi")
        mt_lo = sem("mt_lo")
        out_ready = sem("out_ready")
        logits_ready = sem("logits_ready")
        h2t_ready = sem("h2t_ready")
        router_exp = sem("router_exp")
        router_in = sem("router_in")
        picked = sem("picked")
        counted = sem("counted")
        ranks_ready = sem("ranks_ready")
        onehot_ready = sem("onehot_ready")
        onehot_used = sem("onehot_used")
        gath_ready = sem("gath_ready")
        gath_act = sem("gath_act")
        gath_dve = sem("gath_dve")
        st_ready = sem("st_ready")
        st_evac = sem("st_evac")
        gu_ready = sem("gu_ready")
        silu_done = sem("silu_done")
        a_ready = sem("a_ready")
        at_ready = sem("at_ready")
        at_evac = sem("at_evac")
        y_ready = sem("y_ready")
        y_hi = sem("y_hi")
        y_lo = sem("y_lo")
        back_ready = sem("back_ready")
        back_done = sem("back_done")
        out_done = sem("out_done")
        sem_range = range(min(s.num for s in sems), max(s.num for s in sems) + 1)

        def end_of_stage():
            nc.all_engine_barrier(sems_to_clear=sem_range)

        def chain(eng, s):
            count = [0]

            def link(ins):
                count[0] += 1
                ins.then_inc(s, 1)
                eng.wait_ge(s, count[0])
            return link

        def bcast(ap, shape):
            return ap.to_broadcast(shape)

        with ExitStack() as ctx:
            pos_i = sb("pos_i", [P, TB], I32, ctx)
            pos_f = sb("pos_f", [P, TB], F32, ctx)
            inv = sb("inv", [P, HALF], F32, ctx)
            ang = sb("ang", [P, TB, HALF], F32, ctx)
            turns = sb("turns", [P, TB, HALF], F32, ctx)
            folded = sb("folded", [P, TB, HALF], F32, ctx)
            dist_i = sb("dist_i", [P, 384], I32, ctx)
            dist = sb("dist", [P, 384], F32, ctx)
            rem_i = sb("rem_i", [P, 384], I32, ctx)
            rem = sb("rem", [P, 384], F32, ctx)
            causal = sb("causal", [P, 384], F32, ctx)
            within = sb("within", [P, 384], F32, ctx)
            iota_i = sb("iota_i", [P, EC], I32, ctx)
            iota8_i = sb("iota8_i", [P, PER_GROUP], I32, ctx)

            with nc.Block() as block:
                @block.sync
                def _(sp):
                    sp.dma_start(xs[:], x.rearrange("o (t p) d -> p (o t) d", p=P)).then_inc(ring_in[0], 16)
                    with nc.allow_non_contiguous_dma(reason="256 positions"):
                        sp.dma_start(pos_i[:], positions.rearrange("o (t p) -> p (o t)", p=P)).then_inc(small_in, 16)
                    sp.wait_ge(ring_in[0], 16)

                @block.gpsimd
                def _(pool):
                    link = chain(pool, pool_step)
                    link(pool.memset(ident[:], 0.0))
                    link(pool.affine_select(out=ident[:], in_=ident[:], compare_op=ALU.not_equal, fill=1.0,
                                            base=0, pattern=[[-1, P]], channel_multiplier=1))
                    link(pool.memset(ones[:], 1.0))
                    link(pool.affine_select(out=before[:], in_=ones[:], compare_op=ALU.is_gt, fill=0.0,
                                            base=0, pattern=[[1, P]], channel_multiplier=-1))
                    pool.iota(iota_i[:], pattern=[[1, EC]], base=0, channel_multiplier=0)
                    pool.iota(iota8_i[:], pattern=[[1, PER_GROUP]], base=0, channel_multiplier=0)
                    pool.iota(dist_i[:, 0:P], pattern=[[-1, P]], base=0, channel_multiplier=1)
                    pool.iota(dist_i[:, P:3 * P], pattern=[[-1, 2 * P]], base=P,
                              channel_multiplier=1).then_inc(tril_done, 1)

                @block.vector
                def _(dve):
                    link = chain(dve, dve_step)
                    dve.wait_ge(tril_done, 1)
                    dve.tensor_copy(slot_iota[:], iota_i[:])
                    dve.tensor_copy(idx_iota[:], iota8_i[:])
                    link(dve.tensor_copy(dist[:], dist_i[:]))
                    link(dve.tensor_scalar(causal[:], dist[:], 0.0, None, ALU.is_ge))

                    def finish_mask(m):
                        link(dve.tensor_scalar(m, within[:], 1.0, -NEG, ALU.subtract, ALU.mult))

                    link(dve.scalar_tensor_tensor(out=within[:], in0=dist[:], scalar=float(A_WIN - 1),
                                                  in1=causal[:], op0=ALU.is_le, op1=ALU.mult))
                    finish_mask(mask_a[:])
                    for g, (win, dil) in enumerate(C_PAIRS):
                        link(dve.tensor_scalar(rem_i[:], dist_i[:], dil - 1, None, ALU.bitwise_and))
                        link(dve.tensor_copy(rem[:], rem_i[:]))
                        link(dve.scalar_tensor_tensor(out=rem[:], in0=rem[:], scalar=0.0, in1=causal[:],
                                                      op0=ALU.is_equal, op1=ALU.mult))
                        link(dve.scalar_tensor_tensor(out=within[:], in0=dist[:], scalar=float(win),
                                                      in1=rem[:], op0=ALU.is_le, op1=ALU.mult))
                        finish_mask(mask_c[:, g, :])
                    for i in range(HALF):
                        f = float(np.float32(THETA) ** np.float32(-2.0 * i / ROT))
                        dve.memset(inv[:, i:i + 1], f)
                    dve.wait_ge(small_in, 16)
                    link(dve.tensor_copy(pos_f[:], pos_i[:]))
                    link(dve.tensor_tensor(ang[:], bcast(pos_f[:].unsqueeze(2), [P, TB, HALF]),
                                           bcast(inv[:].unsqueeze(1), [P, TB, HALF]), ALU.mult))
                    magic = 1.5 * 2.0 ** 23
                    link(dve.tensor_scalar(turns[:], ang[:], float(1 / (2 * np.pi)), magic, ALU.mult, ALU.add))
                    link(dve.tensor_scalar(turns[:], turns[:], magic, None, ALU.subtract))
                    c1 = 6.28125
                    c2 = float(np.round((2 * np.pi - c1) * 2 ** 20) / 2 ** 20)
                    c3 = float(2 * np.pi - c1 - c2)
                    for c in (c1, c2, c3):
                        link(dve.scalar_tensor_tensor(out=ang[:], in0=turns[:], scalar=-c, in1=ang[:],
                                                      op0=ALU.mult, op1=ALU.add))
                    link(dve.tensor_scalar(ang[:], ang[:], float(np.float32(3.1415925)),
                                           -float(np.float32(3.1415925)), ALU.min, ALU.max))
                    link(dve.tensor_scalar(folded[:], ang[:], -1.0, None, ALU.mult))
                    link(dve.tensor_tensor(folded[:], folded[:], ang[:], ALU.min))
                    link(dve.tensor_scalar(folded[:], folded[:], float(np.pi / 2), None, ALU.add))
                    dve.sem_inc(picked, 1)

                @block.scalar
                def _(act):
                    act.wait_ge(picked, 1)
                    act.activation(sin[:], ang[:], ACT.Sin)
                    act.activation(cos[:], folded[:], ACT.Sin)
            end_of_stage()

        def rms_inverse(act, dve, which, junk):
            if which == "act":
                for tb in range(TB):
                    last = act.activation(junk[:, tb, :], xs[:, tb, :], ACT.Square, accum_out=ss[:, tb:tb + 1])
                last.then_inc(squares, 1)
                act.wait_ge(recips, 1)
                act.activation(rstd[:], ss[:], ACT.Sqrt).then_inc(roots, 1)
            else:
                link = which
                dve.wait_ge(squares, 1)
                link(dve.tensor_scalar(ss[:], ss[:], 1.0 / D, EPS, ALU.mult, ALU.add))
                dve.reciprocal(ss[:], ss[:]).then_inc(recips, 1)
                dve.wait_ge(roots, 1)
                for tb in range(TB):
                    last = dve.tensor_scalar(work[:, tb, :], xs[:, tb, :], rstd[:, tb:tb + 1], None, ALU.mult)
                last.then_inc(normed, 1)

        def layer_of(w, l):
            return w[ds(l, 1)].squeeze(0)

        def trunk_stage(l):
            with ExitStack() as ctx:
                RING = 4
                Z_CONV = 68
                CHUNKS = 16
                AHEAD = 11
                BATCHES = 12
                TAIL = D_IN - CHUNKS * BANK
                ring = sb("ring_t", [P, RING, SLOT], F32, ctx)
                z = sb("z", [P, TB, D_IN], F32, ctx)
                whi = sb("whi", [P, 2, SLOT // 2], F32R, ctx)
                wlo = sb("wlo", [P, 2, SLOT // 2], F32R, ctx)
                ahi = sb("ahi", [P, 16, S], F32R, ctx)
                alo = sb("alo", [P, 16, S], F32R, ctx)
                wst = sb("wst", [P, B_GROUPS, P], F32, ctx)
                probs = sb("probs", [P, 2, 3, 384], F32, ctx)
                qkt = sb("qkt", [P, 3, BANK], F32, ctx)
                pts = sb("pts", [P, 2, 384], F32, ctx)
                tmp = sb("tmp", [P, 2, BANK], F32, ctx)
                k_twice = sb("k_twice", [P, TB, A_KV, 2 * HD], F32, ctx)
                sinks = sb("sinks", [P, A_HEADS], F32, ctx)
                bsp = sb("bsp", [P, B_GROUPS], F32, ctx)
                mx = sb("mx", [P, 2, TB, 4], F32, ctx)
                neg = sb("neg", [P, 2, TB, 4], F32, ctx)
                ex = sb("ex", [P, 2, TB, 4], F32, ctx)
                den = sb("den", [P, 2, TB, 4], F32, ctx)
                mxg = sb("mxg", [P, 2, TB], F32, ctx)
                stats = sb("stats", [P, TB, 2, 6], F32, ctx)
                mv = sb("mv", [P, TB, 2], F32, ctx)
                wsp = probs[:].rearrange("p a b c -> p (a b c)")[:, 0:B_GROUPS * P].rearrange(
                    "p (g s) -> p g s", g=B_GROUPS)
                ln_gb = work[:].rearrange("p t d -> p (t d)")[:, 0:2 * B_W].rearrange("p (n c) -> p n c", n=2)

                w_in_l = layer_of(w_in, l).rearrange("(p k) n -> p k n", k=KB)
                proj = ([(layer_of(w_proj_a, l), r) for r in range(4)]
                        + [(layer_of(w_proj_b, l), r) for r in range(3)]
                        + [(layer_of(w_proj_c, l), r) for r in range(1)]
                        + [(layer_of(w_out, l), r) for r in range(4)])

                def heads(b):
                    return 2 if b < 8 else 3

                def turned_before(b):
                    return 2 * b if b < 8 else 16 + 3 * (b - 8)

                def qk_banks(b):
                    return 1 if b < 8 else {8: 3, 10: 3}.get(b, 0)

                def t_first(kind, b):
                    n = sum(qk_banks(i) for i in range(b if kind == "qk" else min(b + 2, BATCHES)))
                    return n + turned_before(max(b - 1, 0) if kind == "qk" else b)

                def pairs_of(b):
                    return (b,) if b < 8 else {9: (8,), 11: (9,)}.get(b, ())

                with nc.Block() as block:
                    @block.sync
                    def _(sp):
                        sp.dma_start(wsp, layer_of(w_spatial, l).rearrange("g t s -> t g s")).then_inc(wsp_in, 16)
                        with nc.allow_non_contiguous_dma(reason="small parameters"):
                            sp.dma_start(gain[:], layer_of(norm1_g, l).rearrange("(p k) -> p k", k=KB)).then_inc(small_in, 16)
                            sp.dma_start(bsp[:], layer_of(b_spatial, l).rearrange("g t -> t g")).then_inc(small_in, 16)
                        sp.dma_start(sinks[:], layer_of(attn_sinks, l).partition_broadcast(P)).then_inc(small_in, 16)
                        sp.dma_start(z[:, 0, :], layer_of(b_in, l).partition_broadcast(P)).then_inc(bias_in, 16)

                        def load_z_item(s, it):
                            src = w_in_l[:, 4 * (s % 2):4 * (s % 2) + 4, ds(it * 2 * BANK + (s // 2) * BANK, BANK)]
                            dst = ring[:, s, :].rearrange("p (k n) -> p k n", k=4)
                            sp.dma_start(dst, src).then_inc(ring_in[s], 16)

                        for s in range(4):
                            load_z_item(s, 0)
                        sp.wait_ge(turned, 4)
                        sp.dma_start(ln_gb[:, 0, :], layer_of(sgu_ln_g, l).partition_broadcast(P)).then_inc(ln_in, 16)
                        sp.dma_start(ln_gb[:, 1, :], layer_of(sgu_ln_b, l).partition_broadcast(P)).then_inc(ln_in, 16)
                        with sp.Fori(1, CHUNKS // 2) as it:
                            for s in range(4):
                                sp.wait_ge(low_split, it * 8 + 2 * (s + 1) - 8)
                                load_z_item(s, it)
                        for half in range(2):
                            sp.wait_ge(low_split, 2 * (4 * 7 + half + 1))
                            src = w_in_l[:, 4 * half:4 * half + 4, CHUNKS * BANK:D_IN]
                            dst = ring[:, half, 0:4 * TAIL].rearrange("p (k n) -> p k n", k=4)
                            sp.dma_start(dst, src).then_inc(ring_in[half], 16)
                        for i, (w, r) in enumerate(proj):
                            item = 34 + i
                            sp.wait_ge(low_split, 2 * (item - 4 + 1))
                            src = w[2 * r * P:2 * (r + 1) * P, :].rearrange("(k p) n -> p k n", p=P)
                            dst = ring[:, item % 4, :].rearrange("p (k n) -> p k n", k=2)
                            sp.dma_start(dst, src).then_inc(ring_in[item % 4], 16)

                    @block.gpsimd
                    def _(pool):
                        link = chain(pool, pool_step)
                        pool.wait_ge(wsp_in, 16)
                        pool.affine_select(out=wsp, in_=wsp, compare_op=ALU.is_ge, fill=0.0, base=0,
                                           pattern=[[0, B_GROUPS], [-1, P]], channel_multiplier=1).then_inc(tril_done, 1)

                        def rope(first, n):
                            for tb in range(TB):
                                hd = z[:, tb, first:first + n * HD].rearrange("p (h c) -> p h c", c=HD)
                                t1, t2 = hd[:, :, 0:HALF], hd[:, :, HALF:ROT]
                                c = bcast(cos[:, tb, :].unsqueeze(1), [P, n, HALF])
                                s = bcast(sin[:, tb, :].unsqueeze(1), [P, n, HALF])
                                t1s = tmp[:, 0, 0:n * HALF].rearrange("p (h c) -> p h c", c=HALF)
                                t2s = tmp[:, 1, 0:n * HALF].rearrange("p (h c) -> p h c", c=HALF)
                                pool.tensor_tensor(t1s, t1, s, ALU.mult)
                                link(pool.tensor_tensor(t2s, t2, s, ALU.mult))
                                pool.tensor_tensor(t1, t1, c, ALU.mult)
                                link(pool.tensor_tensor(t2, t2, c, ALU.mult))
                                pool.tensor_tensor(t1, t1, t2s, ALU.subtract)
                                link(pool.tensor_tensor(t2, t2, t1s, ALU.add))

                        pool.wait_ge(z_evac, 2 * 3)
                        rope(ZQ, A_HEADS + A_KV)
                        k_heads = z[:, :, ZK:ZK + A_KV * HD].rearrange("p t (h c) -> p t h c", c=HD)
                        pool.tensor_copy(k_twice[:, :, :, 0:HD], k_heads)
                        pool.tensor_copy(k_twice[:, :, :, HD:2 * HD], k_heads).then_inc(roped, 1)
                        pool.wait_ge(z_evac, 2 * 9)
                        rope(CQ, 2 * 3 * C_PER)
                        pool.sem_inc(roped, 1)
                        v = z[:, :, ZN:ZN + B_W]
                        pool.wait_ge(vn_ready, 1)
                        pool.wait_ge(ln_in, 32)
                        link(pool.tensor_tensor(v, v, bcast(ln_gb[:, 0:1, :], [P, TB, B_W]), ALU.mult))
                        pool.tensor_tensor(v, v, bcast(ln_gb[:, 1:2, :], [P, TB, B_W]), ALU.add).then_inc(v_ready, 1)

                    def o_at(p, n):
                        at = ZQ + p * P if p < 8 else CQ + (p - 8) * P
                        return z[:, :, at:at + n * P]

                    def o_blocks(i):
                        return o_at(2 * i, 2).rearrange("p t (k c) -> p k t c", k=2)

                    def split_at(t, i):
                        kb = 2 * i if i < 4 else 14
                        return t[:, kb:kb + 2, :].rearrange("p k (t c) -> p k t c", t=TB)

                    def half_slot(j, w):
                        n = 2 * w
                        return ring[:, (j // 2) % RING, (j % 2) * n:(j % 2) * n + n]

                    @block.scalar
                    def _(act):
                        rms_inverse(act, None, "act", z[:, 1, 0:2 * D].rearrange("p (t d) -> p t d", t=TB))
                        act.wait_ge(small_in, 48)
                        for i in range(4):
                            act.wait_ge(turned, i + 1)
                            for k in (2 * i, 2 * i + 1):
                                act.activation(ahi[:, k, :], ps[:, i, (k % 2) * S:(k % 2) * S + S], ACT.Copy,
                                               scale=gain[:, k:k + 1]).then_inc(turned_hi, 1)
                        for i in range(3):
                            act.wait_ge(wst_ready, i + 1)
                            act.copy(wst[:, 4 * i:4 * i + 4, :].rearrange("p g t -> p (g t)"),
                                     ps[:, 4 + i, :]).then_inc(wst_evac, 1)

                        def high(jj, w, landed, used):
                            act.wait_ge(ring_in[(jj // 2) % RING], landed)
                            if used is not None:
                                act.wait_ge(conv_used, used)
                            act.copy(whi[:, jj % 2, 0:2 * w], half_slot(jj, w)).then_inc(hi_ready, 1)

                        for j in range(8):
                            high(j, BANK, 16, j - 1 if j >= 2 else None)
                        with act.Fori(1, AHEAD // 2) as it:
                            for j in range(8):
                                high(j, BANK, it * 16 + 16, it * 8 + (j - 1))

                        def high_at(j):
                            high(j, TAIL if 64 <= j < Z_CONV else BANK, 16 * (j // 8 + 1), j - 1)

                        high_at(40)
                        high_at(41)
                        act.wait_ge(z_evac, 2 * 6)
                        act.activation(z[:, :, ZN:ZN + B_W], z[:, :, ZN:ZN + B_W], ACT.Gelu_apprx_tanh).then_inc(gelu_done, 1)
                        high_at(42)
                        act.activation(z[:, :, ZU:ZU + B_W], z[:, :, ZU:ZU + B_W], ACT.Gelu_apprx_tanh).then_inc(gelu_done, 1)
                        high_at(43)
                        act.wait_ge(lnv_ready, 1)
                        act.activation(mv[:, :, 1], mv[:, :, 1], ACT.Sqrt).then_inc(ln_root, 1)
                        high_at(44)
                        high_at(45)

                        def qk_out(b):
                            for i in range(qk_banks(b)):
                                t = t_first("qk", b) + i
                                act.wait_ge(t_ready, t + 1)
                                to, w = (i, BANK) if b >= 8 else (b % 2, S if b % 2 else BANK)
                                act.copy(qkt[:, to, 0:w], ps[:, 3 + t % 2, 0:w]).then_inc(t_evac, 1)

                        def exps(b):
                            act.wait_ge(neg_ready, b + 1)
                            i = b % 2
                            for n in range(heads(b)):
                                for tb, lo, hi in ((0, 0, P), (1, P, 3 * P)):
                                    act.activation(probs[:, i, n, lo:hi], probs[:, i, n, lo:hi], ACT.Exp,
                                                   bias=neg[:, i, tb, n:n + 1], accum_out=den[:, i, tb, n:n + 1])
                            act.activation(ex[:, i, :, 0:heads(b)], ex[:, i, :, 0:heads(b)],
                                           ACT.Exp).then_inc(exp_ready, 1)

                        def pv_out(b, which):
                            for i in which:
                                t, u = t_first("pv", b) + i, turned_before(b) + i
                                act.wait_ge(t_ready, t + 1)
                                if u >= 2:
                                    act.wait_ge(pv_mm, u - 1)
                                act.copy(pts[:, u % 2, :], ps[:, 3 + t % 2, 0:384]).then_inc(t_evac, 1)

                        def o_out(b):
                            for p in pairs_of(b):
                                act.wait_ge(o_ready, p + 1)
                                act.copy(o_at(p, 1), ps[:, 5, 0:S].rearrange("p (t c) -> p t c", t=TB)).then_inc(o_evac, 1)

                        qk_out(0)
                        qk_out(1)
                        exps(0)
                        for b in range(BATCHES):
                            high_at(46 + 2 * b)
                            pv_out(b, range(2))
                            if b + 1 < BATCHES:
                                exps(b + 1)
                            pv_out(b, range(2, heads(b)))
                            o_out(b)
                            if b + 2 < BATCHES:
                                qk_out(b + 2)
                            high_at(47 + 2 * b)

                        def sigmoid(branch):
                            g = z[:, :, ZG + branch * D:ZG + (branch + 1) * D]
                            act.activation(g, g, ACT.Sigmoid).then_inc(gates_ready, 1)

                        act.wait_ge(conv_used, Z_CONV)
                        act.wait_ge(o_evac, 10)
                        for i in range(5):
                            act.copy(split_at(ahi, i), o_blocks(i)).then_inc(o_hi, 1)
                        act.wait_ge(z_evac, 2 * (CHUNKS + 1))
                        for j in range(70, 78):
                            if j % 2 == 1 and j < 77:
                                sigmoid((j - 71) // 2)
                            high_at(j)
                        for i in range(3):
                            act.wait_ge(obt_ready, i + 1)
                            act.copy(ahi[:, 8 + 2 * i:10 + 2 * i, :].rearrange("p k t -> p (k t)"),
                                     ps[:, i, :]).then_inc(obt_hi, 1)
                        for j in range(78, 86):
                            high_at(j)
                        for i in range(4):
                            act.wait_ge(mt_ready, i + 1)
                            act.copy(ahi[:, 2 * i:2 * i + 2, :].rearrange("p k t -> p (k t)"),
                                     ps[:, i, :]).then_inc(mt_hi, 1)
                        for j in range(86, 92):
                            high_at(j)

                    @block.vector
                    def _(dve):
                        link = chain(dve, dve_step)
                        rms_inverse(None, dve, link, None)
                        dve.wait_ge(small_in, 48)
                        for k in range(KB):
                            dve.wait_ge(turned_hi, k // 2 * 2 + 2)
                            dve.scalar_tensor_tensor(out=alo[:, k, :], in0=ps[:, k // 2, (k % 2) * S:(k % 2) * S + S],
                                                     scalar=gain[:, k:k + 1], in1=ahi[:, k, :].bitcast(F32),
                                                     op0=ALU.mult, op1=ALU.subtract).then_inc(turned_lo, 1)

                        def low(jj, w, ready):
                            dve.wait_ge(hi_ready, ready)
                            dve.tensor_tensor(wlo[:, jj % 2, 0:2 * w], half_slot(jj, w),
                                              whi[:, jj % 2, 0:2 * w].bitcast(F32), ALU.subtract).then_inc(low_split, 1)

                        def z_out(bank, c, w, done):
                            dve.wait_ge(z_ready, done)
                            cols = ds(c * BANK, w)
                            dve.tensor_tensor(z[:, 1, cols], ps[:, bank + 1, 0:w], z[:, 0, cols], ALU.add).then_inc(z_evac, 1)
                            dve.tensor_tensor(z[:, 0, cols], ps[:, bank, 0:w], z[:, 0, cols], ALU.add).then_inc(z_evac, 1)

                        for j in range(8):
                            low(j, BANK, j + 1)
                            if j == 5:
                                dve.wait_ge(bias_in, 16)
                                z_out(0, 0, BANK, 1)
                        with dve.Fori(1, AHEAD // 2) as it:
                            for j in range(8):
                                low(j, BANK, it * 8 + (j + 1))
                                if j == 1:
                                    z_out(2, it * 2 - 1, BANK, it * 2)
                                if j == 5:
                                    z_out(0, it * 2, BANK, it * 2 + 1)

                        def low_at(j):
                            low(j, TAIL if 64 <= j < Z_CONV else BANK, j + 1)

                        low_at(40)
                        low_at(41)
                        z_out(2, AHEAD - 2, BANK, AHEAD - 1)
                        low_at(42)
                        low_at(43)
                        dve.wait_ge(gelu_done, 1)
                        for tb in range(TB):
                            for h in range(2):
                                last = dve.bn_stats(stats[:, tb, h, :], z[:, tb, ZN + 384 * h:ZN + 384 * (h + 1)])
                        link(last)
                        for tb in range(TB):
                            last = dve.bn_aggr(mv[:, tb, :], stats[:, tb, :, :])
                        link(last)
                        link(dve.tensor_scalar(mv[:, :, 1], mv[:, :, 1], EPS, None, ALU.add))
                        dve.reciprocal(mv[:, :, 1], mv[:, :, 1]).then_inc(lnv_ready, 1)
                        low_at(44)
                        z_out(0, AHEAD - 1, BANK, AHEAD)
                        low_at(45)

                        def ln_apply():
                            dve.wait_ge(ln_root, 1)
                            for tb in range(TB):
                                v = z[:, tb, ZN:ZN + B_W]
                                last = dve.tensor_scalar(v, v, mv[:, tb, 0:1], mv[:, tb, 1:2], ALU.subtract, ALU.mult)
                            last.then_inc(vn_ready, 1)

                        def softmax_in(b):
                            i, n = b % 2, heads(b)
                            dve.wait_ge(s_ready, b + 1)
                            if b >= 2:
                                dve.wait_ge(pv_turned, b - 1)
                            mask = bcast(mask_a[:].unsqueeze(1), [P, n, 384]) if b < 8 else mask_c[:]
                            ins = dve.scalar_tensor_tensor(out=probs[:, i, 0:n, :], in0=ps[:, 0:n, 0:384],
                                                           scalar=SCALE, in1=mask, op0=ALU.mult, op1=ALU.add)
                            ins.then_inc(s_free, 1)
                            dve.wait_ge(s_free, b + 1)
                            dve.tensor_reduce(mx[:, i, 0, 0:n], probs[:, i, 0:n, 0:P], AX, ALU.max)
                            link(dve.tensor_reduce(mx[:, i, 1, 0:n], probs[:, i, 0:n, P:3 * P], AX, ALU.max))
                            m = mx[:, i, :, 0:n]
                            if b < 8:
                                sk = bcast(sinks[:, n * b:n * b + n].unsqueeze(1), [P, TB, n])
                                link(dve.tensor_tensor(m, m, sk, ALU.max))
                                dve.tensor_tensor(ex[:, i, :, 0:n], sk, m, ALU.subtract)
                            else:
                                link(dve.tensor_reduce(mxg[:, i, :], m, AX, ALU.max))
                                dve.tensor_tensor(ex[:, i, :, 0:n], m, bcast(mxg[:, i, :].unsqueeze(2), [P, TB, n]),
                                                  ALU.subtract)
                            dve.tensor_scalar(neg[:, i, :, 0:n], m, -1.0, None, ALU.mult).then_inc(neg_ready, 1)

                        def softmax_out(b):
                            i, n = b % 2, heads(b)
                            dve.wait_ge(exp_ready, b + 1)
                            d, e = den[:, i, :, 0:n], ex[:, i, :, 0:n]
                            if b < 8:
                                link(dve.tensor_tensor(d, d, e, ALU.add))
                                link(dve.reciprocal(d, d))
                            else:
                                link(dve.tensor_tensor(d, d, e, ALU.mult))
                                link(dve.tensor_reduce(mxg[:, i, :], d, AX, ALU.add))
                                link(dve.reciprocal(mxg[:, i, :], mxg[:, i, :]))
                                link(dve.tensor_tensor(d, e, bcast(mxg[:, i, :].unsqueeze(2), [P, TB, n]), ALU.mult))
                            for tb, lo, hi in ((0, 0, P), (1, P, 3 * P)):
                                p = probs[:, i, 0:n, lo:hi]
                                last = dve.tensor_tensor(p, p, bcast(den[:, i, tb, 0:n].unsqueeze(2), [P, n, hi - lo]),
                                                         ALU.mult)
                            last.then_inc(p_ready, 1)

                        softmax_in(0)
                        softmax_out(0)
                        for b in range(BATCHES):
                            if b + 1 < BATCHES:
                                softmax_in(b + 1)
                            low_at(46 + 2 * b)
                            if b == 0:
                                ln_apply()
                            if b % 2:
                                c = AHEAD + b // 2
                                z_out(6, c, TAIL if c == CHUNKS else BANK, c + 1)
                            if b + 1 < BATCHES:
                                softmax_out(b + 1)
                            low_at(47 + 2 * b)

                        for i in range(5):
                            dve.wait_ge(o_hi, i + 1)
                            dve.tensor_tensor(split_at(alo, i), o_blocks(i), split_at(ahi, i).bitcast(F32),
                                              ALU.subtract).then_inc(o_lo, 1)
                        dve.wait_ge(sv_ready, 1)
                        for g in range(B_GROUPS):
                            u = z[:, :, ZU + HD * g:ZU + HD * (g + 1)]
                            sv = ps[:, g // 4, (g % 4) * P:(g % 4 + 1) * P].rearrange("p (t c) -> p t c", t=TB)
                            last = dve.scalar_tensor_tensor(out=u, in0=sv, scalar=bsp[:, g:g + 1], in1=u,
                                                            op0=ALU.add, op1=ALU.mult)
                        last.then_inc(ob_ready, 1)
                        for j in range(70, 78):
                            low_at(j)
                        for i in range(3):
                            dve.wait_ge(obt_hi, i + 1)
                            dve.tensor_tensor(alo[:, 8 + 2 * i:10 + 2 * i, :].rearrange("p k t -> p (k t)"), ps[:, i, :],
                                              ahi[:, 8 + 2 * i:10 + 2 * i, :].rearrange("p k t -> p (k t)").bitcast(F32),
                                              ALU.subtract).then_inc(obt_lo, 1)

                        def gate(branch):
                            base = (4, 0, 4)[branch]
                            dve.wait_ge(gates_ready, branch + 1)
                            dve.wait_ge(proj_ready, branch + 1)
                            for q in range(4):
                                tb, nh = q // 2, q % 2
                                g = z[:, tb, ZG + branch * D + nh * BANK:ZG + branch * D + (nh + 1) * BANK]
                                to = work[:, tb, nh * BANK:(nh + 1) * BANK]
                                pr = ps[:, base + q, :]
                                if branch == 0:
                                    dve.tensor_tensor(to, pr, g, ALU.mult).then_inc(gated, 1)
                                    continue
                                dve.tensor_tensor(tmp[:, q % 2, :], pr, g, ALU.mult).then_inc(gated, 1)
                                dve.wait_ge(gated, branch * 4 + q + 1)
                                last = dve.tensor_tensor(to, to, tmp[:, q % 2, :], ALU.add)
                            if branch == 2:
                                last.then_inc(merged, 1)

                        gate(0)
                        for j in range(78, 84):
                            low(j, BANK, j + 1)
                        gate(1)
                        low(84, BANK, 85)
                        low(85, BANK, 86)
                        gate(2)
                        for i in range(4):
                            dve.wait_ge(mt_hi, i + 1)
                            dve.tensor_tensor(alo[:, 2 * i:2 * i + 2, :].rearrange("p k t -> p (k t)"), ps[:, i, :],
                                              ahi[:, 2 * i:2 * i + 2, :].rearrange("p k t -> p (k t)").bitcast(F32),
                                              ALU.subtract).then_inc(mt_lo, 1)
                        for j in range(86, 92):
                            low(j, BANK, j + 1)
                        dve.wait_ge(out_ready, 1)
                        for q in range(4):
                            to = xs[:, q // 2, (q % 2) * BANK:(q % 2 + 1) * BANK]
                            dve.tensor_tensor(to, ps[:, 4 + q, :], to, ALU.add)

                    @block.tensor
                    def _(pe):
                        pe.wait_ge(normed, 1)
                        for k in range(KB):
                            for tb in range(TB):
                                mm = pe.transpose(ps[:, k // 2, (k % 2) * S + tb * P:(k % 2) * S + (tb + 1) * P],
                                                  work[:, tb, k:D:KB], ident[:])
                            if k % 2:
                                mm.then_inc(turned, 1)
                        pe.wait_ge(tril_done, 1)
                        for g in range(B_GROUPS):
                            mm = pe.transpose(ps[:, 4 + g // 4, (g % 4) * P:(g % 4 + 1) * P], wsp[:, g, :], ident[:])
                            if g % 4 == 3:
                                mm.then_inc(wst_ready, 1)

                        def three_passes(o, kb, tb, rhs_hi, rhs_lo, first, last):
                            hi = ahi[:, kb, tb * P:(tb + 1) * P]
                            lo = alo[:, kb, tb * P:(tb + 1) * P]
                            pe.matmul(o, hi, rhs_hi, start=first, stop=False)
                            pe.matmul(o, hi, rhs_lo, start=False, stop=False)
                            return pe.matmul(o, lo, rhs_hi, start=False, stop=last)

                        def z_conv(jj, bank, w, ready):
                            pe.wait_ge(low_split, ready)
                            for kk in range(2):
                                kb = 2 * (jj % 4) + kk
                                for tb in range(TB):
                                    mm = three_passes(ps[:, bank + tb, 0:w], kb, tb, whi[:, jj % 2, kk * w:(kk + 1) * w],
                                                      wlo[:, jj % 2, kk * w:(kk + 1) * w], kb == 0, kb == KB - 1)
                            mm.then_inc(conv_used, 1)

                        pe.wait_ge(turned_lo, KB)
                        for j in range(8):
                            z_conv(j, 2 * (j // 4), BANK, j + 1)
                            if j % 4 == 3:
                                pe.wait_ge(conv_used, j + 1)
                                pe.sem_inc(z_ready, 1)
                        with pe.Fori(1, AHEAD // 2) as it:
                            for j in range(8):
                                if j % 4 == 0:
                                    pe.wait_ge(z_evac, it * 4 + (-2 if j == 0 else 0))
                                z_conv(j, 2 * (j // 4), BANK, it * 8 + (j + 1))
                                if j % 4 == 3:
                                    pe.wait_ge(conv_used, it * 8 + (j + 1))
                                    pe.sem_inc(z_ready, 1)
                        pe.wait_ge(z_evac, 2 * (AHEAD - 2))
                        for j in range(4 * (AHEAD - 1), 4 * AHEAD):
                            z_conv(j, 0, BANK, j + 1)
                        pe.wait_ge(conv_used, 4 * AHEAD)
                        pe.sem_inc(z_ready, 1)

                        pe.wait_ge(wst_evac, 3)

                        def gates_conv(j):
                            if j % 4 == 0 and j > 4 * AHEAD:
                                pe.wait_ge(z_evac, 2 * (j // 4))
                            z_conv(j, 6, TAIL if j >= 4 * CHUNKS else BANK, j + 1)
                            if j % 4 == 3:
                                pe.wait_ge(conv_used, j + 1)
                                pe.sem_inc(z_ready, 1)

                        def bank_for(t):
                            if t >= 2:
                                pe.wait_ge(t_evac, t - 1)
                            return 3 + t % 2

                        def qk(b):
                            pe.wait_ge(roped, 1 if b < 8 else 2)
                            for i in range(qk_banks(b)):
                                bank = bank_for(t_first("qk", b) + i)
                                for tb in range(TB):
                                    if b < 8:
                                        srcs = [z[:, tb, ZQ + 2 * b * HD:ZQ + (2 * b + 2) * HD]]
                                        if b % 2 == 0:
                                            srcs.append(k_twice[:, tb, b // 2, :])
                                    else:
                                        h = C_PER * i + b - 8
                                        srcs = [z[:, tb, at + h * HD:at + (h + 2) * HD] for at in (CQ, CK)]
                                    for n_src, src in enumerate(srcs):
                                        mm = pe.transpose(ps[:, bank, n_src * S + tb * P:n_src * S + (tb + 1) * P],
                                                          src, ident[:])
                                mm.then_inc(t_ready, 1)

                        def scores(b):
                            src = b if b < 8 else 8 + 2 * ((b - 8) // 2)
                            pe.wait_ge(t_evac, t_first("qk", src) + qk_banks(src))
                            if b >= 1:
                                pe.wait_ge(s_free, b)
                            for i in range(heads(b)):
                                r = HD * (i if b < 8 else b % 2)
                                rows = slice(r, r + HD)
                                q = qkt[rows, b % 2, 0:S] if b < 8 else qkt[rows, i, 0:S]
                                k = qkt[rows, 0 if b < 8 else i, S:2 * S]
                                pe.matmul(ps[:, i, 0:P], q[:, 0:P], k[:, 0:P], start=True, stop=True)
                                mm = pe.matmul(ps[:, i, P:3 * P], q[:, P:S], k[:, 0:S], start=True, stop=True)
                            mm.then_inc(s_ready, 1)

                        def pv(b, meanwhile):
                            n, u0 = heads(b), turned_before(b)
                            pe.wait_ge(p_ready, b + 1)

                            def turn(i):
                                bank = bank_for(t_first("pv", b) + i)
                                for c in range(3):
                                    mm = pe.transpose(ps[:, bank, c * P:(c + 1) * P],
                                                      probs[:, b % 2, i, c * P:(c + 1) * P], ident[:])
                                mm.then_inc(t_ready, 1)

                            def product(i):
                                pe.wait_ge(t_evac, t_first("pv", b) + i + 1)
                                if b < 8:
                                    p, r, at, g0, g1 = b, HD * i, ZV + b // 2 * HD, True, True
                                else:
                                    p, r, at = 8 + (b - 8) // 2, HD * (b % 2), CV + (C_PER * i + b - 8) * HD
                                    g0, g1 = i == 0, i == n - 1
                                if p >= 1:
                                    pe.wait_ge(o_evac, p)
                                o = ps[r:r + HD, 5, 0:S]
                                pt = pts[:, (u0 + i) % 2, :]
                                pe.matmul(o, z[:, 0, at:at + HD], pt[:, 0:S], start=g0, stop=False)
                                mm = pe.matmul(o[:, P:S], z[:, 1, at:at + HD], pt[:, S:3 * P], start=False, stop=g1)
                                mm.then_inc(pv_mm, 1)

                            turn(0)
                            turn(1)
                            meanwhile()
                            for i in range(n):
                                product(i)
                                if i + 2 < n:
                                    turn(i + 2)
                            pe.wait_ge(pv_mm, u0 + n)
                            pe.sem_inc(pv_turned, 1)
                            for p in pairs_of(b):
                                pe.sem_inc(o_ready, 1)

                        qk(0)
                        pe.wait_ge(z_evac, 2 * AHEAD)
                        scores(0)
                        qk(1)
                        for b in range(BATCHES):
                            gates_conv(44 + 2 * b)
                            if b + 1 < BATCHES:
                                scores(b + 1)
                            pv(b, lambda: gates_conv(45 + 2 * b))
                            if b + 2 < BATCHES:
                                qk(b + 2)

                        pe.wait_ge(s_free, BATCHES)
                        pe.wait_ge(v_ready, 1)
                        for g in range(B_GROUPS):
                            mm = pe.matmul(ps[:, g // 4, (g % 4) * P:(g % 4 + 1) * P], wst[:, g, :],
                                           z[:, :, ZN + HD * g:ZN + HD * (g + 1)], start=True, stop=True)
                        mm.then_inc(sv_ready, 1)

                        def project(j0, kb0, n, base):
                            for i in range(n):
                                j = j0 + i
                                if j0 == 68 and i % 2 == 0:
                                    pe.wait_ge(o_lo, i // 2 + 1)
                                pe.wait_ge(low_split, j + 1)
                                for tb in range(TB):
                                    for nh in range(2):
                                        mm = three_passes(ps[:, base + 2 * tb + nh, :], kb0 + i, tb,
                                                          whi[:, j % 2, nh * BANK:(nh + 1) * BANK],
                                                          wlo[:, j % 2, nh * BANK:(nh + 1) * BANK], i == 0, i == n - 1)
                                mm.then_inc(conv_used, 1)
                            pe.wait_ge(conv_used, j + 1)

                        pe.wait_ge(o_evac, 10)
                        pe.wait_ge(z_evac, 2 * (CHUNKS + 1))
                        project(68, 0, 8, 4)
                        pe.sem_inc(proj_ready, 1)
                        pe.wait_ge(ob_ready, 1)
                        for k in range(6):
                            for tb in range(TB):
                                mm = pe.transpose(ps[:, k // 2, (k % 2) * S + tb * P:(k % 2) * S + (tb + 1) * P],
                                                  z[:, tb, ZU + k * P:ZU + (k + 1) * P], ident[:])
                            if k % 2:
                                mm.then_inc(obt_ready, 1)
                        pe.wait_ge(obt_lo, 3)
                        project(76, 8, 6, 0)
                        pe.sem_inc(proj_ready, 1)
                        pe.wait_ge(gated, 4)
                        pe.wait_ge(o_lo, 5)
                        project(82, 14, 2, 4)
                        pe.sem_inc(proj_ready, 1)
                        pe.wait_ge(merged, 1)
                        for k in range(KB):
                            for tb in range(TB):
                                mm = pe.transpose(ps[:, k // 2, (k % 2) * S + tb * P:(k % 2) * S + (tb + 1) * P],
                                                  work[:, tb, k * P:(k + 1) * P], ident[:])
                            if k % 2:
                                mm.then_inc(mt_ready, 1)
                        pe.wait_ge(mt_lo, 4)
                        project(84, 0, 8, 4)
                        pe.sem_inc(out_ready, 1)
            end_of_stage()

        def expert_stage(l):
            with ExitStack() as ctx:
                xnh = sb("xnh", [P, TB, D], F32R, ctx)
                xnl = sb("xnl", [P, TB, D], F32R, ctx)
                wr = sb("wr", [P, KB, GROUPS + EXPERTS], F32, ctx)
                lg = sb("lg", [P, TB, 8], F32, ctx)
                le = sb("le", [P, TB, EXPERTS], F32, ctx)
                top = sb("top", [P, TB, 8], F32, ctx)
                top_i = sb("top_i", [P, TB, 8], U32, ctx)
                gid = sb("gid", [P, TB, 8], F32, ctx)
                gmask = sb("gmask", [P, TB, GROUPS], F32, ctx)
                les = sb("les", [P, TB, 8], F32, ctx)
                etop = sb("etop", [P, TB, 8], F32, ctx)
                eid = sb("eid", [P, TB, 8], F32, ctx)
                lse = sb("lse", [P, TB, 8], F32, ctx)
                pg = sb("pg", [P, TB], F32, ctx)
                w12 = sb("w12", [P, TB, 2], F32, ctx)
                pick = sb("pick", [P, 2, TB, 8], F32, ctx)
                sel = sb("sel", [P, TB, EXPERTS], F32, ctx)
                wsel = sb("wsel", [P, TB, EXPERTS], F32, ctx)
                big = sb("big", [P, TB, EXPERTS], F32, ctx)
                cnt = sb("cnt", [P, 4], F32, ctx)

                RING = 12
                ring = sb("ring_e", [P, RING, SLOT], F32, ctx)
                onehot = sb("onehot", [P, TB, UNIT], F32R, ctx)
                xsel = sb("xsel", [P, KB, UNIT], F32, ctx)
                h2t = xsel[:].rearrange("p k s -> p (k s)")[:, 0:KB * S].rearrange("p (k s) -> p k s", k=KB)
                st = sb("st", [P, PAIRS, S], F32R, ctx)
                wslot = sb("wslot", [P, PAIRS], F32, ctx)
                sg = sb("sg", [P, 2, F], F32, ctx)
                a_sb = sb("a_sb", [P, 2, F], F32, ctx)
                at_sb = sb("at_sb", [P, 2, 2, P], F32, ctx)
                yh = sb("yh", [P, PAIRS, D], F32R, ctx)
                yl = sb("yl", [P, PAIRS, D], F32R, ctx)
                wg_l = layer_of(w_expert_gate, l)
                wu_l = layer_of(w_expert_up, l)
                wd_l = layer_of(w_expert_down, l)

                def units(eng, body):
                    body(0)
                    with eng.Fori(1, GROUPS) as u:
                        body(u)

                def after(eng, s, u, per_unit, count):
                    if isinstance(u, int):
                        if per_unit * u + count > 0:
                            eng.wait_ge(s, per_unit * u + count)
                    else:
                        eng.wait_ge(s, u * per_unit + count)

                def route_sp(sp):
                    with nc.allow_non_contiguous_dma(reason="small parameters"):
                        sp.dma_start(gain[:], layer_of(norm2_g, l).rearrange("(p k) -> p k", k=KB)).then_inc(small_in, 16)
                        sp.dma_start(wr[:, :, 0:GROUPS], layer_of(w_router_group, l).rearrange(
                            "(p k) n -> p k n", k=KB)).then_inc(small_in, 16)
                        sp.dma_start(wr[:, :, GROUPS:], layer_of(w_router_expert, l).rearrange(
                            "(p k) n -> p k n", k=KB)).then_inc(small_in, 16)

                def route_act(act):
                    rms_inverse(act, None, "act", h2t[:].rearrange("p k s -> p (k s)").rearrange(
                        "p (t d) -> p t d", t=TB))
                    act.wait_ge(normed, 1)
                    act.copy(xnh[:], work[:]).then_inc(hi_ready, 1)
                    act.wait_ge(small_in, 48)
                    for i in range(4):
                        act.wait_ge(turned, i + 1)
                        for k in (2 * i, 2 * i + 1):
                            last = act.activation(h2t[:, k, :], ps[:, i, (k % 2) * S:(k % 2) * S + S], ACT.Copy,
                                                  scale=gain[:, k:k + 1])
                    last.then_inc(h2t_ready, 1)
                    act.wait_ge(router_in, 1)
                    act.activation(lse[:], lse[:], ACT.Exp).then_inc(router_exp, 1)

                def route_pe(pe):
                    pe.wait_ge(normed, 1)
                    for k in range(KB):
                        for tb in range(TB):
                            mm = pe.transpose(ps[:, k // 2, (k % 2) * S + tb * P:(k % 2) * S + (tb + 1) * P],
                                              work[:, tb, k:D:KB], ident[:])
                        if k % 2:
                            mm.then_inc(turned, 1)
                    pe.wait_ge(h2t_ready, 1)
                    n = GROUPS + EXPERTS
                    for tb in range(TB):
                        for k in range(KB):
                            mm = pe.matmul(ps[:, 4 + tb, 0:n], h2t[:, k, tb * P:(tb + 1) * P], wr[:, k, :],
                                           start=(k == 0), stop=(k == KB - 1))
                    mm.then_inc(logits_ready, 1)
                    pe.wait_ge(picked, 1)
                    pe.matmul(ps[:, 6, 0:EXPERTS], before[:], sel[:, 0, :], start=True, stop=True)
                    pe.matmul(ps[:, 6, 64:64 + EXPERTS], before[:], sel[:, 1, :], start=True, stop=False)
                    pe.matmul(ps[:, 6, 64:64 + EXPERTS], ones[:], sel[:, 0, :], start=False, stop=True)
                    pe.matmul(ps[:, 6, 128:128 + EXPERTS], ones[:], sel[:, 0, :], start=True, stop=False)
                    pe.matmul(ps[:, 6, 128:128 + EXPERTS], ones[:], sel[:, 1, :], start=False,
                              stop=True).then_inc(ranks_ready, 1)

                def route_dve(dve, link):
                    link(dve.memset(lg[:], -3e38))
                    rms_inverse(None, dve, link, None)
                    dve.wait_ge(hi_ready, 1)
                    dve.tensor_tensor(xnl[:], work[:], xnh[:].bitcast(F32), ALU.subtract)
                    dve.wait_ge(logits_ready, 1)
                    link(dve.tensor_copy(lg[:, :, 0:GROUPS], ps[:, 4:6, 0:GROUPS]))
                    dve.tensor_copy(le[:], ps[:, 4:6, GROUPS:GROUPS + EXPERTS])
                    for tb in range(TB):
                        link(dve.max(top[:, tb, :], lg[:, tb, :]))
                        link(dve.max_index(top_i[:, tb, :], top[:, tb, :], lg[:, tb, :]))
                    link(dve.tensor_copy(gid[:], top_i[:]))
                    link(dve.tensor_tensor(gmask[:], bcast(idx_iota[:, 0:GROUPS].unsqueeze(1), [P, TB, GROUPS]),
                                           bcast(gid[:, :, 0:1], [P, TB, GROUPS]), ALU.is_equal))
                    for tb in range(TB):
                        link(dve.tensor_tensor(big[:, tb, :].rearrange("p (g e) -> p g e", g=GROUPS),
                                               le[:, tb, :].rearrange("p (g e) -> p g e", g=GROUPS),
                                               bcast(gmask[:, tb, :].unsqueeze(2), [P, GROUPS, PER_GROUP]), ALU.mult))
                        link(dve.tensor_reduce(les[:, tb, :], big[:, tb, :].rearrange("p (g e) -> p e g", g=GROUPS),
                                               AX, ALU.add))
                        link(dve.max(etop[:, tb, :], les[:, tb, :]))
                        link(dve.max_index(top_i[:, tb, :], etop[:, tb, :], les[:, tb, :]))
                    link(dve.tensor_copy(eid[:], top_i[:]))
                    link(dve.tensor_tensor(lse[:, :, 0:GROUPS], lg[:, :, 0:GROUPS],
                                           bcast(top[:, :, 0:1], [P, TB, GROUPS]), ALU.subtract))
                    dve.tensor_tensor(lse[:, :, GROUPS:], etop[:, :, 0:4], bcast(etop[:, :, 0:1], [P, TB, 4]),
                                      ALU.subtract).then_inc(router_in, 1)
                    dve.wait_ge(router_exp, 1)
                    link(dve.tensor_reduce(pg[:], lse[:, :, 0:GROUPS], AX, ALU.add))
                    link(dve.scalar_tensor_tensor(out=pg[:], in0=lse[:, :, GROUPS + 1], scalar=1.0, in1=pg[:],
                                                  op0=ALU.add, op1=ALU.mult))
                    link(dve.reciprocal(w12[:, :, 0], pg[:]))
                    link(dve.tensor_tensor(w12[:, :, 1], w12[:, :, 0], lse[:, :, GROUPS + 1], ALU.mult))
                    for c in range(2):
                        link(dve.tensor_tensor(pick[:, c, :, :], bcast(idx_iota[:].unsqueeze(1), [P, TB, 8]),
                                               bcast(eid[:, :, c:c + 1], [P, TB, 8]), ALU.is_equal))
                    for tb in range(TB):
                        def by_group(t):
                            return t[:, tb, :].rearrange("p (g e) -> p g e", g=GROUPS)
                        gm = bcast(gmask[:, tb, :].unsqueeze(2), [P, GROUPS, PER_GROUP])
                        link(dve.tensor_tensor(big[:, tb, 0:8], pick[:, 0, tb, :], pick[:, 1, tb, :], ALU.add))
                        link(dve.tensor_tensor(by_group(sel), bcast(big[:, tb, 0:8].unsqueeze(1), [P, GROUPS, 8]),
                                               gm, ALU.mult))
                        link(dve.tensor_scalar(big[:, tb, 8:16], pick[:, 0, tb, :], w12[:, tb, 0:1], None, ALU.mult))
                        link(dve.scalar_tensor_tensor(out=big[:, tb, 16:24], in0=pick[:, 1, tb, :],
                                                      scalar=w12[:, tb, 1:2], in1=big[:, tb, 8:16],
                                                      op0=ALU.mult, op1=ALU.add))
                        link(dve.tensor_tensor(by_group(comb), bcast(big[:, tb, 16:24].unsqueeze(1), [P, GROUPS, 8]),
                                               gm, ALU.mult))
                    dve.sem_inc(picked, 1)
                    dve.wait_ge(ranks_ready, 1)
                    for tb in range(TB):
                        link(dve.scalar_tensor_tensor(out=rk[:, tb, :], in0=ps[:, 6, 64 * tb:64 * tb + EXPERTS],
                                                      scalar=1.0, in1=sel[:, tb, :], op0=ALU.add, op1=ALU.mult))
                    link(dve.tensor_scalar(rk[:], rk[:], 1.0, None, ALU.subtract))
                    link(dve.tensor_reduce(cnt[:, 0:1], ps[:, 6, 128:128 + EXPERTS], AX, ALU.max))
                    for i in range(1, S // EC):
                        link(dve.tensor_scalar(cnt[:, i:i + 1], cnt[:, 0:1], float(EC * i), None, ALU.is_gt))
                    dve.tensor_reduce(cnt[:, 0:1], cnt[:, 1:S // EC], AX, ALU.add).then_inc(counted, 1)
                    dve.wait_ge(counted, 1)
                    dve.tensor_copy(extra[:], cnt[:, 0:1])

                def round_sp(sp):
                    def body(u):
                        for q in range(PAIRS):
                            for i in range(6):
                                n = 6 * q + i
                                e = 2 * q + (i // 2 if i < 4 else i - 4)
                                q_old = q - 2
                                after(sp, gu_ready if i < 4 else y_ready, u, PAIRS if i < 4 else 2 * PAIRS,
                                      q_old + 1 if i < 4 else 2 * (q_old + 1))
                                w = (wg_l, wu_l)[i % 2] if i < 4 else wd_l
                                if isinstance(u, int):
                                    src = w[e + u * PER_GROUP]
                                else:
                                    src = w[ds(u * PER_GROUP + e, 1)].squeeze(0)
                                src = src.rearrange("(p k) f -> p (k f)", p=P)
                                sp.dma_start(ring[:, n % RING, :], src).then_inc(ring_in[n % RING], 16)
                    units(sp, body)

                def round_act(act):
                    def body(u):
                        for k in range(0, KB, 2):
                            after(act, gath_ready, u, KB, k + 1)
                            act.activation(xsel[:, k, :], ps[:, 4, :], ACT.Copy, scale=gain[:, k:k + 1]).then_inc(gath_act, 1)
                        for q in range(PAIRS + 1):
                            if q < PAIRS:
                                after(act, st_ready, u, PAIRS, q + 1)
                                act.copy(st[:, q, :], ps[:, 6, 0:S])
                                for e in range(2):
                                    rows = slice(e * EC, (e + 1) * EC)
                                    last = act.copy(wslot[rows, q:q + 1], ps[rows, 6, S + e:S + e + 1])
                                last.then_inc(st_evac, 1)
                                after(act, gu_ready, u, PAIRS, q + 1)
                                after(act, a_ready, u, PAIRS, q - 1)
                                act.activation(sg[:, q % 2, :], ps[:, q % 2, 0:F], ACT.Silu).then_inc(silu_done, 1)
                            if q >= 1:
                                after(act, at_ready, u, PAIRS, q)
                                act.copy(at_sb[:, (q - 1) % 2, :, :].rearrange("p k s -> p (k s)"),
                                         ps[:, 7, 0:2 * P]).then_inc(at_evac, 1)
                                for nh in range(2):
                                    after(act, y_ready, u, 2 * PAIRS, 2 * (q - 1) + nh + 1)
                                    if q == 1 and nh == 0:
                                        after(act, back_ready, u, 4, 0)
                                    act.copy(yh[:, q - 1, nh * BANK:(nh + 1) * BANK], ps[:, 2 + nh, :]).then_inc(y_hi, 1)
                    units(act, body)

                def round_pe(pe):
                    def spread(q, u):
                        after(pe, st_evac, u, PAIRS, q)
                        for tb in range(TB):
                            pe.transpose(ps[:, 6, tb * P:(tb + 1) * P],
                                         onehot[:, tb, q * P:(q + 1) * P].bitcast(F32), ident[:])
                        for tb in range(TB):
                            e = 2 * q if isinstance(u, int) else u * PER_GROUP + 2 * q
                            rhs = comb[:, tb, ds(e, 2)] if not isinstance(e, int) else comb[:, tb, e:e + 2]
                            mm = pe.matmul(ps[:, 6, S:S + 2], onehot[:, tb, q * P:(q + 1) * P].bitcast(F32),
                                           rhs, start=(tb == 0), stop=(tb == TB - 1))
                        mm.then_inc(st_ready, 1)

                    def gate_up(q, u):
                        after(pe, a_ready, u, PAIRS, q - 1)
                        for i in range(4):
                            slot = (6 * q + i) % RING
                            n = (6 * q + i) // RING
                            after(pe, ring_in[slot], u, 32, 16 * (n + 1))
                        for k in range(KB):
                            for e in range(2):
                                slot = (6 * q + 2 * e) % RING
                                w = ring[:, slot:slot + 2, k * F:(k + 1) * F]
                                c = (2 * q + e) * EC
                                mm = pe.matmul(ps[e * EC:(e + 1) * EC, q % 2, :].rearrange("p (a f) -> p a f", a=2),
                                               xsel[:, k, c:c + EC], w, start=(k == 0), stop=(k == KB - 1),
                                               skip_group_check=True)
                        mm.then_inc(gu_ready, 1)

                    def down(q, u):
                        after(pe, a_ready, u, PAIRS, q + 1)
                        after(pe, at_evac, u, PAIRS, q)
                        for kf in range(2):
                            mm = pe.transpose(ps[:, 7, kf * P:(kf + 1) * P], a_sb[:, q % 2, kf:F:2], ident[:])
                        mm.then_inc(at_ready, 1)
                        after(pe, at_evac, u, PAIRS, q + 1)
                        for i in (4, 5):
                            slot = (6 * q + i) % RING
                            after(pe, ring_in[slot], u, 32, 16 * ((6 * q + i) // RING + 1))
                        for nh in range(2):
                            after(pe, y_lo, u, 2 * PAIRS, 2 * q + nh - 1)
                            for kf in range(2):
                                for e in range(2):
                                    slot = (6 * q + 4 + e) % RING
                                    w = ring[:, slot, kf * D + nh * BANK:kf * D + (nh + 1) * BANK]
                                    mm = pe.matmul(ps[e * EC:(e + 1) * EC, 2 + nh, :],
                                                   at_sb[:, q % 2, kf, e * EC:(e + 1) * EC], w, start=(kf == 0),
                                                   stop=(kf == 1), skip_group_check=True)
                            mm.then_inc(y_ready, 1)

                    def body(u):
                        after(pe, onehot_ready, u, 1, 1)
                        for k in range(KB):
                            if k >= 2:
                                after(pe, gath_act if k % 2 == 0 else gath_dve, u, 4, k // 2)
                            elif k == 0:
                                after(pe, back_done, u, 4, 0)
                            for tb in range(TB):
                                for part, p in enumerate((xnh, xnl)):
                                    mm = pe.matmul(ps[:, 4 + k % 2, :], p[:, tb, k:D:KB], onehot[:, tb, :],
                                                   start=(tb == 0 and part == 0), stop=(tb == 1 and part == 1))
                            mm.then_inc(gath_ready, 1)
                        spread(0, u)
                        after(pe, gath_act, u, 4, 4)
                        after(pe, gath_dve, u, 4, 4)
                        gate_up(0, u)
                        for q in range(PAIRS):
                            if q + 1 < PAIRS:
                                spread(q + 1, u)
                                gate_up(q + 1, u)
                            down(q, u)
                        after(pe, y_lo, u, 2 * PAIRS, 2 * PAIRS)
                        for q in range(4):
                            tb, nh = q // 2, q % 2
                            if q >= 2:
                                after(pe, back_done, u, 4, q - 1)
                            for p in range(PAIRS):
                                for part, y in enumerate((yh, yl)):
                                    mm = pe.matmul(ps[:, 4 + q % 2, :], st[:, p, tb * P:(tb + 1) * P],
                                                   y[:, p, nh * BANK:(nh + 1) * BANK],
                                                   start=(p == 0 and part == 0), stop=(p == PAIRS - 1 and part == 1))
                            mm.then_inc(back_ready, 1)
                    units(pe, body)

                def round_dve(dve, link):
                    def build(u):
                        for tb in range(TB):
                            e = 0 if isinstance(u, int) else u * PER_GROUP
                            r = rk[:, tb, ds(e, PER_GROUP)] if not isinstance(e, int) else rk[:, tb, 0:PER_GROUP]
                            last = dve.tensor_tensor(
                                onehot[:, tb, :].rearrange("p (e c) -> p e c", e=PER_GROUP),
                                bcast(slot_iota[:].unsqueeze(1), [P, PER_GROUP, EC]),
                                bcast(r.unsqueeze(2), [P, PER_GROUP, EC]), ALU.is_equal)
                        last.then_inc(onehot_ready, 1)

                    def body(u):
                        after(dve, st_ready, u, PAIRS, 0)
                        build(u)
                        for k in range(1, KB, 2):
                            after(dve, gath_ready, u, KB, k + 1)
                            dve.tensor_scalar(xsel[:, k, :], ps[:, 5, :], gain[:, k:k + 1], None,
                                              ALU.mult).then_inc(gath_dve, 1)
                        for q in range(PAIRS + 1):
                            if q < PAIRS:
                                after(dve, silu_done, u, PAIRS, q + 1)
                                after(dve, at_ready, u, PAIRS, q - 1)
                                dve.scalar_tensor_tensor(out=a_sb[:, q % 2, :], in0=ps[:, q % 2, F:2 * F],
                                                         scalar=wslot[:, q:q + 1], in1=sg[:, q % 2, :],
                                                         op0=ALU.mult, op1=ALU.mult).then_inc(a_ready, 1)
                            if q >= 1:
                                for nh in range(2):
                                    after(dve, y_hi, u, 2 * PAIRS, 2 * (q - 1) + nh + 1)
                                    cols = slice(nh * BANK, (nh + 1) * BANK)
                                    dve.tensor_tensor(yl[:, q - 1, cols], ps[:, 2 + nh, :],
                                                      yh[:, q - 1, cols].bitcast(F32), ALU.subtract).then_inc(y_lo, 1)
                        for q in range(4):
                            after(dve, back_ready, u, 4, q + 1)
                            to = xs[:, q // 2, (q % 2) * BANK:(q % 2 + 1) * BANK]
                            dve.tensor_tensor(to, ps[:, 4 + q % 2, :], to, ALU.add).then_inc(back_done, 1)
                    units(dve, body)
                    dve.tensor_scalar(rk[:], rk[:], float(EC), None, ALU.subtract)

                def one_round(routed):
                    with nc.Block() as block:
                        @block.sync
                        def _(sp):
                            if not routed:
                                route_sp(sp)
                            round_sp(sp)

                        @block.scalar
                        def _(act):
                            if not routed:
                                route_act(act)
                            round_act(act)

                        @block.tensor
                        def _(pe):
                            if not routed:
                                route_pe(pe)
                            round_pe(pe)

                        @block.vector
                        def _(dve):
                            link = chain(dve, dve_step)
                            if not routed:
                                route_dve(dve, link)
                            round_dve(dve, link)

                one_round(routed=False)
                n_extra = nc.values_load(extra[0:1, 0:1], min_val=0, max_val=S // EC - 1)
                end_of_stage()
                with nc.If(n_extra > 0):
                    with nc.Fori(0, n_extra) as _:
                        one_round(routed=True)
                        end_of_stage()

        with nc.Fori(0, DEPTH) as l:
            trunk_stage(l)
            expert_stage(l)

        with ExitStack() as ctx:
            gf = sb("gf", [P, D], F32, ctx)
            junk = sb("junk", [P, TB, D], F32, ctx)
            with nc.Block() as block:
                @block.sync
                def _(sp):
                    sp.dma_start(gf[:], norm_f_g.partition_broadcast(P)).then_inc(small_in, 16)
                    sp.wait_ge(merged, 1)
                    sp.dma_start(out.rearrange("o (t p) d -> p (o t) d", p=P), work[:]).then_inc(out_done, 16)
                    sp.wait_ge(out_done, 16)

                @block.scalar
                def _(act):
                    rms_inverse(act, None, "act", junk[:])

                @block.vector
                def _(dve):
                    link = chain(dve, dve_step)
                    rms_inverse(None, dve, link, None)
                    dve.wait_ge(normed, 1)
                    dve.wait_ge(small_in, 16)
                    dve.tensor_tensor(work[:], work[:], bcast(gf[:].unsqueeze(1), [P, TB, D]), ALU.mult).then_inc(merged, 1)


_INS = ['x', 'positions', 'norm1_g', 'w_in', 'b_in', 'attn_sinks', 'sgu_ln_g', 'sgu_ln_b', 'w_spatial', 'b_spatial',
        'w_proj_a', 'w_proj_b', 'w_proj_c', 'w_out', 'norm2_g', 'w_router_group', 'w_router_expert', 'w_expert_gate',
        'w_expert_up', 'w_expert_down', 'norm_f_g']


def kernel(**inputs):
    import numpy as _np
    import concourse.bacc as _bacc
    from concourse import mybir as _mybir
    from concourse.bass_utils import run_bass_kernel_spmd as _run

    nc = _bacc.Bacc("TRN2", target_bir_lowering=False, num_devices=1)
    arrays, args = {}, []
    for name in _INS:
        a = _np.ascontiguousarray(inputs[name])
        arrays[f"in_{name}_dram"] = a
        args.append(nc.dram_tensor(f"in_{name}_dram", a.shape, _mybir.dt.from_np(a.dtype), kind="ExternalInput").ap())
    args.append(nc.dram_tensor("out_dram", inputs["x"].shape, _mybir.dt.float32, kind="ExternalOutput").ap())
    trunk_program(nc, *args)
    r = _run(nc, [arrays], core_ids=[0])
    return r.results[0]["out_dram"]
```

```python
from contextlib import ExitStack

import concourse.bass as bass
import numpy as np
from concourse import mybir

ALU = mybir.AluOpType
ACT = mybir.ActivationFunctionType
AX = mybir.AxisListType.X
F32 = mybir.dt.float32
F32R = mybir.dt.float32r
I32 = mybir.dt.int32
U32 = mybir.dt.uint32
ds = bass.ds

P = 128
HD = 64
ROT, HALF = 16, 8
THETA = 500000.0
EPS = 1e-5
NEG = -1e30
SCALE = HD ** -0.5
BANK = 512
SLOT = 2048

A_HEADS, A_KV, A_WIN = 16, 4, 128
B_GROUPS, B_W = 12, 768
C_PAIRS = ((128, 1), (512, 4), (2048, 16))
C_PER = 4
ZQ, ZK, ZV = 0, 1024, 1280
ZU, ZN = 1536, 2304
CQ, CK, CV = 3072, 3840, 4608
ZG = 5376

GROUPS, PER_GROUP, F = 4, 8, 256
EXPERTS = GROUPS * PER_GROUP
EC = 64
UNIT = PER_GROUP * EC
PAIRS = PER_GROUP // 2


def trunk_program(nc, x, positions, norm1_g, w_in, b_in, attn_sinks, sgu_ln_g, sgu_ln_b, w_spatial,
                  b_spatial, w_proj_a, w_proj_b, w_proj_c, w_out, norm2_g, w_router_group,
                  w_router_expert, w_expert_gate, w_expert_up, w_expert_down, norm_f_g, out):
    S, D = x.shape[1:]
    DEPTH, _, D_IN = w_in.shape
    TB, KB = S // P, D // P
    assert TB == 2 and KB == 8 and D_IN == ZG + 3 * D

    with ExitStack() as whole:
        def sb(name, shape, dt=F32, ctx=whole):
            return ctx.enter_context(nc.sbuf_tensor(name, shape, dt))

        sems = []

        def sem(name):
            s = whole.enter_context(nc.semaphore(name))
            sems.append(s)
            return s

        ps = whole.enter_context(nc.psum_tensor("ps", [P, 8, BANK], F32))

        xs = sb("xs", [P, TB, D])
        work = sb("work", [P, TB, D])
        warm = sb("warm", [P, 1])
        RING_T, RING_E = 4, 12
        arena = sb("arena", [P, TB * D_IN + RING_T * SLOT])
        experts_ring = arena[:, 0:RING_E * SLOT].rearrange("p (s n) -> p s n", s=RING_E)
        ident = sb("ident", [P, P])
        ones = sb("ones", [P, P], F32R)
        before = sb("before", [P, P], F32R)
        mask_a = sb("mask_a", [P, 384])
        mask_c = sb("mask_c", [P, 3, 384])
        slot_iota = sb("slot_iota", [P, EC])
        idx_iota = sb("idx_iota", [P, PER_GROUP])
        cos = sb("cos", [P, TB, HALF])
        sin = sb("sin", [P, TB, HALF])
        ss = sb("ss", [P, 2, TB])
        rstd = sb("rstd", [P, TB])
        gain = sb("gain", [P, KB])
        gain2 = sb("gain2", [P, KB])
        gains1 = sb("gains1", [P, DEPTH, KB])
        WR = 64
        wr = sb("wr", [P, KB, WR])
        rk = sb("rk", [P, TB, EXPERTS])
        comb = sb("comb", [P, TB, EXPERTS])
        extra = sb("extra", [P, 1], I32)

        ring_in = [sem(f"ring_in{i}") for i in range(12)]
        gain_in = sem("gain_in")
        small_in = sem("small_in")
        bias_in = sem("bias_in")
        bias_rest_in = sem("bias_rest_in")
        wsp_in = sem("wsp_in")
        ln_in = sem("ln_in")
        dve_step = sem("dve_step")
        pool_step = sem("pool_step")
        squares = sem("squares")
        recips = sem("recips")
        roots = sem("roots")
        turned = sem("turned")
        turned_hi = sem("turned_hi")
        turned_lo = sem("turned_lo")
        hi_ready = sem("hi_ready")
        low_first = sem("low_first")
        low_split = sem("low_split")
        conv_used = sem("conv_used")
        z_ready = sem("z_ready")
        z_evac = sem("z_evac")
        tril_done = sem("tril_done")
        wst_ready = sem("wst_ready")
        wst_evac = sem("wst_evac")
        gelu_done = sem("gelu_done")
        lnv_ready = sem("lnv_ready")
        ln_root = sem("ln_root")
        vn_ready = sem("vn_ready")
        v_ready = sem("v_ready")
        gates_ready = sem("gates_ready")
        roped = sem("roped")
        t_ready = sem("t_ready")
        t_evac = sem("t_evac")
        s_ready = sem("s_ready")
        s_free = sem("s_free")
        neg_ready = sem("neg_ready")
        exp_ready = sem("exp_ready")
        p_ready = sem("p_ready")
        pv_turned = sem("pv_turned")
        pv_mm = sem("pv_mm")
        o_ready = sem("o_ready")
        o_evac = sem("o_evac")
        o_hi = sem("o_hi")
        o_lo = sem("o_lo")
        sv_ready = sem("sv_ready")
        ob_ready = sem("ob_ready")
        obt_ready = sem("obt_ready")
        obt_hi = sem("obt_hi")
        obt_lo = sem("obt_lo")
        quarter_ready = sem("quarter_ready")
        gated = sem("gated")
        merged = sem("merged")
        mt_ready = sem("mt_ready")
        mt_hi = sem("mt_hi")
        mt_lo = sem("mt_lo")
        ahead_in = sem("ahead_in")
        x_quarter = sem("x_quarter")
        logits_ready = sem("logits_ready")
        h2t_ready = sem("h2t_ready")
        router_exp = sem("router_exp")
        router_in = sem("router_in")
        picked = sem("picked")
        pool_done = sem("pool_done")
        lgt_ready = sem("lgt_ready")
        lgt_evac = sem("lgt_evac")
        comb_ready = sem("comb_ready")
        totals_ready = sem("totals_ready")
        ranks_ready = sem("ranks_ready")
        onehot_ready = sem("onehot_ready")
        first_onehot = sem("first_onehot")
        first_ready = sem("first_ready")
        first_act = sem("first_act")
        first_dve = sem("first_dve")
        gath_ready = sem("gath_ready")
        gath_act = sem("gath_act")
        gath_dve = sem("gath_dve")
        st_ready = sem("st_ready")
        st_evac = sem("st_evac")
        gu_ready = sem("gu_ready")
        silu_done = sem("silu_done")
        a_ready = sem("a_ready")
        at_ready = sem("at_ready")
        at_evac = sem("at_evac")
        y_ready = sem("y_ready")
        y_hi = sem("y_hi")
        y_lo = sem("y_lo")
        back_ready = sem("back_ready")
        back_done = sem("back_done")
        out_done = sem("out_done")
        sem_range = range(min(s.num for s in sems), max(s.num for s in sems) + 1)

        def end_of_stage():
            nc.all_engine_barrier(sems_to_clear=sem_range)

        def chain(eng, s):
            count = [0]

            def link(ins):
                count[0] += 1
                ins.then_inc(s, 1)
                eng.wait_ge(s, count[0])
            return link

        def bcast(ap, shape):
            return ap.to_broadcast(shape)

        def quarter(t, q):
            return t[:, q % 2, q // 2 * BANK:(q // 2 + 1) * BANK]

        def k_major(t, tb):
            return t[:, tb, :].rearrange("p (c k) -> p k c", k=KB)

        def keep_clock(pe, n):
            for _ in range(n):
                pe.matmul(ps[:, 7, 0:2 * P], ident[:], mask_a[:, 0:2 * P], start=True, stop=True)

        WARM_SETUP, WARM_TRUNK, WARM_ROUTE = 12, 6, 8

        def load_sqrt_table(act):
            act.activation(warm[:], warm[:], ACT.Sqrt)

        def norm_act(act, x_done, junk):
            for q in range(4):
                x_done(q)
                last = act.activation(junk(q), quarter(xs, q), ACT.Square, accum_out=ss[:, q // 2, q % 2:q % 2 + 1])
            last.then_inc(squares, 1)
            act.wait_ge(recips, 1)
            act.activation(rstd[:], ss[:, 0, :], ACT.Sqrt).then_inc(roots, 1)
            act.wait_ge(roots, 1)
            act.activation(work[:, 1, :].rearrange("p (k c) -> p k c", k=KB), k_major(xs, 1), ACT.Copy,
                           scale=rstd[:, 1:2])

        def norm_dve(dve, link):
            dve.wait_ge(squares, 1)
            link(dve.tensor_tensor(ss[:, 0, :], ss[:, 0, :], ss[:, 1, :], ALU.add))
            link(dve.tensor_scalar(ss[:, 0, :], ss[:, 0, :], 1.0 / D, EPS, ALU.mult, ALU.add))
            dve.reciprocal(ss[:, 0, :], ss[:, 0, :]).then_inc(recips, 1)
            dve.wait_ge(roots, 1)
            dve.tensor_scalar(work[:, 0, :].rearrange("p (k c) -> p k c", k=KB), k_major(xs, 0), rstd[:, 0:1],
                              None, ALU.mult)

        with ExitStack() as ctx:
            ones_f = sb("ones_f", [P, P], F32, ctx)
            before_f = sb("before_f", [P, P], F32, ctx)
            pos_i = sb("pos_i", [P, TB], I32, ctx)
            pos_f = sb("pos_f", [P, TB], F32, ctx)
            inv = sb("inv", [P, HALF], F32, ctx)
            ang = sb("ang", [P, TB, HALF], F32, ctx)
            turns = sb("turns", [P, TB, HALF], F32, ctx)
            folded = sb("folded", [P, TB, HALF], F32, ctx)
            dist_i = sb("dist_i", [P, 384], I32, ctx)
            dist = sb("dist", [P, 384], F32, ctx)
            rem_i = sb("rem_i", [P, 384], I32, ctx)
            rem = sb("rem", [P, 384], F32, ctx)
            causal = sb("causal", [P, 384], F32, ctx)
            within = sb("within", [P, 384], F32, ctx)
            iota_i = sb("iota_i", [P, EC], I32, ctx)
            iota8_i = sb("iota8_i", [P, PER_GROUP], I32, ctx)

            with nc.Block() as block:
                @block.sync
                def _(sp):
                    sp.dma_start(xs[:], x.rearrange("o (t p) d -> p (o t) d", p=P)).then_inc(ring_in[0], 16)
                    with nc.allow_non_contiguous_dma(reason="256 positions"):
                        sp.dma_start(gains1[:], norm1_g.rearrange("l (p k) -> p l k", k=KB)).then_inc(gain_in, 16)
                        sp.dma_start(pos_i[:], positions.rearrange("o (t p) -> p (o t)", p=P)).then_inc(small_in, 16)
                    sp.wait_ge(gain_in, 16)
                @block.gpsimd
                def _(pool):
                    link = chain(pool, pool_step)
                    pool.iota(dist_i[:, 0:P], pattern=[[-1, P]], base=0, channel_multiplier=1)
                    pool.iota(dist_i[:, P:3 * P], pattern=[[-1, 2 * P]], base=P,
                              channel_multiplier=1).then_inc(tril_done, 1)
                    pool.iota(iota_i[:], pattern=[[1, EC]], base=0, channel_multiplier=0)
                    pool.iota(iota8_i[:], pattern=[[1, PER_GROUP]], base=0, channel_multiplier=0)
                    pool.memset(wr[:, :, GROUPS + EXPERTS:], 0.0)
                    link(pool.memset(ident[:], 0.0))
                    link(pool.affine_select(out=ident[:], in_=ident[:], compare_op=ALU.not_equal, fill=1.0,
                                            base=0, pattern=[[-1, P]], channel_multiplier=1))
                    link(pool.memset(ones_f[:], 1.0))
                    pool.affine_select(out=before_f[:], in_=ones_f[:], compare_op=ALU.is_gt, fill=0.0,
                                       base=0, pattern=[[1, P]], channel_multiplier=-1).then_inc(pool_done, 1)

                @block.tensor
                def _(pe):
                    pe.wait_ge(merged, 1)
                    keep_clock(pe, WARM_SETUP)

                @block.vector
                def _(dve):
                    link = chain(dve, dve_step)
                    dve.memset(warm[:], 1.0).then_inc(hi_ready, 1)
                    dve.wait_ge(tril_done, 1)
                    link(dve.tensor_copy(dist[:], dist_i[:]))
                    link(dve.tensor_scalar(causal[:], dist[:], 0.0, None, ALU.is_ge))

                    def make_mask(m, win, valid):
                        if win < S - 1:
                            link(dve.scalar_tensor_tensor(out=within[:], in0=dist[:], scalar=float(win),
                                                          in1=valid[:], op0=ALU.is_le, op1=ALU.mult))
                            valid = within
                        link(dve.tensor_scalar(m, valid[:], 1.0, -NEG, ALU.subtract, ALU.mult))

                    def make_dilated(g, win, dil):
                        if dil > 1:
                            link(dve.tensor_scalar(rem_i[:], dist_i[:], dil - 1, None, ALU.bitwise_and))
                            link(dve.tensor_copy(rem[:], rem_i[:]))
                            link(dve.scalar_tensor_tensor(out=rem[:], in0=rem[:], scalar=0.0, in1=causal[:],
                                                          op0=ALU.is_equal, op1=ALU.mult))
                        make_mask(mask_c[:, g, :], win, rem if dil > 1 else causal)

                    make_mask(mask_a[:], A_WIN - 1, causal)
                    dve.wait_ge(pool_done, 1)
                    dve.sem_inc(merged, 1)
                    for i in range(HALF):
                        f = float(np.float32(THETA) ** np.float32(-2.0 * i / ROT))
                        dve.memset(inv[:, i:i + 1], f)
                    dve.wait_ge(small_in, 16)
                    link(dve.tensor_copy(pos_f[:], pos_i[:]))
                    link(dve.tensor_tensor(ang[:], bcast(pos_f[:].unsqueeze(2), [P, TB, HALF]),
                                           bcast(inv[:].unsqueeze(1), [P, TB, HALF]), ALU.mult))
                    magic = 1.5 * 2.0 ** 23
                    link(dve.tensor_scalar(turns[:], ang[:], float(1 / (2 * np.pi)), magic, ALU.mult, ALU.add))
                    link(dve.tensor_scalar(turns[:], turns[:], magic, None, ALU.subtract))
                    c1 = 6.28125
                    c2 = float(np.round((2 * np.pi - c1) * 2 ** 20) / 2 ** 20)
                    c3 = float(2 * np.pi - c1 - c2)
                    for c in (c1, c2, c3):
                        link(dve.scalar_tensor_tensor(out=ang[:], in0=turns[:], scalar=-c, in1=ang[:],
                                                      op0=ALU.mult, op1=ALU.add))
                    link(dve.tensor_scalar(ang[:], ang[:], float(np.float32(3.1415925)),
                                           -float(np.float32(3.1415925)), ALU.min, ALU.max))
                    link(dve.tensor_scalar(folded[:], ang[:], -1.0, None, ALU.mult))
                    link(dve.tensor_tensor(folded[:], folded[:], ang[:], ALU.min))
                    link(dve.tensor_scalar(folded[:], folded[:], float(np.pi / 2), None, ALU.add))
                    dve.sem_inc(picked, 1)

                    make_dilated(0, *C_PAIRS[0])
                    norm_dve(dve, link)
                    make_dilated(1, *C_PAIRS[1])
                    make_dilated(2, *C_PAIRS[2])
                    dve.wait_ge(pool_done, 1)
                    dve.tensor_copy(ones[:], ones_f[:])
                    dve.tensor_copy(before[:], before_f[:])
                    dve.tensor_copy(slot_iota[:], iota_i[:])
                    dve.tensor_copy(idx_iota[:], iota8_i[:])

                @block.scalar
                def _(act):
                    act.wait_ge(hi_ready, 1)
                    load_sqrt_table(act)
                    norm_act(act, lambda q: act.wait_ge(ring_in[0], 16) if q == 0 else None,
                             lambda q: arena[:, q * BANK:(q + 1) * BANK])
                    act.wait_ge(picked, 1)
                    act.activation(sin[:], ang[:], ACT.Sin)
                    act.activation(cos[:], folded[:], ACT.Sin)
                    load_sqrt_table(act)
            end_of_stage()

        def layer_of(w, l):
            return w[ds(l, 1)].squeeze(0)

        AHEAD_SLOTS = range(8)

        def expert_weights(l, u, q, i):
            w = layer_of((w_expert_gate, w_expert_up)[i % 2] if i < 4 else w_expert_down, l)
            e = 2 * q + (i // 2 if i < 4 else i - 4)
            w = w[e + u * PER_GROUP] if isinstance(u, int) else w[ds(u * PER_GROUP + e, 1)].squeeze(0)
            return w.rearrange("(p k) f -> p (k f)", p=P)

        def trunk_stage(l):
            with ExitStack() as ctx:
                RING = RING_T
                Z_CONV = 68
                CHUNKS = 16
                AHEAD = 11
                BATCHES = 12
                TAIL = D_IN - CHUNKS * BANK
                BIAS_FIRST = 4 * BANK
                z = arena[:, 0:TB * D_IN].rearrange("p (t n) -> p t n", t=TB)
                ring = arena[:, TB * D_IN:].rearrange("p (s n) -> p s n", s=RING)
                whi = sb("whi", [P, 2, SLOT // 2], F32R, ctx)
                wlo = sb("wlo", [P, 2, SLOT // 2], F32R, ctx)
                ahi = sb("ahi", [P, 16, S], F32R, ctx)
                alo = sb("alo", [P, 16, S], F32R, ctx)
                wst = sb("wst", [P, B_GROUPS, P], F32, ctx)
                probs = sb("probs", [P, 2, 3, 384], F32, ctx)
                qkt = sb("qkt", [P, 3, BANK], F32, ctx)
                pts = sb("pts", [P, 3, 384], F32, ctx)
                tmp = sb("tmp", [P, 2, BANK], F32, ctx)
                k_twice = sb("k_twice", [P, TB, A_KV, 2 * HD], F32, ctx)
                sinks = sb("sinks", [P, A_HEADS], F32, ctx)
                bsp = sb("bsp", [P, B_GROUPS], F32, ctx)
                mx = sb("mx", [P, 2, TB, 4], F32, ctx)
                neg = sb("neg", [P, 2, TB, 4], F32, ctx)
                ex = sb("ex", [P, 2, TB, 4], F32, ctx)
                den = sb("den", [P, 2, TB, 4], F32, ctx)
                mxg = sb("mxg", [P, 2, TB], F32, ctx)
                stats = sb("stats", [P, TB, 2, 6], F32, ctx)
                mv = sb("mv", [P, TB, 2], F32, ctx)
                wsp = probs[:].rearrange("p a b c -> p (a b c)")[:, 0:B_GROUPS * P].rearrange(
                    "p (g s) -> p g s", g=B_GROUPS)
                ln_gb = work[:].rearrange("p t d -> p (t d)")[:, 0:2 * B_W].rearrange("p (n c) -> p n c", n=2)

                w_in_l = layer_of(w_in, l).rearrange("(p k) n -> p k n", k=KB)
                proj = ([(layer_of(w_proj_a, l), r) for r in range(4)]
                        + [(layer_of(w_proj_c, l), r) for r in range(1)]
                        + [(layer_of(w_proj_b, l), r) for r in range(3)]
                        + [(layer_of(w_out, l), r) for r in range(4)])

                def heads(b):
                    return 2 if b < 8 else 3

                def turned_before(b):
                    return 2 * b if b < 8 else 16 + 3 * (b - 8)

                def qk_banks(b):
                    return 1 if b < 8 else {8: 3, 10: 3}.get(b, 0)

                def t_first(kind, b):
                    n = sum(qk_banks(i) for i in range(b if kind == "qk" else min(b + 2, BATCHES)))
                    return n + turned_before(max(b - 1, 0) if kind == "qk" else b)

                ORDER = (0, 2, 1)

                def pairs_of(b):
                    return (b,) if b < 8 else {9: (8,), 11: (9,)}.get(b, ())

                with nc.Block() as block:
                    @block.sync
                    def _(sp):
                        def load_z_item(s, it):
                            src = w_in_l[:, 4 * (s % 2):4 * (s % 2) + 4, ds(it * 2 * BANK + (s // 2) * BANK, BANK)]
                            dst = ring[:, s, :].rearrange("p (k n) -> p k n", k=4)
                            sp.dma_start(dst, src).then_inc(ring_in[s], 16)

                        for s in range(4):
                            load_z_item(s, 0)
                        b_l = layer_of(b_in, l)
                        sp.dma_start(z[:, 0, 0:BIAS_FIRST], b_l[0:BIAS_FIRST].partition_broadcast(P)).then_inc(bias_in, 16)
                        sp.dma_start(wsp, layer_of(w_spatial, l).rearrange("g t s -> t g s")).then_inc(wsp_in, 16)
                        sp.dma_start(sinks[:], layer_of(attn_sinks, l).partition_broadcast(P)).then_inc(small_in, 16)
                        with nc.allow_non_contiguous_dma(reason="small parameters"):
                            sp.dma_start(bsp[:], layer_of(b_spatial, l).rearrange("g t -> t g")).then_inc(small_in, 16)
                        sp.wait_ge(turned, 4)
                        sp.dma_start(ln_gb[:, 0, :], layer_of(sgu_ln_g, l).partition_broadcast(P)).then_inc(ln_in, 16)
                        sp.dma_start(ln_gb[:, 1, :], layer_of(sgu_ln_b, l).partition_broadcast(P)).then_inc(ln_in, 16)
                        piece = (D_IN - BIAS_FIRST) // 4
                        for s in range(4):
                            sp.wait_ge(low_split, 2 * (s + 1))
                            load_z_item(s, 1)
                            cols = slice(BIAS_FIRST + s * piece, BIAS_FIRST + (s + 1) * piece)
                            sp.dma_start(z[:, 0, cols], b_l[cols].partition_broadcast(P)).then_inc(bias_rest_in, 16)
                        with sp.Fori(2, CHUNKS // 2) as it:
                            for s in range(4):
                                sp.wait_ge(low_split, it * 8 + 2 * (s + 1) - 8)
                                load_z_item(s, it)
                        def load_ahead(*slots):
                            for slot in slots:
                                q, i = slot // 6, slot % 6
                                src, dst = expert_weights(l, 0, q, i), experts_ring[:, slot, :]
                                sp.dma_start(dst, src).then_inc(ahead_in, 16)

                        for half in range(2):
                            sp.wait_ge(low_split, 2 * (4 * 7 + half + 1))
                            src = w_in_l[:, 4 * half:4 * half + 4, CHUNKS * BANK:D_IN]
                            dst = ring[:, half, 0:4 * TAIL].rearrange("p (k n) -> p k n", k=4)
                            sp.dma_start(dst, src).then_inc(ring_in[half], 16)
                        for i, (w, r) in enumerate(proj):
                            item = 34 + i
                            sp.wait_ge(low_split, 2 * (item - 4 + 1))
                            src = w[2 * r * P:2 * (r + 1) * P, :].rearrange("(k p) n -> p k n", p=P)
                            dst = ring[:, item % 4, :].rearrange("p (k n) -> p k n", k=2)
                            sp.dma_start(dst, src).then_inc(ring_in[item % 4], 16)
                            if item == 42:
                                sp.wait_ge(obt_ready, 3)
                                sp.wait_ge(gated, 4)
                                load_ahead(0, 1, 2)
                            if item == 43:
                                sp.wait_ge(gated, 8)
                                load_ahead(6, 4, 5)
                        sp.wait_ge(gated, 12)
                        load_ahead(3, 7)
                        with nc.allow_non_contiguous_dma(reason="small parameters"):
                            sp.dma_start(gain2[:], layer_of(norm2_g, l).rearrange("(p k) -> p k", k=KB)).then_inc(ahead_in, 16)
                            for w, first, n in ((w_router_group, 0, GROUPS), (w_router_expert, GROUPS, EXPERTS)):
                                sp.dma_start(wr[:, :, first:first + n],
                                             layer_of(w, l).rearrange("(p k) n -> p k n", k=KB)).then_inc(ahead_in, 16)
                        sp.wait_ge(ahead_in, 16 * (len(AHEAD_SLOTS) + 3))

                    @block.gpsimd
                    def _(pool):
                        link = chain(pool, pool_step)
                        pool.wait_ge(wsp_in, 16)
                        pool.affine_select(out=wsp, in_=wsp, compare_op=ALU.is_ge, fill=0.0, base=0,
                                           pattern=[[0, B_GROUPS], [-1, P]], channel_multiplier=1).then_inc(tril_done, 1)

                        def rope(first, n):
                            for tb in range(TB):
                                hd = z[:, tb, first:first + n * HD].rearrange("p (h c) -> p h c", c=HD)
                                t1, t2 = hd[:, :, 0:HALF], hd[:, :, HALF:ROT]
                                c = bcast(cos[:, tb, :].unsqueeze(1), [P, n, HALF])
                                s = bcast(sin[:, tb, :].unsqueeze(1), [P, n, HALF])
                                t1s = tmp[:, 0, 0:n * HALF].rearrange("p (h c) -> p h c", c=HALF)
                                t2s = tmp[:, 1, 0:n * HALF].rearrange("p (h c) -> p h c", c=HALF)
                                pool.tensor_tensor(t1s, t1, s, ALU.mult)
                                link(pool.tensor_tensor(t2s, t2, s, ALU.mult))
                                pool.tensor_tensor(t1, t1, c, ALU.mult)
                                link(pool.tensor_tensor(t2, t2, c, ALU.mult))
                                pool.tensor_tensor(t1, t1, t2s, ALU.subtract)
                                link(pool.tensor_tensor(t2, t2, t1s, ALU.add))

                        pool.wait_ge(z_evac, 2 * 3)
                        rope(ZQ, A_HEADS + A_KV)
                        k_heads = z[:, :, ZK:ZK + A_KV * HD].rearrange("p t (h c) -> p t h c", c=HD)
                        pool.tensor_copy(k_twice[:, :, :, 0:HD], k_heads)
                        pool.tensor_copy(k_twice[:, :, :, HD:2 * HD], k_heads).then_inc(roped, 1)
                        pool.wait_ge(z_evac, 2 * 9)
                        rope(CQ, 2 * 3 * C_PER)
                        pool.sem_inc(roped, 1)
                        v = z[:, :, ZN:ZN + B_W]
                        pool.wait_ge(vn_ready, 1)
                        pool.wait_ge(ln_in, 32)
                        link(pool.tensor_tensor(v, v, bcast(ln_gb[:, 0:1, :], [P, TB, B_W]), ALU.mult))
                        pool.tensor_tensor(v, v, bcast(ln_gb[:, 1:2, :], [P, TB, B_W]), ALU.add).then_inc(v_ready, 1)

                    def o_at(p, n):
                        at = ZQ + p * P if p < 8 else CQ + (p - 8) * P
                        return z[:, :, at:at + n * P]

                    def o_blocks(i):
                        return o_at(2 * i, 2).rearrange("p t (k c) -> p k t c", k=2)

                    def split_at(t, i):
                        kb = 2 * i if i < 4 else 14
                        return t[:, kb:kb + 2, :].rearrange("p k (t c) -> p k t c", t=TB)

                    def half_slot(j, w):
                        n = 2 * w
                        return ring[:, (j // 2) % RING, (j % 2) * n:(j % 2) * n + n]

                    @block.scalar
                    def _(act):
                        act.wait_ge(gain_in, 1)
                        for i in range(4):
                            act.wait_ge(turned, i + 1)
                            for k in (2 * i, 2 * i + 1):
                                act.activation(ahi[:, k, :], ps[:, i, (k % 2) * S:(k % 2) * S + S], ACT.Copy,
                                               scale=gain[:, k:k + 1]).then_inc(turned_hi, 1)
                        def high(jj, w, landed, used):
                            act.wait_ge(ring_in[(jj // 2) % RING], landed)
                            if used is not None:
                                act.wait_ge(conv_used, used)
                            act.copy(whi[:, jj % 2, 0:2 * w], half_slot(jj, w)).then_inc(hi_ready, 1)

                        for j in range(8):
                            high(j, BANK, 16, j - 1 if j >= 2 else None)
                        for i in range(3):
                            act.wait_ge(wst_ready, i + 1)
                            act.copy(wst[:, 4 * i:4 * i + 4, :].rearrange("p g t -> p (g t)"),
                                     ps[:, 4 + i, :]).then_inc(wst_evac, 1)
                        with act.Fori(1, AHEAD // 2) as it:
                            for j in range(8):
                                high(j, BANK, it * 16 + 16, it * 8 + (j - 1))

                        def high_at(j):
                            high(j, TAIL if 64 <= j < Z_CONV else BANK, 16 * (j // 8 + 1), j - 1)

                        high_at(40)
                        high_at(41)
                        act.wait_ge(z_evac, 2 * 6)
                        act.activation(z[:, :, ZN:ZN + B_W], z[:, :, ZN:ZN + B_W], ACT.Gelu_apprx_tanh).then_inc(gelu_done, 1)
                        high_at(42)
                        act.activation(z[:, :, ZU:ZU + B_W], z[:, :, ZU:ZU + B_W], ACT.Gelu_apprx_tanh).then_inc(gelu_done, 1)
                        high_at(43)
                        act.wait_ge(lnv_ready, 1)
                        act.activation(mv[:, :, 1], mv[:, :, 1], ACT.Sqrt).then_inc(ln_root, 1)
                        high_at(44)
                        high_at(45)

                        def qk_out(b):
                            for i in range(qk_banks(b)):
                                t = t_first("qk", b) + i
                                act.wait_ge(t_ready, t + 1)
                                to, w = (i, BANK) if b >= 8 else (b % 2, S if b % 2 else BANK)
                                act.copy(qkt[:, to, 0:w], ps[:, 3 + t % 2, 0:w]).then_inc(t_evac, 1)

                        def exps(b):
                            act.wait_ge(neg_ready, b + 1)
                            i = b % 2
                            for n in range(heads(b)):
                                for tb, lo, hi in ((0, 0, P), (1, P, 3 * P)):
                                    act.activation(probs[:, i, n, lo:hi], probs[:, i, n, lo:hi], ACT.Exp,
                                                   bias=neg[:, i, tb, n:n + 1], accum_out=den[:, i, tb, n:n + 1])
                            act.activation(ex[:, i, :, 0:heads(b)], ex[:, i, :, 0:heads(b)],
                                           ACT.Exp).then_inc(exp_ready, 1)

                        def pv_out(b):
                            for i in range(heads(b)):
                                t, u = t_first("pv", b) + i, turned_before(b) + i
                                act.wait_ge(t_ready, t + 1)
                                if u >= 3:
                                    act.wait_ge(pv_mm, u - 2)
                                act.copy(pts[:, u % 3, :], ps[:, 3 + t % 2, 0:384]).then_inc(t_evac, 1)

                        def o_out(b):
                            for p in pairs_of(b):
                                act.wait_ge(o_ready, p + 1)
                                act.copy(o_at(p, 1), ps[:, 5, 0:S].rearrange("p (t c) -> p t c", t=TB)).then_inc(o_evac, 1)

                        qk_out(0)
                        qk_out(1)
                        exps(0)
                        for b in range(BATCHES):
                            high_at(46 + 2 * b)
                            pv_out(b)
                            if b + 1 < BATCHES:
                                exps(b + 1)
                            o_out(b)
                            if b + 2 < BATCHES:
                                qk_out(b + 2)
                            high_at(47 + 2 * b)

                        def sigmoid(branch):
                            g = z[:, :, ZG + branch * D:ZG + (branch + 1) * D]
                            act.activation(g, g, ACT.Sigmoid).then_inc(gates_ready, 1)

                        act.wait_ge(conv_used, Z_CONV)
                        act.wait_ge(o_evac, 10)
                        for i in range(5):
                            act.copy(split_at(ahi, i), o_blocks(i)).then_inc(o_hi, 1)
                        act.wait_ge(z_evac, 2 * (CHUNKS + 1))
                        for j in range(70, 78):
                            if j % 2 == 1 and j < 77:
                                sigmoid(ORDER[(j - 71) // 2])
                            high_at(j)
                            if j == 74:
                                for i in range(3):
                                    act.wait_ge(obt_ready, i + 1)
                                    act.copy(ahi[:, 8 + 2 * i:10 + 2 * i, :].rearrange("p k t -> p (k t)"),
                                             ps[:, i, :]).then_inc(obt_hi, 1)
                        for j in range(78, 86):
                            high_at(j)
                        for i in range(4):
                            act.wait_ge(mt_ready, i + 1)
                            act.copy(ahi[:, 2 * i:2 * i + 2, :].rearrange("p k t -> p (k t)"),
                                     ps[:, 4 + i, :]).then_inc(mt_hi, 1)
                        for j in range(86, 92):
                            high_at(j)
                        load_sqrt_table(act)
                        junk = probs[:].rearrange("p a b c -> p (a b c)")
                        norm_act(act, lambda q: act.wait_ge(x_quarter, q + 1),
                                 lambda q: junk[:, q * BANK:(q + 1) * BANK])

                    @block.vector
                    def _(dve):
                        link = chain(dve, dve_step)
                        dve.tensor_copy(gain[:], gains1[:, ds(l, 1), :].squeeze(1)).then_inc(gain_in, 1)
                        dve.wait_ge(gain_in, 1)
                        for k in range(KB):
                            dve.wait_ge(turned_hi, k // 2 * 2 + 2)
                            dve.scalar_tensor_tensor(out=alo[:, k, :], in0=ps[:, k // 2, (k % 2) * S:(k % 2) * S + S],
                                                     scalar=gain[:, k:k + 1], in1=ahi[:, k, :].bitcast(F32),
                                                     op0=ALU.mult, op1=ALU.subtract).then_inc(turned_lo, 1)

                        def low(jj, w, ready):
                            dve.wait_ge(hi_ready, ready)
                            for cols, done in ((slice(0, w), low_first), (slice(w, 2 * w), low_split)):
                                dve.tensor_tensor(wlo[:, jj % 2, cols], half_slot(jj, w)[:, cols],
                                                  whi[:, jj % 2, cols].bitcast(F32), ALU.subtract).then_inc(done, 1)

                        def z_out(bank, c, w, done):
                            dve.wait_ge(z_ready, done)
                            cols = ds(c * BANK, w)
                            dve.tensor_tensor(z[:, 1, cols], ps[:, bank + 1, 0:w], z[:, 0, cols], ALU.add).then_inc(z_evac, 1)
                            dve.tensor_tensor(z[:, 0, cols], ps[:, bank, 0:w], z[:, 0, cols], ALU.add).then_inc(z_evac, 1)

                        for j in range(8):
                            low(j, BANK, j + 1)
                            if j == 5:
                                dve.wait_ge(bias_in, 16)
                                z_out(0, 0, BANK, 1)
                        with dve.Fori(1, AHEAD // 2) as it:
                            for j in range(8):
                                low(j, BANK, it * 8 + (j + 1))
                                if j == 1:
                                    z_out(2, it * 2 - 1, BANK, it * 2)
                                if j == 5:
                                    dve.wait_ge(bias_rest_in, 16 * 4)
                                    z_out(0, it * 2, BANK, it * 2 + 1)

                        def low_at(j):
                            low(j, TAIL if 64 <= j < Z_CONV else BANK, j + 1)

                        low_at(40)
                        low_at(41)
                        z_out(2, AHEAD - 2, BANK, AHEAD - 1)
                        low_at(42)
                        low_at(43)
                        dve.wait_ge(gelu_done, 1)
                        for tb in range(TB):
                            for h in range(2):
                                last = dve.bn_stats(stats[:, tb, h, :], z[:, tb, ZN + 384 * h:ZN + 384 * (h + 1)])
                        link(last)
                        for tb in range(TB):
                            last = dve.bn_aggr(mv[:, tb, :], stats[:, tb, :, :])
                        link(last)
                        link(dve.tensor_scalar(mv[:, :, 1], mv[:, :, 1], EPS, None, ALU.add))
                        dve.reciprocal(mv[:, :, 1], mv[:, :, 1]).then_inc(lnv_ready, 1)
                        z_out(0, AHEAD - 1, BANK, AHEAD)
                        low_at(44)
                        low_at(45)

                        def ln_apply():
                            dve.wait_ge(ln_root, 1)
                            for tb in range(TB):
                                v = z[:, tb, ZN:ZN + B_W]
                                last = dve.tensor_scalar(v, v, mv[:, tb, 0:1], mv[:, tb, 1:2], ALU.subtract, ALU.mult)
                            last.then_inc(vn_ready, 1)

                        def softmax_in(b):
                            i, n = b % 2, heads(b)
                            dve.wait_ge(s_ready, turned_before(b) + n)
                            if b >= 2:
                                dve.wait_ge(pv_turned, b - 1)
                            mask = bcast(mask_a[:].unsqueeze(1), [P, n, 384]) if b < 8 else mask_c[:]
                            ins = dve.scalar_tensor_tensor(out=probs[:, i, 0:n, :], in0=ps[:, 0:n, 0:384],
                                                           scalar=SCALE, in1=mask, op0=ALU.mult, op1=ALU.add)
                            ins.then_inc(s_free, 1)
                            dve.wait_ge(s_free, b + 1)
                            dve.tensor_reduce(mx[:, i, 0, 0:n], probs[:, i, 0:n, 0:P], AX, ALU.max)
                            link(dve.tensor_reduce(mx[:, i, 1, 0:n], probs[:, i, 0:n, P:3 * P], AX, ALU.max))
                            m = mx[:, i, :, 0:n]
                            if b < 8:
                                sk = bcast(sinks[:, n * b:n * b + n].unsqueeze(1), [P, TB, n])
                                link(dve.tensor_tensor(m, m, sk, ALU.max))
                                dve.tensor_tensor(ex[:, i, :, 0:n], sk, m, ALU.subtract)
                            else:
                                link(dve.tensor_reduce(mxg[:, i, :], m, AX, ALU.max))
                                dve.tensor_tensor(ex[:, i, :, 0:n], m, bcast(mxg[:, i, :].unsqueeze(2), [P, TB, n]),
                                                  ALU.subtract)
                            dve.tensor_scalar(neg[:, i, :, 0:n], m, -1.0, None, ALU.mult).then_inc(neg_ready, 1)

                        def softmax_out(b):
                            i, n = b % 2, heads(b)
                            dve.wait_ge(exp_ready, b + 1)
                            d, e = den[:, i, :, 0:n], ex[:, i, :, 0:n]
                            if b < 8:
                                link(dve.tensor_tensor(d, d, e, ALU.add))
                                link(dve.reciprocal(d, d))
                            else:
                                link(dve.tensor_tensor(d, d, e, ALU.mult))
                                link(dve.tensor_reduce(mxg[:, i, :], d, AX, ALU.add))
                                link(dve.reciprocal(mxg[:, i, :], mxg[:, i, :]))
                                link(dve.tensor_tensor(d, e, bcast(mxg[:, i, :].unsqueeze(2), [P, TB, n]), ALU.mult))
                            for tb, lo, hi in ((0, 0, P), (1, P, 3 * P)):
                                p = probs[:, i, 0:n, lo:hi]
                                last = dve.tensor_tensor(p, p, bcast(den[:, i, tb, 0:n].unsqueeze(2), [P, n, hi - lo]),
                                                         ALU.mult)
                            last.then_inc(p_ready, 1)

                        dve.wait_ge(small_in, 32)
                        softmax_in(0)
                        softmax_out(0)
                        for b in range(BATCHES):
                            if b + 1 < BATCHES:
                                softmax_in(b + 1)
                            low_at(46 + 2 * b)
                            if b == 0:
                                ln_apply()
                            if b % 2:
                                c = AHEAD + b // 2
                                z_out(6, c, TAIL if c == CHUNKS else BANK, c + 1)
                            if b + 1 < BATCHES:
                                softmax_out(b + 1)
                            low_at(47 + 2 * b)

                        for i in range(5):
                            dve.wait_ge(o_hi, i + 1)
                            dve.tensor_tensor(split_at(alo, i), o_blocks(i), split_at(ahi, i).bitcast(F32),
                                              ALU.subtract).then_inc(o_lo, 1)
                        dve.wait_ge(sv_ready, 1)
                        for g in range(B_GROUPS):
                            u = z[:, :, ZU + HD * g:ZU + HD * (g + 1)]
                            sv = ps[:, g // 4, (g % 4) * P:(g % 4 + 1) * P].rearrange("p (t c) -> p t c", t=TB)
                            last = dve.scalar_tensor_tensor(out=u, in0=sv, scalar=bsp[:, g:g + 1], in1=u,
                                                            op0=ALU.add, op1=ALU.mult)
                        last.then_inc(ob_ready, 1)
                        def gate(n, q):
                            branch = ORDER[n]
                            if q == 0:
                                dve.wait_ge(gates_ready, n + 1)
                            dve.wait_ge(quarter_ready, 4 * n + q + 1)
                            tb, nh = q % 2, q // 2
                            g = z[:, tb, ZG + branch * D + nh * BANK:ZG + branch * D + (nh + 1) * BANK]
                            to = work[:, tb, nh * BANK:(nh + 1) * BANK]
                            pr = ps[:, (4, 4, 0)[n] + q, :]
                            if n == 0:
                                dve.tensor_tensor(to, pr, g, ALU.mult).then_inc(gated, 1)
                                return
                            dve.tensor_tensor(tmp[:, q % 2, :], pr, g, ALU.mult).then_inc(gated, 1)
                            dve.wait_ge(gated, n * 4 + q + 1)
                            last = dve.tensor_tensor(to, to, tmp[:, q % 2, :], ALU.add)
                            if n == 2:
                                last.then_inc(merged, 1)

                        def merged_low(i):
                            dve.wait_ge(mt_hi, i + 1)
                            dve.tensor_tensor(alo[:, 2 * i:2 * i + 2, :].rearrange("p k t -> p (k t)"), ps[:, 4 + i, :],
                                              ahi[:, 2 * i:2 * i + 2, :].rearrange("p k t -> p (k t)").bitcast(F32),
                                              ALU.subtract).then_inc(mt_lo, 1)

                        for j in range(70, 77):
                            low_at(j)
                            if j == 74:
                                for i in range(3):
                                    dve.wait_ge(obt_hi, i + 1)
                                    dve.tensor_tensor(
                                        alo[:, 8 + 2 * i:10 + 2 * i, :].rearrange("p k t -> p (k t)"), ps[:, i, :],
                                        ahi[:, 8 + 2 * i:10 + 2 * i, :].rearrange("p k t -> p (k t)").bitcast(F32),
                                        ALU.subtract).then_inc(obt_lo, 1)
                        for q in range(4):
                            gate(0, q)
                        low_at(77)
                        for j in range(78, 84):
                            low_at(j)
                            if j < 82:
                                gate(1, j - 78)
                        gate(2, 0)
                        gate(2, 1)
                        low_at(84)
                        merged_low(0)
                        gate(2, 2)
                        gate(2, 3)
                        low_at(85)
                        for i in range(1, 4):
                            merged_low(i)
                        for j in range(86, 92):
                            low(j, BANK, j + 1)
                        for q in range(4):
                            dve.wait_ge(quarter_ready, 12 + q + 1)
                            to = quarter(xs, q)
                            dve.tensor_tensor(to, ps[:, q, :], to, ALU.add).then_inc(x_quarter, 1)
                        norm_dve(dve, link)

                    @block.tensor
                    def _(pe):
                        for k in range(KB):
                            for tb in range(TB):
                                mm = pe.transpose(ps[:, k // 2, (k % 2) * S + tb * P:(k % 2) * S + (tb + 1) * P],
                                                  work[:, tb, k * P:(k + 1) * P], ident[:])
                            if k % 2:
                                mm.then_inc(turned, 1)
                        def three_passes(o, kb, tb, rhs_hi, rhs_lo, first, last):
                            hi = ahi[:, kb, tb * P:(tb + 1) * P]
                            lo = alo[:, kb, tb * P:(tb + 1) * P]
                            pe.matmul(o, hi, rhs_hi, start=first, stop=False)
                            pe.matmul(o, hi, rhs_lo, start=False, stop=False)
                            return pe.matmul(o, lo, rhs_hi, start=False, stop=last)

                        def z_conv(jj, bank, w, ready, between=None):
                            for kk in range(2):
                                if kk and between:
                                    between()
                                pe.wait_ge(low_split if kk else low_first, ready)
                                kb = 2 * (jj % 4) + kk
                                for tb in range(TB):
                                    mm = three_passes(ps[:, bank + tb, 0:w], kb, tb, whi[:, jj % 2, kk * w:(kk + 1) * w],
                                                      wlo[:, jj % 2, kk * w:(kk + 1) * w], kb == 0, kb == KB - 1)
                            mm.then_inc(conv_used, 1)

                        def turn_w_spatial():
                            pe.wait_ge(tril_done, 1)
                            for g in range(B_GROUPS):
                                mm = pe.transpose(ps[:, 4 + g // 4, (g % 4) * P:(g % 4 + 1) * P], wsp[:, g, :], ident[:])
                                if g % 4 == 3:
                                    mm.then_inc(wst_ready, 1)

                        for j in range(8):
                            if j < 4:
                                pe.wait_ge(turned_lo, 2 * (j + 1))
                            if j == 6:
                                turn_w_spatial()
                            z_conv(j, 2 * (j // 4), BANK, j + 1)
                            if j % 4 == 3:
                                pe.wait_ge(conv_used, j + 1)
                                pe.sem_inc(z_ready, 1)
                        with pe.Fori(1, AHEAD // 2) as it:
                            for j in range(8):
                                if j % 4 == 0:
                                    pe.wait_ge(z_evac, it * 4 + (-2 if j == 0 else 0))
                                z_conv(j, 2 * (j // 4), BANK, it * 8 + (j + 1))
                                if j % 4 == 3:
                                    pe.wait_ge(conv_used, it * 8 + (j + 1))
                                    pe.sem_inc(z_ready, 1)
                        pe.wait_ge(z_evac, 2 * (AHEAD - 2))
                        for j in range(4 * (AHEAD - 1), 4 * AHEAD):
                            z_conv(j, 0, BANK, j + 1)
                        pe.wait_ge(conv_used, 4 * AHEAD)
                        pe.sem_inc(z_ready, 1)

                        pe.wait_ge(wst_evac, 3)

                        def gates_conv(j, between=None):
                            if j % 4 == 0 and j > 4 * AHEAD:
                                pe.wait_ge(z_evac, 2 * (j // 4))
                            z_conv(j, 6, TAIL if j >= 4 * CHUNKS else BANK, j + 1, between)
                            if j % 4 == 3:
                                pe.wait_ge(conv_used, j + 1)
                                pe.sem_inc(z_ready, 1)

                        def bank_for(t):
                            if t >= 2:
                                pe.wait_ge(t_evac, t - 1)
                            return 3 + t % 2

                        def qk(b):
                            pe.wait_ge(roped, 1 if b < 8 else 2)
                            for i in range(qk_banks(b)):
                                bank = bank_for(t_first("qk", b) + i)
                                for tb in range(TB):
                                    if b < 8:
                                        srcs = [z[:, tb, ZQ + 2 * b * HD:ZQ + (2 * b + 2) * HD]]
                                        if b % 2 == 0:
                                            srcs.append(k_twice[:, tb, b // 2, :])
                                    else:
                                        h = C_PER * i + b - 8
                                        srcs = [z[:, tb, at + h * HD:at + (h + 2) * HD] for at in (CQ, CK)]
                                    for n_src, src in enumerate(srcs):
                                        mm = pe.transpose(ps[:, bank, n_src * S + tb * P:n_src * S + (tb + 1) * P],
                                                          src, ident[:])
                                mm.then_inc(t_ready, 1)

                        def scores(b):
                            src = b if b < 8 else 8 + 2 * ((b - 8) // 2)
                            pe.wait_ge(t_evac, t_first("qk", src) + qk_banks(src))
                            if b >= 1:
                                pe.wait_ge(s_free, b)
                            for tb in range(TB):
                                for i in range(heads(b)):
                                    r = HD * (i if b < 8 else b % 2)
                                    rows = slice(r, r + HD)
                                    q = qkt[rows, b % 2, 0:S] if b < 8 else qkt[rows, i, 0:S]
                                    k = qkt[rows, 0 if b < 8 else i, S:2 * S]
                                    mm = pe.matmul(ps[:, i, tb * P:tb * P + (tb + 1) * P], q[:, tb * P:(tb + 1) * P],
                                                   k[:, 0:(tb + 1) * P], start=True, stop=True)
                                    if tb:
                                        mm.then_inc(s_ready, 1)

                        def pv(b):
                            n, u0 = heads(b), turned_before(b)
                            pe.wait_ge(p_ready, b + 1)

                            def turn(i):
                                bank = bank_for(t_first("pv", b) + i)
                                for c in range(3):
                                    mm = pe.transpose(ps[:, bank, c * P:(c + 1) * P],
                                                      probs[:, b % 2, i, c * P:(c + 1) * P], ident[:])
                                mm.then_inc(t_ready, 1)

                            def product_pair():
                                pe.wait_ge(t_evac, t_first("pv", b) + 2)
                                if b >= 1:
                                    pe.wait_ge(o_evac, b)
                                v = z[:, :, ZV + b // 2 * HD:ZV + (b // 2 + 1) * HD]
                                for tb in range(TB):
                                    for i in range(2):
                                        o = ps[HD * i:HD * (i + 1), 5, tb * P:S]
                                        pt = pts[:, (u0 + i) % 3, tb * S:tb * P + S]
                                        mm = pe.matmul(o, v[:, tb, :], pt, start=tb == 0, stop=tb == 1,
                                                       skip_group_check=True)
                                        if tb:
                                            mm.then_inc(pv_mm, 1)

                            def product(i):
                                pe.wait_ge(t_evac, t_first("pv", b) + i + 1)
                                p, r, at = 8 + (b - 8) // 2, HD * (b % 2), CV + (C_PER * i + b - 8) * HD
                                g0, g1 = i == 0, i == n - 1
                                pe.wait_ge(o_evac, p)
                                o = ps[r:r + HD, 5, 0:S]
                                pt = pts[:, (u0 + i) % 3, :]
                                pe.matmul(o, z[:, 0, at:at + HD], pt[:, 0:S], start=g0, stop=False)
                                mm = pe.matmul(o[:, P:S], z[:, 1, at:at + HD], pt[:, S:3 * P], start=False, stop=g1)
                                mm.then_inc(pv_mm, 1)

                            turn(0)
                            turn(1)
                            gates_conv(45 + 2 * b, (lambda: turn(2)) if n == 3 else None)
                            if b < 8:
                                product_pair()
                            for i in range(n if b >= 8 else 0):
                                product(i)
                            pe.wait_ge(pv_mm, u0 + n)
                            pe.sem_inc(pv_turned, 1)
                            for p in pairs_of(b):
                                pe.sem_inc(o_ready, 1)

                        qk(0)
                        pe.wait_ge(z_evac, 2 * AHEAD)
                        scores(0)
                        qk(1)
                        for b in range(BATCHES):
                            gates_conv(44 + 2 * b)
                            if b + 1 < BATCHES:
                                scores(b + 1)
                            pv(b)
                            if b + 2 < BATCHES:
                                qk(b + 2)

                        def base_quarters(j):
                            return 4 * sum(j >= j0 for j0 in (76, 78, 84))

                        pe.wait_ge(s_free, BATCHES)
                        pe.wait_ge(v_ready, 1)
                        for g in range(B_GROUPS):
                            mm = pe.matmul(ps[:, g // 4, (g % 4) * P:(g % 4 + 1) * P], wst[:, g, :],
                                           z[:, :, ZN + HD * g:ZN + HD * (g + 1)], start=True, stop=True)
                        mm.then_inc(sv_ready, 1)

                        def project(j0, kb0, n, base, reads=None, between={}):
                            for i in range(n):
                                j = j0 + i
                                if j0 == 68 and i % 2 == 0:
                                    pe.wait_ge(o_lo, i // 2 + 1)
                                if j0 == 84 and i % 2 == 0:
                                    pe.wait_ge(mt_lo, i // 2 + 1)
                                if i in between:
                                    between[i]()
                                for q in range(4):
                                    if q % 2 == 0:
                                        pe.wait_ge(low_split if q else low_first, j + 1)
                                    tb, nh = q % 2, q // 2
                                    if i == 0 and reads is not None:
                                        pe.wait_ge(gated, reads + q + 1)
                                    mm = three_passes(ps[:, base + q, :], kb0 + i, tb,
                                                      whi[:, j % 2, nh * BANK:(nh + 1) * BANK],
                                                      wlo[:, j % 2, nh * BANK:(nh + 1) * BANK], i == 0, i == n - 1)
                                    if i == n - 1:
                                        mm.then_inc(quarter_ready, 1)
                                if i < n - 1:
                                    mm.then_inc(conv_used, 1)
                            pe.wait_ge(quarter_ready, base_quarters(j) + 4)
                            pe.sem_inc(conv_used, 1)

                        pe.wait_ge(o_evac, 10)
                        pe.wait_ge(z_evac, 2 * (CHUNKS + 1))

                        def turn_b():
                            pe.wait_ge(ob_ready, 1)
                            for k in range(6):
                                for tb in range(TB):
                                    mm = pe.transpose(ps[:, k // 2, (k % 2) * S + tb * P:(k % 2) * S + (tb + 1) * P],
                                                      z[:, tb, ZU + k * P:ZU + (k + 1) * P], ident[:])
                                if k % 2:
                                    mm.then_inc(obt_ready, 1)

                        def turn_merged(half):
                            pe.wait_ge(merged, 2 * (half + 1))
                            for k in range(4 * half, 4 * half + 4):
                                for tb in range(TB):
                                    at = (k % 2) * S + tb * P
                                    mm = pe.transpose(ps[:, 4 + k // 2, at:at + P], work[:, tb, k * P:(k + 1) * P],
                                                      ident[:])
                                if k % 2:
                                    mm.then_inc(mt_ready, 1)

                        project(68, 0, 8, 4, between={4: turn_b})
                        pe.wait_ge(o_lo, 5)
                        project(76, 14, 2, 4, reads=0)
                        pe.wait_ge(obt_lo, 3)
                        project(78, 8, 6, 0)
                        turn_merged(0)
                        project(84, 0, 8, 0, reads=8, between={1: lambda: turn_merged(1)})
                        keep_clock(pe, WARM_TRUNK)
            end_of_stage()

        def expert_stage(l):
            with ExitStack() as ctx:
                xnh = sb("xnh", [P, TB, D], F32R, ctx)
                xnl = sb("xnl", [P, TB, D], F32R, ctx)
                lgt = sb("lgt", [WR, S], F32, ctx)
                lg = sb("lg", [P, TB, 8], F32, ctx)
                top = sb("top", [P, TB, 8], F32, ctx)
                top_i = sb("top_i", [P, TB, 8], U32, ctx)
                gid = sb("gid", [P, TB, 8], F32, ctx)
                gmask = sb("gmask", [P, TB, GROUPS], F32, ctx)
                les = sb("les", [P, TB, 8], F32, ctx)
                etop = sb("etop", [P, TB, 8], F32, ctx)
                eid = sb("eid", [P, TB, 8], F32, ctx)
                lse = sb("lse", [P, TB, 8], F32, ctx)
                pg = sb("pg", [P, TB], F32, ctx)
                w12 = sb("w12", [P, TB, 2], F32, ctx)
                pick = sb("pick", [P, TB, 2, 8], F32, ctx)
                either = sb("either", [P, TB, 8], F32, ctx)
                weighted = sb("weighted", [P, TB, 2, 8], F32, ctx)
                sel = sb("sel", [P, TB, EXPERTS], F32R, ctx)
                big = sb("big", [P, TB, EXPERTS], F32, ctx)
                cnt = sb("cnt", [P, 4], F32, ctx)

                RING = RING_E
                ring = experts_ring
                onehot = sb("onehot", [P, TB, UNIT], F32R, ctx)
                xsel = sb("xsel", [P, KB, UNIT], F32, ctx)
                h2t = xsel[:].rearrange("p k s -> p (k s)")[:, 0:KB * S].rearrange("p (k s) -> p k s", k=KB)
                st = sb("st", [P, PAIRS, S], F32R, ctx)
                wslot = sb("wslot", [P, PAIRS], F32, ctx)
                sg = sb("sg", [P, 2, F], F32, ctx)
                a_sb = sb("a_sb", [P, 2, F], F32, ctx)
                at_sb = sb("at_sb", [P, 2, 2, P], F32, ctx)
                yh = sb("yh", [P, PAIRS, D], F32R, ctx)
                yl = sb("yl", [P, PAIRS, D], F32R, ctx)

                TAIL_BANKS = (4, 5, 0, 1)
                FIRST = UNIT // 2

                def units(eng, main, turn, tail):
                    main(0)
                    turn(0)
                    with eng.Fori(1, GROUPS - 1) as u:
                        main(u)
                        turn(u)
                    main(GROUPS - 1)
                    tail(GROUPS - 1)

                def after(eng, s, u, per_unit, count):
                    if isinstance(u, int):
                        if per_unit * u + count > 0:
                            eng.wait_ge(s, per_unit * u + count)
                    else:
                        eng.wait_ge(s, u * per_unit + count)

                def route_act(act):
                    for i in (0, 2):
                        act.wait_ge(turned, i + 1)
                        for k in (2 * i, 2 * i + 1):
                            last = act.activation(h2t[:, k, :], ps[:, i, (k % 2) * S:(k % 2) * S + S], ACT.Copy,
                                                  scale=gain2[:, k:k + 1])
                    last.then_inc(h2t_ready, 1)
                    act.copy(xnh[:], work[:]).then_inc(hi_ready, 1)
                    act.wait_ge(lgt_ready, 1)
                    act.copy(lgt[:], ps[0:WR, 4, 0:S]).then_inc(lgt_evac, 1)
                    act.wait_ge(router_in, 1)
                    act.activation(lse[:], lse[:], ACT.Exp).then_inc(router_exp, 1)

                def route_pe(pe):
                    for k in range(KB):
                        for tb in range(TB):
                            mm = pe.transpose(ps[:, k // 2, (k % 2) * S + tb * P:(k % 2) * S + (tb + 1) * P],
                                              work[:, tb, k * P:(k + 1) * P], ident[:])
                        if k % 2:
                            mm.then_inc(turned, 1)
                    pe.wait_ge(h2t_ready, 2)
                    for k in range(KB):
                        mm = pe.matmul(ps[0:WR, 4, 0:S], wr[:, k, :], h2t[:, k, :], start=(k == 0), stop=(k == KB - 1))
                    mm.then_inc(lgt_ready, 1)
                    pe.wait_ge(lgt_evac, 1)
                    for tb in range(TB):
                        mm = pe.transpose(ps[:, 5, WR * tb:WR * tb + WR], lgt[:, tb * P:(tb + 1) * P], ident[0:WR, 0:WR])
                    mm.then_inc(logits_ready, 1)
                    keep_clock(pe, WARM_ROUTE)
                    pe.wait_ge(picked, 1)
                    pe.matmul(ps[:, 6, 0:EXPERTS], before[:], sel[:, 0, :], start=True, stop=True)
                    pe.matmul(ps[:, 6, 64:64 + EXPERTS], before[:], sel[:, 1, :], start=True, stop=False)
                    pe.matmul(ps[:, 6, 64:64 + EXPERTS], ones[:], sel[:, 0, :], start=False,
                              stop=True).then_inc(ranks_ready, 1)
                    pe.matmul(ps[:, 7, 0:EXPERTS], ones[:], sel[:, 0, :], start=True, stop=False)
                    pe.matmul(ps[:, 7, 0:EXPERTS], ones[:], sel[:, 1, :], start=False,
                              stop=True).then_inc(totals_ready, 1)
                    pe.wait_ge(low_split, 1)

                def route_pool(pool):
                    pool.wait_ge(hi_ready, 1)
                    pool.tensor_tensor(xnl[:], work[:], xnh[:].bitcast(F32), ALU.subtract).then_inc(low_split, 1)

                def by_group(t):
                    return t[:].rearrange("p t (g e) -> p t g e", g=GROUPS)

                def over_experts(t):
                    return bcast(t.unsqueeze(3), [P, TB, GROUPS, PER_GROUP])

                def over_groups(t):
                    return bcast(t.unsqueeze(2), [P, TB, GROUPS, PER_GROUP])

                def route_dve(dve, link):
                    link(dve.memset(lg[:], -3e38))
                    for i in (1, 3):
                        dve.wait_ge(turned, i + 1)
                        for k in (2 * i, 2 * i + 1):
                            last = dve.tensor_scalar(h2t[:, k, :], ps[:, i, (k % 2) * S:(k % 2) * S + S],
                                                     gain2[:, k:k + 1], None, ALU.mult)
                    last.then_inc(h2t_ready, 1)
                    dve.wait_ge(logits_ready, 1)
                    logits = ps[:, 5, 0:TB * WR].rearrange("p (t n) -> p t n", t=TB)
                    link(dve.tensor_copy(lg[:, :, 0:GROUPS], logits[:, :, 0:GROUPS]))
                    dve.max(top[:, 0, :], lg[:, 0, :])
                    link(dve.max(top[:, 1, :], lg[:, 1, :]))
                    dve.max_index(top_i[:, 0, :], top[:, 0, :], lg[:, 0, :])
                    link(dve.max_index(top_i[:, 1, :], top[:, 1, :], lg[:, 1, :]))
                    link(dve.tensor_copy(gid[:], top_i[:]))
                    link(dve.tensor_tensor(gmask[:], bcast(idx_iota[:, 0:GROUPS].unsqueeze(1), [P, TB, GROUPS]),
                                           bcast(gid[:, :, 0:1], [P, TB, GROUPS]), ALU.is_equal))
                    link(dve.tensor_tensor(
                        by_group(big), logits[:, :, GROUPS:GROUPS + EXPERTS].rearrange("p t (g e) -> p t g e", g=GROUPS),
                        over_experts(gmask[:]), ALU.mult))
                    link(dve.tensor_reduce(les[:], big[:].rearrange("p t (g e) -> p t e g", g=GROUPS), AX, ALU.add))
                    dve.max(etop[:, 0, :], les[:, 0, :])
                    link(dve.max(etop[:, 1, :], les[:, 1, :]))
                    dve.max_index(top_i[:, 0, :], etop[:, 0, :], les[:, 0, :])
                    link(dve.max_index(top_i[:, 1, :], etop[:, 1, :], les[:, 1, :]))
                    link(dve.tensor_copy(eid[:], top_i[:]))
                    link(dve.tensor_tensor(pick[:], bcast(idx_iota[:].unsqueeze(1).unsqueeze(1), [P, TB, 2, 8]),
                                           bcast(eid[:, :, 0:2].unsqueeze(3), [P, TB, 2, 8]), ALU.is_equal))
                    link(dve.tensor_tensor(either[:], pick[:, :, 0, :], pick[:, :, 1, :], ALU.add))
                    dve.tensor_tensor(by_group(sel), over_groups(either[:]), over_experts(gmask[:]),
                                      ALU.mult).then_inc(picked, 1)
                    dve.tensor_tensor(lse[:, :, 0:GROUPS], lg[:, :, 0:GROUPS],
                                      bcast(top[:, :, 0:1], [P, TB, GROUPS]), ALU.subtract)
                    dve.tensor_tensor(lse[:, :, GROUPS:], etop[:, :, 0:4], bcast(etop[:, :, 0:1], [P, TB, 4]),
                                      ALU.subtract).then_inc(router_in, 1)
                    dve.wait_ge(ranks_ready, 1)
                    ranks = ps[:, 6, 0:2 * 64].rearrange("p (t n) -> p t n", t=TB)[:, :, 0:EXPERTS]
                    link(dve.scalar_tensor_tensor(out=rk[:], in0=ranks, scalar=1.0, in1=sel[:].bitcast(F32),
                                                  op0=ALU.add, op1=ALU.mult))
                    link(dve.tensor_scalar(rk[:], rk[:], 1.0, None, ALU.subtract))

                def combine_weights(dve, link):
                    dve.wait_ge(router_exp, 1)
                    link(dve.tensor_reduce(pg[:], lse[:, :, 0:GROUPS], AX, ALU.add))
                    link(dve.scalar_tensor_tensor(out=pg[:], in0=lse[:, :, GROUPS + 1], scalar=1.0, in1=pg[:],
                                                  op0=ALU.add, op1=ALU.mult))
                    link(dve.reciprocal(w12[:, :, 0], pg[:]))
                    link(dve.tensor_tensor(w12[:, :, 1], w12[:, :, 0], lse[:, :, GROUPS + 1], ALU.mult))
                    link(dve.tensor_tensor(weighted[:], pick[:], bcast(w12[:].unsqueeze(3), [P, TB, 2, 8]), ALU.mult))
                    link(dve.tensor_tensor(either[:], weighted[:, :, 0, :], weighted[:, :, 1, :], ALU.add))
                    dve.tensor_tensor(by_group(comb), over_groups(either[:]), over_experts(gmask[:]),
                                      ALU.mult).then_inc(comb_ready, 1)

                def count_rounds(dve, link):
                    dve.wait_ge(totals_ready, 1)
                    link(dve.tensor_reduce(cnt[:, 0:1], ps[:, 7, 0:EXPERTS], AX, ALU.max))
                    for i in range(1, S // EC):
                        last = dve.tensor_scalar(cnt[:, i:i + 1], cnt[:, 0:1], float(EC * i), None, ALU.is_gt)
                    link(last)
                    link(dve.tensor_reduce(cnt[:, 0:1], cnt[:, 1:S // EC], AX, ALU.add))
                    dve.tensor_copy(extra[:], cnt[:, 0:1])

                def round_sp(sp, routed):
                    def load(u, q, which):
                        for i in which:
                            slot = 6 * (q % 2) + i
                            if not routed and isinstance(u, int) and u == 0 and q < 2 and slot in AHEAD_SLOTS:
                                sp.sem_inc(ring_in[slot], 16)
                                continue
                            after(sp, gu_ready if i < 4 else y_ready, u, PAIRS if i < 4 else 2 * PAIRS,
                                  q - 1 if i < 4 else 2 * (q - 1))
                            sp.dma_start(ring[:, slot, :], expert_weights(l, u, q, i)).then_inc(ring_in[slot], 16)

                    def main(u):
                        for q in range(1, PAIRS):
                            load(u, q, range(4))
                            load(u, q - 1, (4, 5))

                    def turn(u):
                        load(u, PAIRS - 1, (4, 5))
                        load(u + 1, 0, range(4))

                    load(0, 0, range(4))
                    units(sp, main, turn, lambda u: load(u, PAIRS - 1, (4, 5)))

                def round_act(act):
                    def gathered(u, c0=0):
                        for k in range(0, KB, 2):
                            after(act, gath_ready, u, KB, k + 1)
                            act.activation(xsel[:, k, c0:], ps[:, 4, c0:], ACT.Copy, scale=gain2[:, k:k + 1]).then_inc(gath_act, 1)

                    def hidden(q, u):
                        after(act, st_ready, u, PAIRS, q + 1)
                        act.copy(st[:, q, :], ps[:, 6, 0:S])
                        for e in range(2):
                            rows = slice(e * EC, (e + 1) * EC)
                            last = act.copy(wslot[rows, q:q + 1], ps[rows, 6, S + e:S + e + 1])
                        last.then_inc(st_evac, 1)
                        after(act, gu_ready, u, PAIRS, q + 1)
                        after(act, a_ready, u, PAIRS, q - 1)
                        act.activation(sg[:, q % 2, :], ps[:, q % 2, 0:F], ACT.Silu).then_inc(silu_done, 1)

                    def rows_out(q, u):
                        after(act, at_ready, u, PAIRS, q + 1)
                        act.copy(at_sb[:, q % 2, :, :].rearrange("p k s -> p (k s)"), ps[:, 7, 0:2 * P]).then_inc(at_evac, 1)
                        for nh in range(2):
                            after(act, y_ready, u, 2 * PAIRS, 2 * q + nh + 1)
                            if q == 0 and nh == 0:
                                after(act, back_ready, u, 4, 0)
                            act.copy(yh[:, q, nh * BANK:(nh + 1) * BANK], ps[:, 2 + nh, :]).then_inc(y_hi, 1)

                    def main(u):
                        for q in range(1, PAIRS):
                            hidden(q, u)
                            rows_out(q - 1, u)

                    def turn(u):
                        gathered(u + 1)
                        rows_out(PAIRS - 1, u)
                        hidden(0, u + 1)

                    def tail(u):
                        load_sqrt_table(act)
                        rows_out(PAIRS - 1, u)
                        norm_act(act, lambda q: after(act, back_done, u, 4, q + 1), lambda q: xsel[:, q, :])

                    for i in (0, 2):
                        act.wait_ge(first_ready, i + 1)
                        for k in (2 * i, 2 * i + 1):
                            last = act.activation(xsel[:, k, 0:FIRST], ps[:, 2 + i, (k % 2) * FIRST:(k % 2 + 1) * FIRST],
                                                  ACT.Copy, scale=gain2[:, k:k + 1])
                        last.then_inc(first_act, 1)
                    hidden(0, 0)
                    gathered(0, FIRST)
                    units(act, main, turn, tail)

                def round_pe(pe, routed):
                    def gather_first():
                        pe.wait_ge(first_onehot, 1)
                        for k in range(KB):
                            for tb in range(TB):
                                for part, p in enumerate((xnh, xnl)):
                                    mm = pe.matmul(ps[:, 2 + k // 2, (k % 2) * FIRST:(k % 2 + 1) * FIRST],
                                                   p[:, tb, k * P:(k + 1) * P], onehot[:, tb, 0:FIRST],
                                                   start=(tb == 0 and part == 0), stop=(tb == 1 and part == 1))
                            if k % 2:
                                mm.then_inc(first_ready, 1)

                    def gather(u, c0=0):
                        after(pe, onehot_ready, u, 1, 1)
                        for k in range(KB):
                            if k >= 2:
                                after(pe, gath_act if k % 2 == 0 else gath_dve, u, 4, k // 2)
                            elif k == 0:
                                after(pe, back_done, u, 4, -4)
                            for tb in range(TB):
                                for part, p in enumerate((xnh, xnl)):
                                    mm = pe.matmul(ps[:, 4 + k % 2, c0:], p[:, tb, k * P:(k + 1) * P], onehot[:, tb, c0:],
                                                   start=(tb == 0 and part == 0), stop=(tb == 1 and part == 1))
                            mm.then_inc(gath_ready, 1)

                    def spread(q, u):
                        after(pe, st_evac, u, PAIRS, q)
                        for tb in range(TB):
                            pe.transpose(ps[:, 6, tb * P:(tb + 1) * P],
                                         onehot[:, tb, q * P:(q + 1) * P].bitcast(F32), ident[:])
                        for tb in range(TB):
                            e = u * PER_GROUP + 2 * q
                            rhs = comb[:, tb, ds(e, 2)] if not isinstance(e, int) else comb[:, tb, e:e + 2]
                            mm = pe.matmul(ps[:, 6, S:S + 2], onehot[:, tb, q * P:(q + 1) * P].bitcast(F32),
                                           rhs, start=(tb == 0), stop=(tb == TB - 1))
                        mm.then_inc(st_ready, 1)

                    def gate_up(q, u):
                        very_first = isinstance(u, int) and u == 0 and q == 0
                        if q == 0 and not very_first or q == 2 and isinstance(u, int) and u == 0:
                            after(pe, gath_act, u, 4, 4)
                            after(pe, gath_dve, u, 4, 4)
                        after(pe, a_ready, u, PAIRS, q - 1)
                        for i in range(4):
                            slot = (6 * q + i) % RING
                            n = (6 * q + i) // RING
                            after(pe, ring_in[slot], u, 32, 16 * (n + 1))
                        for k in range(KB):
                            if very_first and k % 2 == 0:
                                pe.wait_ge(first_dve if k % 4 else first_act, k // 4 + 1)
                            for e in range(2):
                                slot = (6 * q + 2 * e) % RING
                                w = ring[:, slot:slot + 2, k * F:(k + 1) * F]
                                c = (2 * q + e) * EC
                                mm = pe.matmul(ps[e * EC:(e + 1) * EC, q % 2, :].rearrange("p (a f) -> p a f", a=2),
                                               xsel[:, k, c:c + EC], w, start=(k == 0), stop=(k == KB - 1),
                                               skip_group_check=True)
                        mm.then_inc(gu_ready, 1)

                    def down(q, u):
                        after(pe, a_ready, u, PAIRS, q + 1)
                        after(pe, at_evac, u, PAIRS, q)
                        for kf in range(2):
                            mm = pe.transpose(ps[:, 7, kf * P:(kf + 1) * P], a_sb[:, q % 2, kf:F:2], ident[:])
                        mm.then_inc(at_ready, 1)
                        after(pe, at_evac, u, PAIRS, q + 1)
                        for i in (4, 5):
                            slot = (6 * q + i) % RING
                            after(pe, ring_in[slot], u, 32, 16 * ((6 * q + i) // RING + 1))
                        for nh in range(2):
                            after(pe, y_lo, u, 2 * PAIRS, 2 * q + nh - 1)
                            for kf in range(2):
                                for e in range(2):
                                    slot = (6 * q + 4 + e) % RING
                                    w = ring[:, slot, kf * D + nh * BANK:kf * D + (nh + 1) * BANK]
                                    mm = pe.matmul(ps[e * EC:(e + 1) * EC, 2 + nh, :],
                                                   at_sb[:, q % 2, kf, e * EC:(e + 1) * EC], w, start=(kf == 0),
                                                   stop=(kf == 1), skip_group_check=True)
                            mm.then_inc(y_ready, 1)

                    def scatter_part(bank, q, pairs):
                        tb, nh = q % 2, q // 2
                        for p in pairs:
                            for part, y in enumerate((yh, yl)):
                                mm = pe.matmul(ps[:, bank, :], st[:, p, tb * P:(tb + 1) * P],
                                               y[:, p, nh * BANK:(nh + 1) * BANK],
                                               start=(p == 0 and part == 0), stop=(p == PAIRS - 1 and part == 1))
                        return mm

                    def scatter(u):
                        after(pe, y_lo, u, 2 * PAIRS, 2 * PAIRS)
                        for q in range(4):
                            if q >= 2:
                                after(pe, back_done, u, 4, q - 1)
                            scatter_part(4 + q % 2, q, range(PAIRS)).then_inc(back_ready, 1)

                    def main(u):
                        for q in range(1, PAIRS):
                            spread(q, u)
                            if q == PAIRS - 1 and isinstance(u, int) and u == GROUPS - 1:
                                after(pe, a_ready, u, PAIRS, q)
                                after(pe, back_done, u, 4, 0)
                                after(pe, y_lo, u, 2 * PAIRS, 4)
                                for quart in range(3):
                                    scatter_part(TAIL_BANKS[quart], quart, (0, 1))
                            gate_up(q, u)
                            down(q - 1, u)

                    def turn(u):
                        gather(u + 1)
                        down(PAIRS - 1, u)
                        gate_up(0, u + 1)
                        scatter(u)
                        spread(0, u + 1)

                    def tail(u):
                        after(pe, a_ready, u, PAIRS, PAIRS)
                        scatter_part(TAIL_BANKS[3], 3, (0, 1))
                        down(PAIRS - 1, u)
                        after(pe, y_lo, u, 2 * PAIRS, 2 * PAIRS - 2)
                        for q in range(4):
                            scatter_part(TAIL_BANKS[q], q, [PAIRS - 2])
                        after(pe, y_lo, u, 2 * PAIRS, 2 * PAIRS)
                        for q in range(4):
                            scatter_part(TAIL_BANKS[q], q, [PAIRS - 1]).then_inc(back_ready, 1)
                        keep_clock(pe, WARM_TRUNK)

                    gather_first()
                    gate_up(0, 0)
                    if not routed:
                        pe.wait_ge(comb_ready, 1)
                    spread(0, 0)
                    gather(0, FIRST)
                    units(pe, main, turn, tail)

                def round_dve(dve, link, routed):
                    def build(u, done, e0=0, n=PER_GROUP):
                        after(dve, st_ready, u, PAIRS, 0)
                        for tb in range(TB):
                            e = u * PER_GROUP + e0
                            r = rk[:, tb, ds(e, n)] if not isinstance(e, int) else rk[:, tb, e:e + n]
                            last = dve.tensor_tensor(
                                onehot[:, tb, e0 * EC:(e0 + n) * EC].rearrange("p (e c) -> p e c", e=n),
                                bcast(slot_iota[:].unsqueeze(1), [P, n, EC]),
                                bcast(r.unsqueeze(2), [P, n, EC]), ALU.is_equal)
                        last.then_inc(done, 1)

                    def gathered_first():
                        for i in (1, 3):
                            dve.wait_ge(first_ready, i + 1)
                            for k in (2 * i, 2 * i + 1):
                                last = dve.tensor_scalar(xsel[:, k, 0:FIRST], ps[:, 2 + i, (k % 2) * FIRST:(k % 2 + 1) * FIRST],
                                                         gain2[:, k:k + 1], None, ALU.mult)
                            last.then_inc(first_dve, 1)

                    def gathered(u, c0=0):
                        for k in range(1, KB, 2):
                            after(dve, gath_ready, u, KB, k + 1)
                            dve.tensor_scalar(xsel[:, k, c0:], ps[:, 5, c0:], gain2[:, k:k + 1], None,
                                              ALU.mult).then_inc(gath_dve, 1)

                    def hidden(q, u):
                        after(dve, silu_done, u, PAIRS, q + 1)
                        after(dve, at_ready, u, PAIRS, q - 1)
                        dve.scalar_tensor_tensor(out=a_sb[:, q % 2, :], in0=ps[:, q % 2, F:2 * F],
                                                 scalar=wslot[:, q:q + 1], in1=sg[:, q % 2, :],
                                                 op0=ALU.mult, op1=ALU.mult).then_inc(a_ready, 1)

                    def rows_out(q, u):
                        for nh in range(2):
                            after(dve, y_hi, u, 2 * PAIRS, 2 * q + nh + 1)
                            cols = slice(nh * BANK, (nh + 1) * BANK)
                            dve.tensor_tensor(yl[:, q, cols], ps[:, 2 + nh, :],
                                              yh[:, q, cols].bitcast(F32), ALU.subtract).then_inc(y_lo, 1)

                    def back(u, banks):
                        for q in range(4):
                            after(dve, back_ready, u, 4, q + 1)
                            to = quarter(xs, q)
                            dve.tensor_tensor(to, ps[:, banks[q], :], to, ALU.add).then_inc(back_done, 1)

                    def main(u, more=True):
                        for q in range(1, PAIRS):
                            if q == PAIRS - 1 and more:
                                build(u + 1, onehot_ready)
                            hidden(q, u)
                            rows_out(q - 1, u)

                    def turn(u):
                        gathered(u + 1)
                        rows_out(PAIRS - 1, u)
                        back(u, (4, 5, 4, 5))
                        hidden(0, u + 1)

                    def tail(u):
                        rows_out(PAIRS - 1, u)
                        back(u, TAIL_BANKS)
                        norm_dve(dve, link)

                    build(0, first_onehot, 0, PER_GROUP // 2)
                    build(0, onehot_ready, PER_GROUP // 2, PER_GROUP // 2)
                    gathered_first()
                    if not routed:
                        combine_weights(dve, link)
                        count_rounds(dve, link)
                    hidden(0, 0)
                    gathered(0, FIRST)
                    units(dve, lambda u: main(u, not isinstance(u, int) or u < GROUPS - 1), turn, tail)
                    dve.tensor_scalar(rk[:], rk[:], float(EC), None, ALU.subtract)

                def one_round(routed):
                    with nc.Block() as block:
                        @block.sync
                        def _(sp):
                            round_sp(sp, routed)

                        @block.scalar
                        def _(act):
                            if not routed:
                                route_act(act)
                            round_act(act)

                        @block.tensor
                        def _(pe):
                            if not routed:
                                route_pe(pe)
                            round_pe(pe, routed)

                        @block.gpsimd
                        def _(pool):
                            if not routed:
                                route_pool(pool)

                        @block.vector
                        def _(dve):
                            link = chain(dve, dve_step)
                            if not routed:
                                route_dve(dve, link)
                            round_dve(dve, link, routed)

                one_round(routed=False)
                n_extra = nc.values_load(extra[0:1, 0:1], min_val=0, max_val=S // EC - 1)
                end_of_stage()
                with nc.If(n_extra > 0):
                    with nc.Fori(0, n_extra) as _:
                        one_round(routed=True)
                        end_of_stage()

        with nc.Fori(0, DEPTH) as l:
            trunk_stage(l)
            expert_stage(l)

        with ExitStack() as ctx:
            gf = sb("gf", [P, D], F32, ctx)
            result = sb("result", [P, TB, D], F32, ctx)
            with nc.Block() as block:
                @block.sync
                def _(sp):
                    sp.dma_start(gf[:], norm_f_g.partition_broadcast(P)).then_inc(small_in, 16)
                    for tb in range(TB):
                        sp.wait_ge(merged, tb + 1)
                        sp.dma_start(out[0, tb * P:(tb + 1) * P, :], result[:, tb, :]).then_inc(out_done, 16)
                    sp.wait_ge(out_done, 16 * TB)

                @block.vector
                def _(dve):
                    dve.wait_ge(small_in, 16)
                    for tb in range(TB):
                        dve.tensor_tensor(result[:, tb, :].rearrange("p (c k) -> p c k", k=KB),
                                          work[:, tb, :].rearrange("p (k c) -> p c k", k=KB),
                                          gf[:].rearrange("p (c k) -> p c k", k=KB), ALU.mult).then_inc(merged, 1)


_INS = ['x', 'positions', 'norm1_g', 'w_in', 'b_in', 'attn_sinks', 'sgu_ln_g', 'sgu_ln_b', 'w_spatial', 'b_spatial',
        'w_proj_a', 'w_proj_b', 'w_proj_c', 'w_out', 'norm2_g', 'w_router_group', 'w_router_expert', 'w_expert_gate',
        'w_expert_up', 'w_expert_down', 'norm_f_g']


def kernel(**inputs):
    import numpy as _np
    import concourse.bacc as _bacc
    from concourse import mybir as _mybir
    from concourse.bass_utils import run_bass_kernel_spmd as _run

    nc = _bacc.Bacc("TRN2", target_bir_lowering=False, num_devices=1)
    arrays, args = {}, []
    for name in _INS:
        a = _np.ascontiguousarray(inputs[name])
        arrays[f"in_{name}_dram"] = a
        args.append(nc.dram_tensor(f"in_{name}_dram", a.shape, _mybir.dt.from_np(a.dtype), kind="ExternalInput").ap())
    args.append(nc.dram_tensor("out_dram", inputs["x"].shape, _mybir.dt.float32, kind="ExternalOutput").ap())
    trunk_program(nc, *args)
    r = _run(nc, [arrays], core_ids=[0])
    return r.results[0]["out_dram"]
```
